# Optimizing a Trainium2 kernel written in Bass

```python
import math
import jax
import jax.numpy as jnp
from jax import lax
import numpy as np

D_MODEL = 1024
BATCH = 1
SEQ = 128
DEPTH = 2
DEC_BATCH = 1
DEC_SEQ = 128
PAST_LEN = 128

GRID_W = 64
BLOCK = 128
WINDOW = 128
ROPE_BASE = 10000.0
A_HEADS = 8
A_KV_HEADS = 2
A_GROUP = A_HEADS // A_KV_HEADS
A_HEAD_DIM = 64
A_SCALE = A_HEAD_DIM ** -0.5
MLA_HEADS = 8
MLA_Q_RANK = 256
MLA_KV_RANK = 128
MLA_NOPE_DIM = 64
MLA_ROPE_DIM = 32
MLA_V_DIM = 64
MLA_SCALE = (MLA_NOPE_DIM + MLA_ROPE_DIM) ** -0.5
A_Q_W = A_HEADS * A_HEAD_DIM
A_KV_W = A_KV_HEADS * A_HEAD_DIM
AB_SPLITS = (A_Q_W, A_Q_W + A_KV_W, A_Q_W + 2 * A_KV_W,
             A_Q_W + 2 * A_KV_W + MLA_Q_RANK,
             A_Q_W + 2 * A_KV_W + MLA_Q_RANK + MLA_KV_RANK)
AB_IN_W = A_Q_W + 2 * A_KV_W + MLA_Q_RANK + MLA_KV_RANK + MLA_ROPE_DIM
AB_OUT_W = A_Q_W + MLA_HEADS * MLA_V_DIM
S5_WIDTH = D_MODEL
S5_GROUP_CH = 16
S5_GROUPS = S5_WIDTH // S5_GROUP_CH
S5_STATE = 64
N_EXPERTS = 64
TOP_K = 6
EXPERT_FF = 128
SHARED_FF = 128
ROUTED_SCALE = 2.5
N_EVEN = (DEPTH + 1) // 2
N_ODD = DEPTH // 2
DEEPNORM_ALPHA = (2.0 * DEPTH) ** 0.25
DEEPNORM_BETA = (8.0 * DEPTH) ** -0.25
LN_EPS = 1e-5
RMS_EPS = 1e-6
NEG_INF = -1e30

kernel_name = "hybrid_diffusion_prefix_trunk"

def layer_norm(x, g, b):
    x32 = x.astype(jnp.float32)
    mu = jnp.mean(x32, axis=-1, keepdims=True)
    var = jnp.mean(jnp.square(x32 - mu), axis=-1, keepdims=True)
    y = (x32 - mu) * lax.rsqrt(var + LN_EPS) * g.astype(jnp.float32) + b.astype(jnp.float32)
    return y.astype(x.dtype)

def rms_norm(x, g):
    x32 = x.astype(jnp.float32)
    y = x32 * lax.rsqrt(jnp.mean(jnp.square(x32), axis=-1, keepdims=True) + RMS_EPS) * g.astype(jnp.float32)
    return y.astype(x.dtype)

def rope_1d(x, pos):
    half = x.shape[-1] // 2
    inv_freq = ROPE_BASE ** (-jnp.arange(half, dtype=jnp.float32) / half)
    ang = pos[:, None] * inv_freq[None, :]
    cos = jnp.cos(ang)[None, :, None, :]
    sin = jnp.sin(ang)[None, :, None, :]
    x32 = x.astype(jnp.float32)
    x1, x2 = x32[..., :half], x32[..., half:]
    return jnp.concatenate([x1 * cos - x2 * sin, x1 * sin + x2 * cos], axis=-1).astype(x.dtype)

def axial_rope(x, row, col):
    half = x.shape[-1] // 2
    return jnp.concatenate([rope_1d(x[..., :half], row), rope_1d(x[..., half:], col)], axis=-1)

def adaln(cvec, w, b):
    m = jax.nn.silu(cvec) @ w + b
    return [p[:, None, :] for p in jnp.split(m, 6, axis=-1)]

def modulate(x, shift, scale):
    return x * (1.0 + scale) + shift

def dense_attention(q, k, v, scale, sink):
    bsz, n_q, n_kv, n_grp, dim = q.shape
    n_blk = n_q // BLOCK
    q_blocks = jnp.moveaxis(q.reshape(bsz, n_blk, BLOCK, n_kv, n_grp, dim), 1, 0)

    def one_block(q_blk):
        s = jnp.einsum("bqhgd,bkhd->bhgqk", q_blk, k).astype(jnp.float32) * scale
        if sink is not None:
            s_sink = jnp.broadcast_to(sink.astype(jnp.float32)[None, :, :, None, None], s.shape[:-1] + (1,))
            s = jnp.concatenate([s, s_sink], axis=-1)
        p = jax.nn.softmax(s, axis=-1)
        if sink is not None:
            p = p[..., :-1]
        return jnp.einsum("bhgqk,bkhe->bqhge", p.astype(v.dtype), v)

    out = lax.map(one_block, q_blocks)
    return jnp.moveaxis(out, 0, 1).reshape(bsz, n_q, n_kv, n_grp, v.shape[-1])

def windowed_prefix_attention(q, k, v, k_ctx, v_ctx, sink, scale):
    bsz, n_tok, n_kv, n_grp, dim = q.shape
    n_blk = n_tok // BLOCK
    q_b = q.reshape(bsz, n_blk, BLOCK, n_kv, n_grp, dim)
    pad = ((0, 0), (BLOCK, BLOCK), (0, 0), (0, 0))

    def band(t):
        tp = jnp.pad(t, pad).reshape(bsz, n_blk + 2, BLOCK, n_kv, t.shape[-1])
        return jnp.concatenate([tp[:, :-2], tp[:, 1:-1], tp[:, 2:]], axis=2)

    k_b, v_b = band(k), band(v)
    q_pos = jnp.arange(n_blk)[:, None] * BLOCK + jnp.arange(BLOCK)[None, :]
    k_pos = (jnp.arange(n_blk)[:, None] - 1) * BLOCK + jnp.arange(3 * BLOCK)[None, :]
    valid = ((jnp.abs(q_pos[:, :, None] - k_pos[:, None, :]) <= WINDOW)
             & (k_pos >= 0)[:, None, :] & (k_pos < n_tok)[:, None, :])
    s_win = jnp.einsum("bnqhgd,bnkhd->bnhgqk", q_b, k_b).astype(jnp.float32) * scale
    s_win = jnp.where(valid[None, :, None, None], s_win, NEG_INF)
    s_ctx = jnp.einsum("bnqhgd,bchd->bnhgqc", q_b, k_ctx).astype(jnp.float32) * scale
    s_sink = jnp.broadcast_to(sink.astype(jnp.float32)[None, None, :, :, None, None], s_win.shape[:-1] + (1,))
    p = jax.nn.softmax(jnp.concatenate([s_win, s_ctx, s_sink], axis=-1), axis=-1)
    n_win = 3 * BLOCK
    p_win = p[..., :n_win].astype(v.dtype)
    p_ctx = p[..., n_win:n_win + k_ctx.shape[1]].astype(v.dtype)
    out = (jnp.einsum("bnhgqk,bnkhd->bnqhgd", p_win, v_b)
           + jnp.einsum("bnhgqc,bchd->bnqhgd", p_ctx, v_ctx))
    return out.reshape(bsz, n_tok, n_kv, n_grp, dim)

def ab_project(h, w_in, q_norm, kv_norm):
    bsz, n_tok = h.shape[:2]
    q_a, k_a, v_a, c_q, c_kv, k_rope = jnp.split(h @ w_in, AB_SPLITS, axis=-1)
    q_a = q_a.reshape(bsz, n_tok, A_HEADS, A_HEAD_DIM)
    k_a = k_a.reshape(bsz, n_tok, A_KV_HEADS, A_HEAD_DIM)
    v_a = v_a.reshape(bsz, n_tok, A_KV_HEADS, A_HEAD_DIM)
    return q_a, k_a, v_a, rms_norm(c_q, q_norm), rms_norm(c_kv, kv_norm), k_rope

def mla_queries(c_q, w_uq):
    bsz, n_tok = c_q.shape[:2]
    q = (c_q @ w_uq).reshape(bsz, n_tok, MLA_HEADS, MLA_NOPE_DIM + MLA_ROPE_DIM)
    return q[..., :MLA_NOPE_DIM], q[..., MLA_NOPE_DIM:]

def mla_keys_values(c_kv, k_rope, w_ukv):
    bsz, n_tok = c_kv.shape[:2]
    kv = (c_kv @ w_ukv).reshape(bsz, n_tok, MLA_HEADS, MLA_NOPE_DIM + MLA_V_DIM)
    k_nope, v = kv[..., :MLA_NOPE_DIM], kv[..., MLA_NOPE_DIM:]
    k_r = jnp.broadcast_to(k_rope, (bsz, n_tok, MLA_HEADS, MLA_ROPE_DIM)).astype(k_nope.dtype)
    return jnp.concatenate([k_nope, k_r], axis=-1), v

def ab_mixer_context(h, w_in, sink, q_norm, kv_norm, w_uq, w_ukv, w_out):
    bsz, n_tok = h.shape[:2]
    q_a, k_a, v_a, c_q, c_kv, k_rope = ab_project(h, w_in, q_norm, kv_norm)
    out_a = dense_attention(q_a.reshape(bsz, n_tok, A_KV_HEADS, A_GROUP, A_HEAD_DIM), k_a, v_a,
                            A_SCALE, sink.reshape(A_KV_HEADS, A_GROUP))
    q_nope, q_rope = mla_queries(c_q, w_uq)
    k_m, v_m = mla_keys_values(c_kv, k_rope[:, :, None, :], w_ukv)
    q_m = jnp.concatenate([q_nope, q_rope], axis=-1)[:, :, :, None, :]
    out_b = dense_attention(q_m, k_m, v_m, MLA_SCALE, None)
    merged = jnp.concatenate([out_a.reshape(bsz, n_tok, A_Q_W),
                              out_b.reshape(bsz, n_tok, MLA_HEADS * MLA_V_DIM)], axis=-1)
    return merged @ w_out, k_a, v_a, c_kv, k_rope

def ab_mixer_latent(h, row, col, ctx_k, ctx_v, ctx_ckv, ctx_krope,
                    w_in, sink, q_norm, kv_norm, w_uq, w_ukv, w_out):
    bsz, n_tok = h.shape[:2]
    q_a, k_a, v_a, c_q, c_kv, k_rope = ab_project(h, w_in, q_norm, kv_norm)
    q_a = axial_rope(q_a, row, col)
    k_a = axial_rope(k_a, row, col)
    out_a = windowed_prefix_attention(q_a.reshape(bsz, n_tok, A_KV_HEADS, A_GROUP, A_HEAD_DIM),
                                      k_a, v_a, ctx_k, ctx_v,
                                      sink.reshape(A_KV_HEADS, A_GROUP), A_SCALE)
    q_nope, q_rope = mla_queries(c_q, w_uq)
    q_rope = axial_rope(q_rope, row, col)
    k_lat, v_lat = mla_keys_values(c_kv, axial_rope(k_rope[:, :, None, :], row, col), w_ukv)
    k_ctx, v_ctx = mla_keys_values(ctx_ckv, ctx_krope[:, :, None, :], w_ukv)
    q_m = jnp.concatenate([q_nope, q_rope], axis=-1)[:, :, :, None, :]
    out_b = dense_attention(q_m, jnp.concatenate([k_ctx, k_lat], axis=1),
                            jnp.concatenate([v_ctx, v_lat], axis=1), MLA_SCALE, None)
    merged = jnp.concatenate([out_a.reshape(bsz, n_tok, A_Q_W),
                              out_b.reshape(bsz, n_tok, MLA_HEADS * MLA_V_DIM)], axis=-1)
    return merged @ w_out

def ssm_combine(left, right):
    a1, b1 = left
    a2, b2 = right
    return a1 * a2, a2 * b1 + b2

def s5_scan(u_g, h0, lam_re, lam_im, log_dt, b_re, b_im, c_re, c_im, reverse):
    lam = lax.complex(lam_re.astype(jnp.float32), lam_im.astype(jnp.float32))
    dt = jnp.exp(log_dt.astype(jnp.float32))[:, None]
    lam_bar = jnp.exp(lam * dt)
    b = lax.complex(b_re.astype(jnp.float32), b_im.astype(jnp.float32))
    b_bar = ((lam_bar - 1.0) / lam)[..., None] * b
    bu = jnp.einsum("blgc,gpc->blgp", u_g.astype(jnp.complex64), b_bar)
    first = -1 if reverse else 0
    bu = bu.at[:, first].add(lam_bar[None] * h0)
    a = jnp.broadcast_to(lam_bar, bu.shape)
    _, states = lax.associative_scan(ssm_combine, (a, bu), axis=1, reverse=reverse)
    c = lax.complex(c_re.astype(jnp.float32), c_im.astype(jnp.float32))
    y = jnp.real(jnp.einsum("gcp,blgp->blgc", c, states))
    h_final = states[:, 0] if reverse else states[:, -1]
    return y, h_final

def s5_mixer(h, h0_fwd, h0_bwd, w_in, lam_re, lam_im, log_dt, b_re, b_im, c_re, c_im, d, w_out):
    bsz, n_tok = h.shape[:2]
    u = (h @ w_in).astype(jnp.float32)
    u_g = u.reshape(bsz, n_tok, S5_GROUPS, S5_GROUP_CH)
    y_f, h_f = s5_scan(u_g, h0_fwd, lam_re[0], lam_im[0], log_dt[0], b_re[0], b_im[0], c_re[0], c_im[0], False)
    y_b, h_b = s5_scan(u_g, h0_bwd, lam_re[1], lam_im[1], log_dt[1], b_re[1], b_im[1], c_re[1], c_im[1], True)
    y = (y_f + y_b).reshape(bsz, n_tok, S5_WIDTH) + d.astype(jnp.float32) * u
    z = jax.nn.gelu(y).astype(w_out.dtype) @ w_out
    z_val, z_gate = jnp.split(z, 2, axis=-1)
    return (z_val * jax.nn.sigmoid(z_gate)).astype(h.dtype), h_f, h_b

def pack_state(h_f, h_b):
    return jnp.stack([jnp.stack([jnp.real(h_f), jnp.imag(h_f)], axis=1),
                      jnp.stack([jnp.real(h_b), jnp.imag(h_b)], axis=1)], axis=1)

def moe(h, router_w, router_bias, w_gate, w_up, w_down, s_gate, s_up, s_down):
    bsz, n_tok, dim = h.shape
    t = h.reshape(-1, dim)
    n_rows = t.shape[0]
    scores = jax.nn.sigmoid((t @ router_w).astype(jnp.float32))
    _, idx = lax.top_k(scores + router_bias.astype(jnp.float32)[None, :], TOP_K)
    w_sel = jnp.take_along_axis(scores, idx, axis=-1)
    w_sel = w_sel / jnp.sum(w_sel, axis=-1, keepdims=True) * ROUTED_SCALE
    gates = jnp.zeros((n_rows, N_EXPERTS), jnp.float32).at[jnp.arange(n_rows)[:, None], idx].set(w_sel)
    hidden = jax.nn.silu(jnp.einsum("td,edf->tef", t, w_gate)) * jnp.einsum("td,edf->tef", t, w_up)
    routed = jnp.einsum("tef,efd->td", hidden * gates[..., None].astype(hidden.dtype), w_down)
    shared = (jax.nn.silu(t @ s_gate) * (t @ s_up)) @ s_down
    return (routed + shared).astype(h.dtype).reshape(bsz, n_tok, dim)

def setup_inputs(seed: int = 0) -> dict:
    key = jax.random.key(seed)
    keys = list(jax.random.split(key, 48))

    def nrm(shape, scale):
        return jax.random.normal(keys.pop(), shape, jnp.float32) * scale

    s5_n = jnp.pi * jnp.arange(S5_STATE, dtype=jnp.float32)
    return {
        "x_prompt": nrm((BATCH, SEQ, D_MODEL), 1.0),
        "x_sample": nrm((DEC_BATCH, DEC_SEQ, D_MODEL), 1.0),
        "c": nrm((DEC_BATCH, D_MODEL), 1.0),
        "cache_attn_k": nrm((DEC_BATCH, N_EVEN, PAST_LEN, A_KV_HEADS, A_HEAD_DIM), 1.0),
        "cache_attn_v": nrm((DEC_BATCH, N_EVEN, PAST_LEN, A_KV_HEADS, A_HEAD_DIM), 1.0),
        "cache_mla_ckv": nrm((DEC_BATCH, N_EVEN, PAST_LEN, MLA_KV_RANK), 1.0),
        "cache_mla_krope": nrm((DEC_BATCH, N_EVEN, PAST_LEN, MLA_ROPE_DIM), 1.0),
        "state_ssm": nrm((DEC_BATCH, N_ODD, 2, 2, S5_GROUPS, S5_STATE), 0.5),
        "c_ctx": nrm((D_MODEL,), 1.0),
        "ada_w": nrm((DEPTH, D_MODEL, 6 * D_MODEL), D_MODEL ** -0.5),
        "ada_b": nrm((DEPTH, 6 * D_MODEL), 0.01),
        "ln_mix_g": 1.0 + nrm((DEPTH, D_MODEL), 0.01),
        "ln_mix_b": nrm((DEPTH, D_MODEL), 0.01),
        "ln_ffn_g": 1.0 + nrm((DEPTH, D_MODEL), 0.01),
        "ln_ffn_b": nrm((DEPTH, D_MODEL), 0.01),
        "w_in_ab": nrm((N_EVEN, D_MODEL, AB_IN_W), D_MODEL ** -0.5),
        "attn_sink": nrm((N_EVEN, A_HEADS), 0.5),
        "mla_q_norm": 1.0 + nrm((N_EVEN, MLA_Q_RANK), 0.01),
        "mla_kv_norm": 1.0 + nrm((N_EVEN, MLA_KV_RANK), 0.01),
        "mla_w_uq": nrm((N_EVEN, MLA_Q_RANK, MLA_HEADS * (MLA_NOPE_DIM + MLA_ROPE_DIM)), MLA_Q_RANK ** -0.5),
        "mla_w_ukv": nrm((N_EVEN, MLA_KV_RANK, MLA_HEADS * (MLA_NOPE_DIM + MLA_V_DIM)), MLA_KV_RANK ** -0.5),
        "w_out_ab": nrm((N_EVEN, AB_OUT_W, D_MODEL), DEEPNORM_BETA * AB_OUT_W ** -0.5),
        "w_in_c": nrm((N_ODD, D_MODEL, S5_WIDTH), D_MODEL ** -0.5),
        "s5_lam_re": -0.5 + nrm((N_ODD, 2, S5_GROUPS, S5_STATE), 0.01),
        "s5_lam_im": s5_n + nrm((N_ODD, 2, S5_GROUPS, S5_STATE), 0.01),
        "s5_log_dt": jax.random.uniform(keys.pop(), (N_ODD, 2, S5_GROUPS), jnp.float32,
                                        math.log(1e-3), math.log(1e-1)),
        "s5_b_re": nrm((N_ODD, 2, S5_GROUPS, S5_STATE, S5_GROUP_CH), (2 * S5_GROUP_CH) ** -0.5),
        "s5_b_im": nrm((N_ODD, 2, S5_GROUPS, S5_STATE, S5_GROUP_CH), (2 * S5_GROUP_CH) ** -0.5),
        "s5_c_re": nrm((N_ODD, 2, S5_GROUPS, S5_GROUP_CH, S5_STATE), S5_STATE ** -0.5),
        "s5_c_im": nrm((N_ODD, 2, S5_GROUPS, S5_GROUP_CH, S5_STATE), S5_STATE ** -0.5),
        "s5_d": nrm((N_ODD, S5_WIDTH), 1.0),
        "w_out_c": nrm((N_ODD, S5_WIDTH, 2 * D_MODEL), DEEPNORM_BETA * S5_WIDTH ** -0.5),
        "router_w": nrm((DEPTH, D_MODEL, N_EXPERTS), D_MODEL ** -0.5),
        "router_bias": nrm((DEPTH, N_EXPERTS), 0.01),
        "exp_w_gate": nrm((DEPTH, N_EXPERTS, D_MODEL, EXPERT_FF), D_MODEL ** -0.5),
        "exp_w_up": nrm((DEPTH, N_EXPERTS, D_MODEL, EXPERT_FF), D_MODEL ** -0.5),
        "exp_w_down": nrm((DEPTH, N_EXPERTS, EXPERT_FF, D_MODEL), DEEPNORM_BETA * EXPERT_FF ** -0.5),
        "sh_w_gate": nrm((DEPTH, D_MODEL, SHARED_FF), D_MODEL ** -0.5),
        "sh_w_up": nrm((DEPTH, D_MODEL, SHARED_FF), D_MODEL ** -0.5),
        "sh_w_down": nrm((DEPTH, SHARED_FF, D_MODEL), DEEPNORM_BETA * SHARED_FF ** -0.5),
    }

def reference(x_prompt, x_sample, c, cache_attn_k, cache_attn_v, cache_mla_ckv, cache_mla_krope,
              state_ssm, c_ctx, ada_w, ada_b, ln_mix_g, ln_mix_b, ln_ffn_g, ln_ffn_b,
              w_in_ab, attn_sink, mla_q_norm, mla_kv_norm, mla_w_uq, mla_w_ukv, w_out_ab,
              w_in_c, s5_lam_re, s5_lam_im, s5_log_dt, s5_b_re, s5_b_im, s5_c_re, s5_c_im,
              s5_d, w_out_c, router_w, router_bias, exp_w_gate, exp_w_up, exp_w_down,
              sh_w_gate, sh_w_up, sh_w_down):

    def channel_mixer(h, l):
        return moe(h, router_w[l], router_bias[l], exp_w_gate[l], exp_w_up[l], exp_w_down[l],
                   sh_w_gate[l], sh_w_up[l], sh_w_down[l])

    def s5_layer(h, h0_f, h0_b, i):
        return s5_mixer(h, h0_f, h0_b, w_in_c[i], s5_lam_re[i], s5_lam_im[i], s5_log_dt[i],
                        s5_b_re[i], s5_b_im[i], s5_c_re[i], s5_c_im[i], s5_d[i], w_out_c[i])

    x = x_prompt
    new_k, new_v, new_ckv, new_krope, new_ssm = [], [], [], [], []
    for l in range(DEPTH):
        i = l // 2
        sh_m, sc_m, g_m, sh_f, sc_f, g_f = adaln(c_ctx[None, :], ada_w[l], ada_b[l])
        h = modulate(x, sh_m, sc_m)
        if l % 2 == 0:
            out, k_a, v_a, c_kv, k_rope = ab_mixer_context(
                h, w_in_ab[i], attn_sink[i], mla_q_norm[i], mla_kv_norm[i],
                mla_w_uq[i], mla_w_ukv[i], w_out_ab[i])
            new_k.append(k_a)
            new_v.append(v_a)
            new_ckv.append(c_kv)
            new_krope.append(k_rope)
        else:
            zeros = jnp.zeros((x.shape[0], S5_GROUPS, S5_STATE), jnp.complex64)
            out, h_f, h_b = s5_layer(h, zeros, zeros, i)
            new_ssm.append(pack_state(h_f, h_b))
        x = layer_norm(DEEPNORM_ALPHA * x + g_m * out, ln_mix_g[l], ln_mix_b[l])
        h = modulate(x, sh_f, sc_f)
        x = layer_norm(DEEPNORM_ALPHA * x + g_f * channel_mixer(h, l), ln_ffn_g[l], ln_ffn_b[l])
    y_prompt = x

    n_tok = x_sample.shape[1]
    n_rows = n_tok // GRID_W
    row = jnp.repeat(jnp.arange(n_rows, dtype=jnp.float32), GRID_W)
    col = jnp.tile(jnp.arange(GRID_W, dtype=jnp.float32), n_rows)
    x = x_sample
    for l in range(DEPTH):
        i = l // 2
        sh_m, sc_m, g_m, sh_f, sc_f, g_f = adaln(c, ada_w[l], ada_b[l])
        h = modulate(x, sh_m, sc_m)
        if l % 2 == 0:
            out = ab_mixer_latent(h, row, col, cache_attn_k[:, i], cache_attn_v[:, i],
                                  cache_mla_ckv[:, i], cache_mla_krope[:, i],
                                  w_in_ab[i], attn_sink[i], mla_q_norm[i], mla_kv_norm[i],
                                  mla_w_uq[i], mla_w_ukv[i], w_out_ab[i])
        else:
            st = state_ssm[:, i].astype(jnp.float32)
            h0_f = lax.complex(st[:, 0, 0], st[:, 0, 1])
            h0_b = lax.complex(st[:, 1, 0], st[:, 1, 1])
            out, _, _ = s5_layer(h, h0_f, h0_b, i)
        x = layer_norm(DEEPNORM_ALPHA * x + g_m * out, ln_mix_g[l], ln_mix_b[l])
        h = modulate(x, sh_f, sc_f)
        x = layer_norm(DEEPNORM_ALPHA * x + g_f * channel_mixer(h, l), ln_ffn_g[l], ln_ffn_b[l])
    y_sample = x

    new_attn_k = jnp.stack(new_k, axis=1)
    new_attn_v = jnp.stack(new_v, axis=1)
    new_mla_ckv = jnp.stack(new_ckv, axis=1)
    new_mla_krope = jnp.stack(new_krope, axis=1)
    new_state_ssm = jnp.stack(new_ssm, axis=1)
    return (y_prompt, y_sample, new_attn_k, new_attn_v, new_mla_ckv, new_mla_krope, new_state_ssm)


_drawn_inputs = setup_inputs


def setup_inputs(seed=0):
    import zlib

    import numpy as np

    out = dict(_drawn_inputs(seed))
    spreads = {}
    factors = {'attn_sink': 8.0,
     'mla_q_norm': 3.877,
     'mla_kv_norm': 5.828,
     's5_lam_re': 18.827,
     'cache_mla_ckv': 8.0,
     'cache_mla_krope': 8.0}
    for name, (base, spread) in spreads.items():
        noise = np.random.default_rng([zlib.crc32(name.encode()), seed]).standard_normal(out[name].shape)
        drawn = base * np.exp(spread * noise) if base else spread * noise
        out[name] = jnp.asarray(drawn.astype(out[name].dtype))
    for name, factor in factors.items():
        out[name] = (out[name] * factor).astype(out[name].dtype)
    return out
```

```python
import math
from contextlib import ExitStack

import numpy as np

import concourse.bass as bass
from concourse import mybir

F32 = mybir.dt.float32
F32R = mybir.dt.float32r
U32 = mybir.dt.uint32
ALU = mybir.AluOpType
ACT = mybir.ActivationFunctionType
AX_X = mybir.AxisListType.X

P = 128
D = 1024
KD = D // P
TOK = 128
REQ = 2
DEPTH = 2
LAYERS = 2
H, KV, HD = 8, 2, 64
GRP = H // KV
RQ, RKV, NOPE, ROPE, VD = 256, 128, 64, 32, 64
QK = NOPE + ROPE
A_Q, A_K, A_V = 0, H * HD, (H + KV) * HD
A_CQ = (H + 2 * KV) * HD
A_CKV = A_CQ + RQ
A_KR = A_CKV + RKV
W_AB = A_KR + ROPE
SC_A = HD ** -0.5
SC_M = QK ** -0.5
NE, TOPK, FF = 64, 6, 128
ROUTED = 2.5
ALPHA = (2.0 * DEPTH) ** 0.25
LN_EPS, RMS_EPS = 1e-5, 1e-6
RING = 4
SLOT = 3 * KD * FF
NADA = 24
GRID_W, ROPE_BASE = 64, 10000.0

G5, C5, P5 = 64, 16, 64
CH = 8
NC5 = TOK // CH
CC = CH * C5


def wait(eng, sem, value):
    if not isinstance(value, int) or value > 0:
        eng.wait_ge(sem, value)


def shape_constants():
    ident = np.eye(P, dtype=np.float32)
    pick = np.zeros((4, 2 + 2 * P), np.float32)
    for row in range(4):
        pick[row, row % 2] = 1.0
        pick[row, 2 + P * (row % 2):2 + P * (row % 2) + P] = 1.0
    tok = np.arange(TOK)
    pos = np.stack([tok // GRID_W, tok % GRID_W], 1).astype(np.float32)

    def rope(width):
        quarter = width // 4
        inv = (np.float32(ROPE_BASE) ** (-np.arange(quarter, dtype=np.float32) / np.float32(quarter))).astype(np.float32)
        ang = (pos[:, :, None] * inv[None, None, :]).astype(np.float32)
        return np.stack([np.cos(ang), np.sin(ang)], 1).astype(np.float32).reshape(TOK, -1)

    table = np.concatenate([ident, rope(HD), rope(ROPE), np.tile(np.arange(NE, dtype=np.float32), (P, 1))], 1)
    step = np.arange(P) // C5
    later = (step[None, :] >= step[:, None]).astype(np.float32)
    masks = np.stack([later, later.T], 1).reshape(P, 2 * P)
    return (np.ascontiguousarray(np.concatenate([table, masks], 1)), np.ascontiguousarray(pick))


T_ID = 0
T_RA = P
T_RM = T_RA + HD
T_IO = T_RM + ROPE
T_MK = T_IO + NE
T_W = T_MK + 2 * P


def build(nc, t, outs):
    y_out = outs[0:2]
    k_out, v_out, ckv_out, kr_out, ssm_out = outs[2:7]

    top = ExitStack()
    with top:
        def sb(name, shape, dt=F32, scope=top):
            return scope.enter_context(nc.sbuf_tensor(name, shape, dt))

        layer_sems = []

        def sem(name):
            layer_sems.append(nc.alloc_semaphore(name=name))
            return layer_sems[-1]

        def lasting_sem(name):
            return nc.alloc_semaphore(name=name)

        PS = top.enter_context(nc.psum_tensor("PS", [P, 8, 512], F32))
        table = sb("table", [P, T_W])
        pick = sb("pick", [4, 2 + 2 * P])
        ident = table[:, T_ID:T_ID + P]
        X = sb("X", [P, REQ, D])
        HTh = sb("HTh", [P, KD, REQ * TOK], F32R)
        HTl = sb("HTl", [P, KD, REQ * TOK], F32R)
        G = sb("G", [P, 2, REQ, D])
        COL = sb("COL", [P, 4, KD, REQ])
        stat = sb("stat", [P, 64])
        eps = sb("eps", [P, 2])
        raw = [sb(f"raw{i}", [P, SLOT]) for i in range(RING)]
        gate_rows = nc.dram_tensor("gate_rows", [DEPTH, NE, REQ * TOK], F32, kind="Internal").ap()

        s_const = lasting_sem("constants_landed")
        s_x = lasting_sem("x_landed")
        s_eps = lasting_sem("eps_ready")
        s_out = lasting_sem("outputs_stored")
        n_out = [0]
        act_link = lasting_sem("act_step_done")
        dve_link = lasting_sem("dve_step_done")
        links = {"act": 0, "dve": 0}

        def act_step(act, ins):
            links["act"] += 1
            ins.then_inc(act_link, 1)
            act.wait_ge(act_link, links["act"])

        def dve_step(dve, ins):
            links["dve"] += 1
            ins.then_inc(dve_link, 1)
            dve.wait_ge(dve_link, links["dve"])

        def store(eng, out, in_):
            n_out[0] += 16
            eng.dma_start(out, in_).then_inc(s_out, 16)

        class Stream:
            def __init__(self, name, sources):
                self.src = sources
                self.landed = [sem(f"{name}_landed{i}") for i in range(RING)]
                self.hi = sem(f"{name}_high_parts")
                self.lo = sem(f"{name}_low_parts")
                self.used = sem(f"{name}_multiplied")

            def load(self, sp, b):
                src = self.src(b)
                width = 1
                for n in src.shape[1:]:
                    width *= n
                dst = raw[b % RING][:, 0:width]
                if len(src.shape) == 3:
                    dst = dst.rearrange("p (k n) -> p k n", k=src.shape[1])
                sp.dma_start(dst, src).then_inc(self.landed[b % RING], 16)

        def colblocks(name, w, width, count):
            view = w.rearrange("(p k) n -> p k n", k=KD)
            return Stream(name, lambda b: view[:, :, b * width:(b + 1) * width]), count, width

        def ada(l, prefetch):
            with ExitStack() as scope:
                wh = [sb(f"ada{l}_wh{i}", [P, KD, 256], F32R, scope) for i in range(2)]
                wl = [sb(f"ada{l}_wl{i}", [P, KD, 256], F32R, scope) for i in range(2)]
                row4 = sb(f"ada{l}_row4", [4, 6 * D], F32, scope)
                bias4 = sb(f"ada{l}_bias4", [4, 6 * D], F32, scope)
                craw = sb(f"ada{l}_c", [P, REQ, KD], F32, scope)
                csil = sb(f"ada{l}_silu", [P, KD, REQ], F32, scope)
                cs = sb(f"ada{l}_cs", [P, KD, 4], F32R, scope)
                n = f"ada{l}_"
                landed = [sem(f"{n}weights_landed{i}") for i in range(RING)]
                c_landed, b_landed, b_zero = sem(n + "c_landed"), sem(n + "bias_landed"), sem(n + "bias_zeroed")
                c_silu, c_hi, c_lo = sem(n + "c_silu"), sem(n + "c_high"), sem(n + "c_low")
                w_hi, w_lo = sem(n + "weights_high"), sem(n + "weights_low")
                rows_mm, rows = sem(n + "rows_multiplied"), sem(n + "rows_ready")
                cols_mm, cols = sem(n + "columns_multiplied"), sem(n + "columns_ready")
                gates_mm, gates_ready = sem(n + "gates_multiplied"), sem(n + "gates_ready")
                w_view = t["ada_w"][l].rearrange("(p k) n -> p k n", k=KD)
                GB = [3, 4, 5, 6, 7, 0, 1, 2]
                with nc.Block() as block:
                    @block.sync
                    def _(sp):
                        if l == 0:
                            sp.dma_start(table[:, :], t["table"]).then_inc(s_const, 16)
                            sp.dma_start(pick[:, :], t["pick"]).then_inc(s_const, 16)
                        sp.dma_start(craw[:, 0, :], t["c_ctx"].rearrange("(p k) -> p k", k=KD)).then_inc(c_landed, 16)
                        sp.dma_start(craw[:, 1, :], t["c"][0].rearrange("(p k) -> p k", k=KD)).then_inc(c_landed, 16)

                        def load(it, j):
                            b = it * RING + j
                            wait(sp, w_lo, b - RING + 1)
                            sp.dma_start(raw[j][:, 0:KD * 256].rearrange("p (k n) -> p k n", k=KD),
                                         w_view[:, :, bass.ds(b * 256, 256)]).then_inc(landed[j], 16)
                        for j in range(RING):
                            load(0, j)
                        sp.wait_ge(b_zero, 1)
                        sp.dma_start(bias4[0:2, :], t["ada_b"][l:l + 1, :].partition_broadcast(2)).then_inc(b_landed, 16)
                        if l == 0:
                            sp.dma_start(X[:, 0, :], t["x_prompt"][0]).then_inc(s_x, 16)
                            sp.dma_start(X[:, 1, :], t["x_sample"][0]).then_inc(s_x, 16)
                        with sp.Fori(1, NADA // RING) as it:
                            for j in range(RING):
                                load(it, j)
                        for j in range(RING):
                            sp.wait_ge(w_lo, NADA - RING + j + 1)
                            prefetch(sp, j)

                    @block.scalar
                    def _(act):
                        act.wait_ge(c_landed, 32)
                        act.activation(csil[:, :, :], craw[:, :, :].rearrange("p r k -> p k r"), ACT.Silu).then_inc(c_silu, 1)
                        act.wait_ge(c_silu, 1)
                        act.activation(cs[:, :, 0:2], csil[:, :, :], ACT.Copy).then_inc(c_hi, 1)

                        def high(it, j):
                            b = it * RING + j
                            act.wait_ge(landed[j], it * 16 + 16)
                            wait(act, rows_mm, b - 1)
                            act.activation(wh[j % 2][:, :, :], raw[j][:, 0:KD * 256].rearrange("p (k n) -> p k n", k=KD),
                                           ACT.Copy).then_inc(w_hi, 1)
                        for j in range(RING):
                            high(0, j)
                        with act.Fori(1, NADA // RING) as it:
                            for j in range(RING):
                                high(it, j)
                        for i in range(8):
                            act.wait_ge(gates_mm, i + 1)
                            act.activation(G[:, i // 4, i // 2 % 2, i % 2 * 512:i % 2 * 512 + 512], PS[:, GB[i], :],
                                           ACT.Copy).then_inc(gates_ready, 1)
                        act.wait_ge(gates_ready, 8)

                    @block.vector
                    def _(dve):
                        if l == 0:
                            dve.memset(eps[:, 0:1], LN_EPS)
                            dve.memset(eps[:, 1:2], RMS_EPS).then_inc(s_eps, 1)
                        dve.memset(bias4[:, :], 0.0).then_inc(b_zero, 1)
                        dve.wait_ge(c_hi, 1)
                        dve.tensor_tensor(cs[:, :, 2:4], csil[:, :, :], cs[:, :, 0:2].bitcast(F32), ALU.subtract).then_inc(c_lo, 1)

                        def low(it, j):
                            b = it * RING + j
                            dve.wait_ge(w_hi, b + 1)
                            wait(dve, rows_mm, b - 1)
                            dve.tensor_tensor(wl[j % 2][:, :, :], raw[j][:, 0:KD * 256].rearrange("p (k n) -> p k n", k=KD),
                                              wh[j % 2][:, :, :].bitcast(F32), ALU.subtract).then_inc(w_lo, 1)

                        def row(it, j):
                            b = it * RING + j
                            dve.wait_ge(rows_mm, b + 1)
                            at = bass.ds(b * 256, 256)
                            dve.tensor_tensor(row4[:, at], PS[0:4, j % 2, 0:256], bias4[:, at], ALU.add).then_inc(rows, 1)
                        low(0, 0)
                        dve.wait_ge(b_landed, 16)
                        for j in range(1, RING):
                            low(0, j)
                            row(0, j - 1)
                        with dve.Fori(1, NADA // RING) as it:
                            for j in range(RING):
                                low(it, j)
                                if j:
                                    row(it, j - 1)
                                else:
                                    row(it - 1, RING - 1)
                        row(NADA // RING - 1, RING - 1)
                        dve.wait_ge(cols_mm, 1)
                        c4 = PS[:, 2, 0:4 * KD * REQ].rearrange("p (s k r) -> p s k r", s=4, k=KD)
                        for s in range(4):
                            dve.tensor_scalar(COL[:, s, :, :], c4[:, s, :, :], float(s % 2), None, ALU.add).then_inc(cols, 1)
                        dve.wait_ge(cols, 4)

                    @block.tensor
                    def _(pe):
                        pe.wait_ge(c_lo, 1)

                        def rows_product(it, j):
                            b = it * RING + j
                            pe.wait_ge(w_lo, b + 1)
                            wait(pe, rows, b - 1)
                            for k in range(KD):
                                pe.matmul(PS[0:4, j % 2, 0:256], cs[:, k, :], wh[j % 2][:, k, :], start=(k == 0), stop=False)
                                mm = pe.matmul(PS[0:4, j % 2, 0:256], cs[:, k, :], wl[j % 2][:, k, :], start=False, stop=(k == KD - 1))
                            mm.then_inc(rows_mm, 1)
                        for j in range(RING):
                            rows_product(0, j)
                        with pe.Fori(1, NADA // RING) as it:
                            for j in range(RING):
                                rows_product(it, j)
                        pe.wait_ge(rows, NADA)
                        pe.wait_ge(s_const, 32)
                        for s, which in enumerate((0, 1, 3, 4)):
                            for k in range(KD):
                                at = (s * KD + k) * REQ
                                mm = pe.matmul(PS[:, 2, at:at + REQ], row4[:, which * D + k:which * D + D:KD], pick[:, 0:2],
                                               start=True, stop=True)
                        mm.then_inc(cols_mm, 1)
                        for i in range(8):
                            if i == 7:
                                pe.wait_ge(cols, 4)
                            src = (2 if i < 4 else 5) * D + i % 2 * 512
                            pe.matmul(PS[:, GB[i], :], pick[:, 2 + P * (i // 2 % 2):2 + P * (i // 2 % 2) + P], row4[:, src:src + 512],
                                      start=True, stop=True).then_inc(gates_mm, 1)

        class Modulate:
            def __init__(self, name, s, scope):
                self.s = s
                self.HT = sb(name + "_HT", [P, KD, REQ * TOK], F32, scope)
                self.turned = sem(name + "_turned")
                self.mod = [sem(f"{name}_modulated{r}") for r in range(REQ)]
                self.hi = sem(name + "_high")
                self.lo = sem(name + "_low")

            def tensor(self, pe):
                for r in range(REQ):
                    for half in range(2):
                        for i in range(4):
                            k = half * 4 + i
                            mm = pe.transpose(PS[:, 2 * r + half, i * P:(i + 1) * P], X[:, r, k:D:KD], ident)
                        mm.then_inc(self.turned, 1)

            def scalar(self, act):
                act.wait_ge(self.turned, 2)
                for k in range(KD):
                    act.activation(self.HT[:, k, 0:TOK], PS[:, k // 4, k % 4 * P:k % 4 * P + P], ACT.Identity,
                                   bias=COL[:, self.s, k, 0:1], scale=COL[:, self.s + 1, k, 0:1]).then_inc(self.mod[0], 1)
                act.wait_ge(self.mod[0], KD)
                act.activation(HTh[:, :, 0:TOK], self.HT[:, :, 0:TOK], ACT.Copy).then_inc(self.hi, 1)
                act.wait_ge(self.mod[1], KD)
                act.activation(HTh[:, :, TOK:], self.HT[:, :, TOK:], ACT.Copy).then_inc(self.hi, 1)

            def vector(self, dve):
                dve.wait_ge(self.turned, 4)
                for k in range(KD):
                    dve.tensor_scalar(self.HT[:, k, TOK:], PS[:, 2 + k // 4, k % 4 * P:k % 4 * P + P],
                                      COL[:, self.s + 1, k, 1:2], COL[:, self.s, k, 1:2], ALU.mult, ALU.add).then_inc(self.mod[1], 1)
                for r in range(REQ):
                    dve.wait_ge(self.hi, r + 1)
                    at = slice(r * TOK, (r + 1) * TOK)
                    dve.tensor_tensor(HTl[:, :, at], self.HT[:, :, at], HTh[:, :, at].bitcast(F32), ALU.subtract).then_inc(self.lo, 1)

        def three(pe, out, ah, al, bh, bl, start, stop):
            pe.matmul(out, ah, bh, start=start, stop=False, skip_group_check=True)
            pe.matmul(out, ah, bl, start=False, stop=False, skip_group_check=True)
            return pe.matmul(out, al, bh, start=False, stop=stop, skip_group_check=True)

        class Norm:
            def __init__(self, name, l, ffn, banks, out_ready, scope, g_ap, b_ap):
                self.name, self.l, self.ffn, self.banks, self.out_ready = name, l, ffn, banks, out_ready
                self.gb = sb(name + "_gain_bias", [P, 2, D], F32, scope)
                self.tmp = sb(name + "_tmp", [P, REQ, D], F32, scope)
                self.st = sb(name + "_stats", [P, REQ, 2, 6], F32, scope)
                self.mv = sb(name + "_mean_var", [P, REQ, 2], F32, scope)
                self.rs = sb(name + "_rstd", [P, REQ, 4], F32, scope)
                self.landed = sem(name + "_gain_landed")
                self.var = sem(name + "_variance")
                self.std = sem(name + "_std")
                self.coef = sem(name + "_coefficients")
                self.unit = sem(name + "_unit")
                self.done = sem(name + "_done")
                self.g_ap, self.b_ap = g_ap, b_ap
                self.source = lambda r, n: PS[:, self.banks[2 * r + n], :]

            def sync(self, sp):
                sp.dma_start(self.gb[:, 0, :], self.g_ap.partition_broadcast(P)).then_inc(self.landed, 16)
                sp.dma_start(self.gb[:, 1, :], self.b_ap.partition_broadcast(P)).then_inc(self.landed, 16)

            def vector(self, dve):
                for r in range(REQ):
                    self.out_ready(dve, r)
                    for n in range(2):
                        at = slice(n * 512, n * 512 + 512)
                        i = dve.tensor_tensor(self.tmp[:, r, at], self.source(r, n), G[:, self.ffn, r, at], ALU.mult)
                    dve_step(dve, i)
                    dve_step(dve, dve.scalar_tensor_tensor(self.tmp[:, r, :], X[:, r, :], ALPHA, self.tmp[:, r, :], ALU.mult, ALU.add))
                    for n in range(2):
                        i = dve.bn_stats(self.st[:, r, n, :], self.tmp[:, r, n * 512:n * 512 + 512])
                    dve_step(dve, i)
                    dve.bn_aggr(self.mv[:, r, :], self.st[:, r, :, :]).then_inc(self.var, 1)
                for r in range(REQ):
                    dve.wait_ge(self.std, r + 1)
                    dve_step(dve, dve.reciprocal(self.rs[:, r, 1:2], self.rs[:, r, 0:1]))
                    dve.scalar_tensor_tensor(self.rs[:, r, 2:3], self.mv[:, r, 0:1], -1.0, self.rs[:, r, 1:2],
                                             ALU.mult, ALU.mult).then_inc(self.coef, 1)
                dve.wait_ge(self.landed, 32)
                for r in range(REQ):
                    dve.wait_ge(self.unit, r + 1)
                    dve_step(dve, dve.tensor_tensor(X[:, r, :], self.tmp[:, r, :], self.gb[:, 0, :], ALU.mult))
                    dve.tensor_tensor(X[:, r, :], X[:, r, :], self.gb[:, 1, :], ALU.add).then_inc(self.done, 1)
                dve.wait_ge(self.done, REQ)

            def scalar(self, act):
                act.wait_ge(s_eps, 1)
                for r in range(REQ):
                    act.wait_ge(self.var, r + 1)
                    act.activation(self.rs[:, r, 0:1], self.mv[:, r, 1:2], ACT.Sqrt, bias=eps[:, 0:1]).then_inc(self.std, 1)
                for r in range(REQ):
                    act.wait_ge(self.coef, r + 1)
                    act.activation(self.tmp[:, r, :], self.tmp[:, r, :], ACT.Identity, bias=self.rs[:, r, 2:3],
                                   scale=self.rs[:, r, 1:2]).then_inc(self.unit, 1)

        class Project:
            def __init__(self, name, w, width, count, bank, lh, ll, scope, evac):
                self.name, self.width, self.count, self.bank, self.lh, self.ll, self.evac = name, width, count, bank, lh, ll, evac
                self.view = w.rearrange("(p k) n -> p k n", k=KD)
                self.wh = [sb(f"{name}_wh{i}", [P, KD, width], F32R, scope) for i in range(2)]
                self.wl = [sb(f"{name}_wl{i}", [P, KD, width], F32R, scope) for i in range(2)]
                self.landed = [sem(f"{name}_landed{i}") for i in range(RING)]
                self.hi, self.lo = sem(name + "_high"), sem(name + "_low")
                self.mm = sem(name + "_multiplied")
                self.ready = [sem(f"{name}_out{r}") for r in range(REQ)]

            def raw(self, b):
                return raw[b % RING][:, 0:KD * self.width].rearrange("p (k n) -> p k n", k=KD)

            def load(self, sp, b):
                sp.dma_start(self.raw(b), self.view[:, :, b * self.width:(b + 1) * self.width]).then_inc(self.landed[b % RING], 16)

            def sync(self, sp):
                for b in range(RING, self.count):
                    sp.wait_ge(self.lo, b - RING + 1)
                    self.load(sp, b)

            def scalar(self, act):
                for b in range(self.count + 1):
                    if b < self.count:
                        act.wait_ge(self.landed[b % RING], 16 * (b // RING + 1))
                        wait(act, self.mm, 2 * (b - 1))
                        act.activation(self.wh[b % 2][:, :, :], self.raw(b), ACT.Copy).then_inc(self.hi, 1)
                    if b and self.evac:
                        act.wait_ge(self.mm, 2 * b - 1)
                        self.evac(act, b - 1, 0).then_inc(self.ready[0], 1)

            def vector(self, dve):
                for b in range(self.count + 1):
                    if b < self.count:
                        dve.wait_ge(self.hi, b + 1)
                        dve.tensor_tensor(self.wl[b % 2][:, :, :], self.raw(b), self.wh[b % 2][:, :, :].bitcast(F32),
                                          ALU.subtract).then_inc(self.lo, 1)
                    if b and self.evac:
                        dve.wait_ge(self.mm, 2 * b)
                        self.evac(dve, b - 1, 1).then_inc(self.ready[1], 1)

            def tensor(self, pe):
                for b in range(self.count):
                    pe.wait_ge(self.lo, b + 1)
                    for r in range(REQ):
                        out = self.bank(b, r)
                        for k in range(KD):
                            at = slice(r * TOK, r * TOK + TOK)
                            mm = three(pe, out, self.lh[:, k, at], self.ll[:, k, at], self.wh[b % 2][:, k, :], self.wl[b % 2][:, k, :],
                                       start=(k == 0), stop=(k == KD - 1))
                        mm.then_inc(self.mm, 1)

        class Turn:
            def __init__(self, name, src, oh, ol):
                self.src, self.oh, self.ol = src, oh, ol
                self.turned, self.hi, self.lo = sem(name + "_turned"), sem(name + "_high"), sem(name + "_low")

            def tensor(self, pe):
                for r in range(REQ):
                    for half in range(2):
                        for i in range(4):
                            k = half * 4 + i
                            mm = pe.transpose(PS[:, 2 * r + half, i * P:(i + 1) * P], self.src[:, r, k:D:KD], ident)
                        mm.then_inc(self.turned, 1)

            def scalar(self, act):
                for q in range(4):
                    act.wait_ge(self.turned, q + 1)
                    act.activation(self.oh[:, q % 2 * 4:q % 2 * 4 + 4, q // 2 * TOK:q // 2 * TOK + TOK],
                                   PS[:, q, :].rearrange("p (k t) -> p k t", k=4), ACT.Copy).then_inc(self.hi, 1)

            def vector(self, dve):
                for q in range(4):
                    dve.wait_ge(self.hi, q + 1)
                    at = (slice(None), slice(q % 2 * 4, q % 2 * 4 + 4), slice(q // 2 * TOK, q // 2 * TOK + TOK))
                    dve.tensor_tensor(self.ol[at], PS[:, q, :].rearrange("p (k t) -> p k t", k=4), self.oh[at].bitcast(F32),
                                      ALU.subtract).then_inc(self.lo, 1)

        class Attend:
            def __init__(self, name, QT, KT, V, dim, scale, sink, merged, at, bufs):
                self.n, self.QT, self.KT, self.V, self.dim, self.scale, self.sink, self.merged, self.at = \
                    name, QT, KT, V, dim, scale, sink, merged, at
                self.Pb, self.PT = bufs
                self.st = sb(name + "_softmax", [P, 8, REQ, H], F32, mix_scope[0])
                self.scores, self.maxed = sem(name + "_scores"), sem(name + "_negmax")
                self.probs, self.tot, self.es = sem(name + "_probs"), sem(name + "_rowsums"), sem(name + "_sink_exp")
                self.pturn, self.pt = sem(name + "_probs_turned"), [sem(f"{name}_probsT{i}") for i in range(2)]
                self.pv, self.done = sem(name + "_values"), sem(name + "_merged")

            def sbank(self, r):
                if r == 0:
                    return PS[:, 0:2, :].rearrange("p b (h k) -> p (b h) k", k=TOK)
                return PS[:, 2:6, :].rearrange("p b (h k) -> p (b h) k", k=2 * TOK)

            def tensor(self, pe):
                for r in range(REQ):
                    for h in range(H):
                        mm = pe.matmul(self.sbank(r)[:, h, :], self.QT[0:self.dim, r, h, :],
                                       self.KT(h, r, 1 + r), start=True, stop=True)
                    mm.then_inc(self.scores, 1)
                for c in range(6):
                    if c < 2:
                        pe.wait_ge(self.probs, 4 * c + 4)
                        if c == 0:
                            pe.wait_ge(self.probs, 8)
                    else:
                        pe.wait_ge(self.probs, 8 + 2 * (c - 1))
                        if c == 2:
                            pe.wait_ge(self.probs, 16)
                    bank = [6, 7, 0, 1, 2, 3][c]
                    if c >= 2:
                        pe.wait_ge(self.probs, 16)
                    for i in range(4):
                        mm = pe.transpose(PS[:, bank, i * P:(i + 1) * P], self.Pb[:, (4 * c + i) * P:(4 * c + i + 1) * P], ident)
                    mm.then_inc(self.pturn, 1)
                for r in range(REQ):
                    pe.wait_ge(self.pt[0], 1 if r == 0 else 3)
                    pe.wait_ge(self.pt[1], 1 if r == 0 else 3)
                    for h in range(H):
                        out = PS[:, 4 + r, h * VD:(h + 1) * VD]
                        if r == 0:
                            mm = pe.matmul(out, self.PT[:, h * P:(h + 1) * P], self.V(h, 0), start=True, stop=True)
                        else:
                            for s in range(2):
                                c = H + 2 * h + s
                                mm = pe.matmul(out, self.PT[:, c * P:(c + 1) * P], self.V(h, 1 + s), start=(s == 0), stop=(s == 1))
                    mm.then_inc(self.pv, 1)

            def vector(self, dve):
                st = self.st
                for r in range(REQ):
                    dve.wait_ge(self.scores, r + 1)
                    dve_step(dve, dve.tensor_reduce(st[:, 0, r, :], self.sbank(r), AX_X, ALU.max))
                    if self.sink is None:
                        dve.tensor_scalar(st[:, 1, r, :], st[:, 0, r, :], -self.scale, None, ALU.mult).then_inc(self.maxed, 1)
                    else:
                        dve_step(dve, dve.scalar_tensor_tensor(st[:, 2, r, :], st[:, 0, r, :], self.scale, self.sink, ALU.mult, ALU.max))
                        dve_step(dve, dve.tensor_scalar(st[:, 1, r, :], st[:, 2, r, :], -1.0, None, ALU.mult))
                        dve.tensor_tensor(st[:, 3, r, :], self.sink, st[:, 1, r, :], ALU.add).then_inc(self.maxed, 1)
                for c in (1, 3, 5):
                    dve.wait_ge(self.pturn, c + 1)
                    bank = [6, 7, 0, 1, 2, 3][c]
                    dve.tensor_copy(self.PT[:, 4 * c * P:4 * (c + 1) * P], PS[:, bank, :]).then_inc(self.pt[1], 1)
                for r in range(REQ):
                    if self.sink is None:
                        dve.wait_ge(self.probs, 16)
                        dve_step(dve, dve.reciprocal(st[:, 6, r, :], st[:, 4, r, :]))
                    else:
                        dve.wait_ge(self.es, r + 1)
                        dve_step(dve, dve.tensor_tensor(st[:, 7, r, :], st[:, 4, r, :], st[:, 5, r, :], ALU.add))
                        dve_step(dve, dve.reciprocal(st[:, 6, r, :], st[:, 7, r, :]))
                    dve.wait_ge(self.pv, r + 1)
                    dve.tensor_tensor(self.merged[:, r, self.at:self.at + H * VD].rearrange("p (h e) -> p h e", h=H),
                                      PS[:, 4 + r, :].rearrange("p (h e) -> p h e", h=H),
                                      st[:, 6, r, :].unsqueeze(2).to_broadcast([P, H, VD]), ALU.mult).then_inc(self.done, 1)

            def scalar(self, act):
                st = self.st
                for r in range(REQ):
                    act.wait_ge(self.maxed, r + 1)
                    for h in range(H):
                        w = TOK * (1 + r)
                        base = h * TOK if r == 0 else H * TOK + 2 * h * TOK
                        act.activation(self.Pb[:, base:base + w], self.sbank(r)[:, h, :], ACT.Exp, bias=st[:, 1, r, h:h + 1],
                                       scale=self.scale, accum_out=st[:, 4, r, h:h + 1]).then_inc(self.probs, 1)
                    if self.sink is not None:
                        act.activation(st[:, 5, r, :], st[:, 3, r, :], ACT.Exp).then_inc(self.es, 1)
                for c in (0, 2, 4):
                    act.wait_ge(self.pturn, c + 1)
                    bank = [6, 7, 0, 1, 2, 3][c]
                    act.activation(self.PT[:, 4 * c * P:4 * (c + 1) * P], PS[:, bank, :], ACT.Copy).then_inc(self.pt[0], 1)

        mix_scope = [None]

        def mixer0(project_in, project_out_holder, prefetch_next):
            proj, merged = project_in.proj, project_in.merged
            with ExitStack() as scope:
                mod = Modulate("mix0_mod", 0, scope)
                pr = project_in
                pr.alloc(scope)
                with nc.Block() as block:
                    @block.sync
                    def _(sp):
                        sp.wait_ge(pr.p.lo, 1)
                        sp.dma_start(raw[0][:, 0:2 * H * QK].rearrange("p (k n) -> p k n", k=2),
                                     t["mla_w_uq"][0].rearrange("(p k) n -> p k n", k=2)).then_inc(pr.uq_landed, 16)
                        sp.dma_start(raw[0][:, 2 * H * QK:2 * H * QK + H * (NOPE + VD)], t["mla_w_ukv"][0]).then_inc(pr.uq_landed, 16)

                    @block.tensor
                    def _(pe):
                        pe.wait_ge(s_x, 32)
                        mod.tensor(pe)
                        pe.wait_ge(mod.lo, 2)
                        pr.p.tensor(pe)

                    @block.scalar
                    def _(act):
                        mod.scalar(act)
                        pr.p.scalar(act)
                        act.wait_ge(pr.p.ready[0], pr.p.count)

                    @block.vector
                    def _(dve):
                        mod.vector(dve)
                        pr.p.vector(dve)
                        dve.wait_ge(pr.p.ready[1], pr.p.count)
            with ExitStack() as scope:
                mix_scope[0] = scope
                Pb = sb("probs", [P, 3 * H * TOK], F32, scope)
                PT = sb("probsT", [P, 3 * H * TOK], F32, scope)
                QT = sb("QT", [QK, REQ, H, TOK], F32, scope)
                KT = sb("KT", [QK, H, 3, TOK], F32, scope)
                cq = sb("cq_n", [P, REQ, RQ], F32, scope)
                ckv = sb("ckv_n", [P, 3, RKV], F32, scope)
                cqT = sb("cqT", [P, 2, REQ, TOK], F32, scope)
                ckvT = sb("ckvT", [P, 3, TOK], F32, scope)
                QM = sb("QM", [P, REQ, H, QK], F32, scope)
                KM = sb("KM", [P, 3, H, QK], F32, scope)
                VM = sb("VM", [P, 3, H, VD], F32, scope)
                kcv = sb("cache_kv", [P, 2, KV * HD], F32, scope)
                krc = sb("cache_kr", [P, ROPE], F32, scope)
                norms = sb("norm_gains", [P, RQ + RKV], F32, scope)
                sink = sb("sink_b", [P, H], F32, scope)
                rt = sb("rope_tmp", [P, 4, 10 * 32], F32, scope)
                rms = sb("rms", [P, 3, 4], F32, scope)
                junk = sb("junk", [P, RQ], F32, scope)
                landed = sem("attn_inputs_landed")
                roped, kr_roped = sem("rope_done"), sem("mla_k_rope_done")
                a_turn, a_t = sem("a_turned"), [sem("a_turned_act"), sem("a_turned_dve")]
                sq, msq, std, rmsed = sem("rms_squares"), sem("rms_mean"), sem("rms_root"), sem("rms_done")
                c_turn, cT = sem("c_turned"), sem("cT_ready")
                qm_mm, qm = sem("qm_multiplied"), sem("qm_ready")
                kv_mm, kv_e = sem("kv_multiplied"), [sem("kv_act"), sem("kv_dve")]
                qroped = sem("qm_roped")
                m_turn, m_t = sem("m_turned"), [sem("m_turned_act"), sem("m_turned_dve")]
                kfill = sem("k_rope_filled")
                proj_v = proj
                atA = Attend("attA", QT, lambda h, s, n: KT[0:HD, h // GRP, s:s + n, :],
                             lambda h, s: (proj[:, s, A_V + h // GRP * HD:A_V + (h // GRP + 1) * HD] if s < 2
                                           else kcv[:, 1, h // GRP * HD:(h // GRP + 1) * HD]),
                             HD, SC_A, sink[:, :], merged, 0, (Pb, PT))
                atM = Attend("attM", QT, lambda h, s, n: KT[0:QK, h, s:s + n, :], lambda h, s: VM[:, s, h, :],
                             QK, SC_M, None, merged, H * HD, (Pb, PT))

                def rotate(dve, src, heads, quarter, tab):
                    x = src.rearrange("p h (a b w) -> p h a b w", a=2, b=2)
                    x1, x2 = x[:, :, :, 0, :], x[:, :, :, 1, :]
                    cs = tab.rearrange("p (s a w) -> p s a w", s=2, a=2)
                    shape = [P, heads, 2, quarter]
                    co = cs[:, 0, :, :].unsqueeze(1).to_broadcast(shape)
                    si = cs[:, 1, :, :].unsqueeze(1).to_broadcast(shape)
                    tm = [rt[:, i, 0:heads * 2 * quarter].rearrange("p (h a w) -> p h a w", h=heads, a=2) for i in range(4)]
                    dve.tensor_tensor(tm[0], x1, co, ALU.mult)
                    dve.tensor_tensor(tm[1], x2, si, ALU.mult)
                    dve.tensor_tensor(tm[2], x1, si, ALU.mult)
                    dve_step(dve, dve.tensor_tensor(tm[3], x2, co, ALU.mult))
                    dve_step(dve, dve.tensor_tensor(x1, tm[0], tm[1], ALU.subtract))
                    return dve.tensor_tensor(x2, tm[2], tm[3], ALU.add)

                def a_copy(eng, q):
                    src = PS[0:HD, q, :]
                    if q < 4:
                        dst = QT[0:HD, q // 2, q % 2 * 4:q % 2 * 4 + 4, :]
                        src = src.rearrange("p (h t) -> p h t", h=4)
                    else:
                        src = src[:, 0:3 * TOK].rearrange("p (h t) -> p h t", h=3)
                        dst = KT[0:HD, q - 4, :, :]
                    if q % 2 == 0:
                        eng.activation(dst, src, ACT.Copy).then_inc(a_t[0], 1)
                    else:
                        eng.tensor_copy(dst, src).then_inc(a_t[1], 1)

                def kv_copy(eng, i):
                    eng.wait_ge(kv_mm, i + 1)
                    bank = [4, 5, 6, 7, 0, 1][i]
                    v = PS[:, bank, :].rearrange("p (h e) -> p h e", h=4)
                    hs = slice(i % 2 * 4, i % 2 * 4 + 4)
                    if i % 2 == 0:
                        eng.activation(KM[:, i // 2, hs, 0:NOPE], v[:, :, 0:NOPE], ACT.Copy)
                        eng.activation(VM[:, i // 2, hs, :], v[:, :, NOPE:], ACT.Copy).then_inc(kv_e[0], 1)
                    else:
                        eng.tensor_copy(KM[:, i // 2, hs, 0:NOPE], v[:, :, 0:NOPE])
                        eng.tensor_copy(VM[:, i // 2, hs, :], v[:, :, NOPE:]).then_inc(kv_e[1], 1)

                MB = [2, 3, 4, 5, 6, 7, 0, 1, 2, 3]

                def m_copy(eng, q):
                    src = PS[0:QK, MB[q], :].rearrange("p (h t) -> p h t", h=4)
                    hs = slice(q % 2 * 4, q % 2 * 4 + 4)
                    dst = QT[:, q // 2, hs, :] if q < 4 else KT[:, hs, (q - 4) // 2, :]
                    if q % 2 == 0:
                        eng.activation(dst, src, ACT.Copy).then_inc(m_t[0], 1)
                    else:
                        eng.tensor_copy(dst, src).then_inc(m_t[1], 1)

                with nc.Block() as block:
                    @block.sync
                    def _(sp):
                        sp.dma_start(kcv[:, 0, :], t["cache_attn_k"][0, 0].rearrange("k h d -> k (h d)")).then_inc(landed, 16)
                        sp.dma_start(kcv[:, 1, :], t["cache_attn_v"][0, 0].rearrange("k h d -> k (h d)")).then_inc(landed, 16)
                        sp.dma_start(krc[:, :], t["cache_mla_krope"][0, 0]).then_inc(landed, 16)
                        sp.dma_start(ckv[:, 2, :], t["cache_mla_ckv"][0, 0]).then_inc(landed, 16)
                        sp.dma_start(sink[:, :], t["attn_sink"].partition_broadcast(P)).then_inc(landed, 16)
                        sp.dma_start(norms[:, 0:RQ], t["mla_q_norm"].partition_broadcast(P)).then_inc(landed, 16)
                        sp.dma_start(norms[:, RQ:], t["mla_kv_norm"].partition_broadcast(P)).then_inc(landed, 16)
                        store(sp, k_out[0, 0].rearrange("k h d -> k (h d)"), proj[:, 0, A_K:A_V])
                        store(sp, v_out[0, 0].rearrange("k h d -> k (h d)"), proj[:, 0, A_V:A_CQ])
                        store(sp, kr_out[0, 0], proj[:, 0, A_KR:W_AB])
                        sp.wait_ge(rmsed, 4)
                        store(sp, ckv_out[0, 0], ckv[:, 0, :])
                        for b in range(1, RING):
                            project_out_holder.load(sp, b)
                        sp.wait_ge(kv_mm, 6)
                        project_out_holder.load(sp, 0)
                        sp.wait_ge(s_out, n_out[0])

                    @block.scalar
                    def _(act):
                        for r in range(REQ):
                            act.activation(junk[:, 0:RQ], proj[:, r, A_CQ:A_CKV], ACT.Square, accum_out=rms[:, 0, 2 * r:2 * r + 1]).then_inc(sq, 1)
                            act.wait_ge(sq, 2 * r + 1)
                            act.activation(junk[:, 0:RKV], proj[:, r, A_CKV:A_KR], ACT.Square, accum_out=rms[:, 0, 2 * r + 1:2 * r + 2]).then_inc(sq, 1)
                            act.wait_ge(sq, 2 * r + 2)
                        act.wait_ge(msq, 2)
                        act.activation(rms[:, 2, :], rms[:, 1, :], ACT.Sqrt).then_inc(std, 1)
                        for q in (0, 2, 4):
                            act.wait_ge(a_turn, q + 1)
                            a_copy(act, q)
                        atA.scalar(act)
                        for q in range(2):
                            act.wait_ge(c_turn, q + 1)
                            if q == 0:
                                act.activation(cqT[:, :, :, :], PS[:, 6, :].rearrange("p (k r t) -> p k r t", k=2, r=2), ACT.Copy).then_inc(cT, 1)
                            else:
                                act.activation(ckvT[:, :, :], PS[:, 7, 0:3 * TOK].rearrange("p (s t) -> p s t", s=3), ACT.Copy).then_inc(cT, 1)
                        for i in range(4):
                            act.wait_ge(qm_mm, i + 1)
                            act.activation(QM[:, i // 2, i % 2 * 4:i % 2 * 4 + 4, :], PS[:, i, 0:4 * QK].rearrange("p (h d) -> p h d", h=4),
                                           ACT.Copy).then_inc(qm, 1)
                        for i in (0, 2, 4):
                            kv_copy(act, i)
                        for q in range(0, 10, 2):
                            act.wait_ge(m_turn, q + 1)
                            m_copy(act, q)
                        atM.scalar(act)

                    @block.vector
                    def _(dve):
                        rotate(dve, proj[:, 1, 0:A_V].rearrange("p (h d) -> p h d", d=HD), H + KV, HD // 4, table[:, T_RA:T_RM]).then_inc(roped, 1)
                        dve.wait_ge(roped, 1)
                        rotate(dve, proj[:, 1, A_KR:W_AB].unsqueeze(1), 1, ROPE // 4, table[:, T_RM:T_IO]).then_inc(kr_roped, 1)
                        dve.wait_ge(sq, 4)
                        for j, n in enumerate((RQ, RKV)):
                            dve.tensor_scalar(rms[:, 1, j:4:2], rms[:, 0, j:4:2], 1.0 / n, RMS_EPS, ALU.mult, ALU.add).then_inc(msq, 1)
                        dve.wait_ge(std, 1)
                        dve_step(dve, dve.reciprocal(rms[:, 0, :], rms[:, 2, :]))
                        dve.wait_ge(landed, 7 * 16)
                        for r in range(REQ):
                            dve.scalar_tensor_tensor(cq[:, r, :], proj[:, r, A_CQ:A_CKV], rms[:, 0, 2 * r:2 * r + 1], norms[:, 0:RQ],
                                                     ALU.mult, ALU.mult).then_inc(rmsed, 1)
                            dve.scalar_tensor_tensor(ckv[:, r, :], proj[:, r, A_CKV:A_KR], rms[:, 0, 2 * r + 1:2 * r + 2], norms[:, RQ:],
                                                     ALU.mult, ALU.mult).then_inc(rmsed, 1)
                        dve.wait_ge(kr_roped, 1)
                        for s in range(3):
                            src = krc[:, :] if s == 2 else proj[:, s, A_KR:W_AB]
                            dve.tensor_copy(KM[:, s, :, NOPE:], src.unsqueeze(1).to_broadcast([P, H, ROPE])).then_inc(kfill, 1)
                        for q in (1, 3, 5):
                            dve.wait_ge(a_turn, q + 1)
                            a_copy(dve, q)
                        atA.vector(dve)
                        dve.wait_ge(qm, 4)
                        rotate(dve, QM[:, 1, :, NOPE:], H, ROPE // 4, table[:, T_RM:T_IO]).then_inc(qroped, 1)
                        for i in (1, 3, 5):
                            kv_copy(dve, i)
                        for q in range(1, 10, 2):
                            dve.wait_ge(m_turn, q + 1)
                            m_copy(dve, q)
                        atM.vector(dve)
                        dve.wait_ge(atM.done, 2)

                    @block.tensor
                    def _(pe):
                        pe.wait_ge(landed, 7 * 16)
                        pe.wait_ge(roped, 1)
                        for q in range(4):
                            for i in range(4):
                                h = q % 2 * 4 + i
                                mm = pe.transpose(PS[0:HD, q, i * P:(i + 1) * P], proj[:, q // 2, h * HD:(h + 1) * HD], ident)
                            mm.then_inc(a_turn, 1)
                        for g in range(KV):
                            for s in range(3):
                                src = kcv[:, 0, g * HD:(g + 1) * HD] if s == 2 else proj[:, s, A_K + g * HD:A_K + (g + 1) * HD]
                                mm = pe.transpose(PS[0:HD, 4 + g, s * P:(s + 1) * P], src, ident)
                            mm.then_inc(a_turn, 1)
                        pe.wait_ge(a_t[0], 3)
                        pe.wait_ge(a_t[1], 3)
                        atA.tensor(pe)
                        pe.wait_ge(rmsed, 4)
                        for k in range(2):
                            for r in range(REQ):
                                mm = pe.transpose(PS[:, 6, (2 * k + r) * P:(2 * k + r + 1) * P], cq[:, r, k:RQ:2], ident)
                        mm.then_inc(c_turn, 1)
                        for s in range(3):
                            mm = pe.transpose(PS[:, 7, s * P:(s + 1) * P], ckv[:, s, :], ident)
                        mm.then_inc(c_turn, 1)
                        pe.wait_ge(cT, 2)
                        pe.wait_ge(project_in.uq_landed, 32)
                        uq = raw[0][:, 0:2 * H * QK].rearrange("p (k n) -> p k n", k=2)
                        for i in range(4):
                            for k in range(2):
                                mm = pe.matmul(PS[:, i, 0:4 * QK], cqT[:, k, i // 2, :], uq[:, k, i % 2 * 4 * QK:i % 2 * 4 * QK + 4 * QK],
                                               start=(k == 0), stop=(k == 1))
                            mm.then_inc(qm_mm, 1)
                        pe.wait_ge(atA.done, 2)
                        for i in range(6):
                            if i == 4:
                                pe.wait_ge(qm, 2)
                            bank = [4, 5, 6, 7, 0, 1][i]
                            w0 = 2 * H * QK + i % 2 * 512
                            pe.matmul(PS[:, bank, :], ckvT[:, i // 2, :], raw[0][:, w0:w0 + 512], start=True, stop=True).then_inc(kv_mm, 1)
                        pe.wait_ge(qm, 4)
                        pe.wait_ge(qroped, 1)
                        pe.wait_ge(kfill, 3)
                        pe.wait_ge(kv_e[0], 3)
                        pe.wait_ge(kv_e[1], 3)
                        for q in range(10):
                            if q >= 8:
                                pe.wait_ge(m_t[q % 2], (q - 8) // 2 + 1)
                            for i in range(4):
                                h = q % 2 * 4 + i
                                src = QM[:, q // 2, h, :] if q < 4 else KM[:, (q - 4) // 2, h, :]
                                mm = pe.transpose(PS[0:QK, MB[q], i * P:(i + 1) * P], src, ident)
                            mm.then_inc(m_turn, 1)
                        pe.wait_ge(m_t[0], 5)
                        pe.wait_ge(m_t[1], 5)
                        atM.tensor(pe)

        class In0:
            def __init__(self, scope):
                self.proj = sb("proj", [P, REQ, W_AB], F32, scope)
                self.merged = sb("merged", [P, REQ, D], F32, scope)
                self.uq_landed = sem("uq_landed")

            def alloc(self, scope):
                pass

        def ab_width():
            return W_AB // 4

        def run_layer0():
            with ExitStack() as outer:
                in0 = In0(outer)
                wi = ab_width()

                def evac_in(eng, b, r):
                    src = PS[:, (2 * b + r) % 8, 0:wi]
                    dst = in0.proj[:, r, b * wi:(b + 1) * wi]
                    return eng.activation(dst, src, ACT.Copy) if r == 0 else eng.tensor_copy(dst, src)
                w_in_holder = LateProject("w_in_ab", t["w_in_ab"][0], wi, 4, lambda b, r: PS[:, (2 * b + r) % 8, 0:wi], HTh, HTl, evac_in)
                ada(0, lambda sp, j: w_in_holder.load(sp, j))
                in0.p = w_in_holder
                in0.alloc = w_in_holder.alloc
                w_out = LateProject("w_out_ab", t["w_out_ab"][0], 256, 4,
                                    lambda b, r: PS[:, 4 + 2 * r + b // 2, b % 2 * 256:b % 2 * 256 + 256], None, None, None)
                mixer0(in0, w_out, None)
                with ExitStack() as scope:
                    MTh = sb("mergedT_h", [P, KD, REQ * TOK], F32R, scope)
                    MTl = sb("mergedT_l", [P, KD, REQ * TOK], F32R, scope)
                    w_out.lh, w_out.ll = MTh, MTl
                    w_out.alloc(scope)
                    turn = Turn("merged", in0.merged, MTh, MTl)
                    norm = Norm("ln_mix0", 0, 0, [4, 5, 6, 7], lambda e, r: e.wait_ge(w_out.mm, 8), scope, t["ln_mix_g"][0:1, :], t["ln_mix_b"][0:1, :])
                    with nc.Block() as block:
                        @block.sync
                        def _(sp):
                            norm.sync(sp)
                            for j in range(RING):
                                sp.wait_ge(w_out.lo, j + 1)
                                moes[0].load_weights(sp, 0, j)

                        @block.tensor
                        def _(pe):
                            turn.tensor(pe)
                            pe.wait_ge(turn.lo, 4)
                            w_out.tensor(pe)

                        @block.scalar
                        def _(act):
                            turn.scalar(act)
                            w_out.scalar(act)
                            norm.scalar(act)

                        @block.vector
                        def _(dve):
                            turn.vector(dve)
                            w_out.vector(dve)
                            norm.vector(dve)

        class LateProject(Project):
            def __init__(self, name, w, width, count, bank, lh, ll, evac):
                self.name, self.width, self.count, self.bank, self.lh, self.ll, self.evac = name, width, count, bank, lh, ll, evac
                self.view = w.rearrange("(p k) n -> p k n", k=KD)
                self.landed = [sem(f"{name}_landed{i}") for i in range(RING)]
                self.hi, self.lo = sem(name + "_high"), sem(name + "_low")
                self.mm = sem(name + "_multiplied")
                self.ready = [sem(f"{name}_out{r}") for r in range(REQ)]

            def alloc(self, scope):
                self.wh = [sb(f"{self.name}_wh{i}", [P, KD, self.width], F32R, scope) for i in range(2)]
                self.wl = [sb(f"{self.name}_wl{i}", [P, KD, self.width], F32R, scope) for i in range(2)]

        class Moe:
            def __init__(self, l):
                self.l = l
                n = f"moe{l}_"
                self.landed = [sem(f"{n}weights_landed{i}") for i in range(RING)]
                self.gate_landed = [sem(f"{n}gate_landed{i}") for i in range(RING)]
                names = ("up_high", "up_low", "down_high", "down_low", "up_multiplied", "down_multiplied",
                         "silu", "product", "gated", "hidden_high", "hidden_low",
                         "router_landed", "router_high", "router_low", "router_multiplied", "router_scores",
                         "gates", "gates_turned", "gatesT", "gates_stored")
                self.s = {k: sem(n + k) for k in names}

            def load_weights(self, sp, it, j):
                l, e = self.l, it * RING + j - 1
                if isinstance(e, int) and e < 0:
                    src = (t["sh_w_gate"][l], t["sh_w_up"][l], t["sh_w_down"][l])
                else:
                    src = [t[k][l, bass.ds(e, 1)].rearrange("o a b -> (o a) b") for k in ("exp_w_gate", "exp_w_up", "exp_w_down")]
                for i in range(2):
                    sp.dma_start(raw[j][:, i * D:(i + 1) * D], src[i].rearrange("(p k) f -> p (k f)", k=KD)).then_inc(self.landed[j], 16)
                sp.dma_start(raw[j][:, 2 * D:3 * D], src[2]).then_inc(self.landed[j], 16)

            def run(self, prefetch, final):
                l, s = self.l, self.s
                n = f"moe{l}_"
                GRPS = (NE - RING) // RING
                with ExitStack() as scope:
                    mod = Modulate(n + "mod", 2, scope)
                    uh = [sb(f"{n}up_h{i}", [P, 2, KD, FF], F32R, scope) for i in range(2)]
                    ul = [sb(f"{n}up_l{i}", [P, 2, KD, FF], F32R, scope) for i in range(2)]
                    dh = [sb(f"{n}down_h{i}", [P, D], F32R, scope) for i in range(2)]
                    dl = [sb(f"{n}down_l{i}", [P, D], F32R, scope) for i in range(2)]
                    gb = [sb(f"{n}gate_b{i}", [P, REQ * TOK], F32, scope) for i in range(RING)]
                    sg = [sb(f"{n}silu{i}", [P, REQ * TOK], F32, scope) for i in range(2)]
                    pr = [sb(f"{n}prod{i}", [P, REQ * TOK], F32, scope) for i in range(2)]
                    hg = [sb(f"{n}hid{i}", [P, REQ * TOK], F32, scope) for i in range(2)]
                    hh = [sb(f"{n}hid_h{i}", [P, REQ * TOK], F32R, scope) for i in range(2)]
                    hl = [sb(f"{n}hid_l{i}", [P, REQ * TOK], F32R, scope) for i in range(2)]
                    rw = sb(n + "router", [P, KD, NE], F32, scope)
                    rwh = sb(n + "router_h", [P, KD, NE], F32R, scope)
                    rwl = sb(n + "router_l", [P, KD, NE], F32R, scope)
                    rb = sb(n + "router_b", [P, NE], F32, scope)
                    sc = sb(n + "scores", [P, REQ, NE], F32, scope)
                    sel = sb(n + "biased", [P, REQ, NE], F32, scope)
                    m8 = sb(n + "top8", [P, REQ, 8], F32, scope)
                    i8 = sb(n + "top8_at", [P, REQ, 8], U32, scope)
                    f8 = sb(n + "top8_f", [P, REQ, 8], F32, scope)
                    mask = sb(n + "mask", [P, REQ, NE], F32, scope)
                    gt = sb(n + "gates_t", [P, REQ, NE], F32, scope)
                    sm = sb(n + "gate_sum", [P, REQ, 2], F32, scope)
                    gT = sb(n + "gatesT_sb", [NE, REQ * TOK], F32, scope)
                    norm = Norm(f"ln_ffn{l}", l, 1, [4, 5, 6, 7], lambda e, r: e.wait_ge(s["down_multiplied"], NE + 1), scope,
                                t["ln_ffn_g"][l:l + 1, :], t["ln_ffn_b"][l:l + 1, :])

                    def items(eng, first, body):
                        for j in range(first, RING):
                            body(0, j)
                        with eng.Fori(1, 1 + GRPS) as it:
                            for j in range(RING):
                                body(it, j)
                        body(1 + GRPS, 0)

                    def split_up_high(act, it, j):
                        act.wait_ge(self.landed[j], it * 48 + 48)
                        wait(act, s["up_multiplied"], it * RING + j - 1)
                        act.activation(uh[j % 2][:, :, :, :].rearrange("p a k f -> p (a k f)"), raw[j][:, 0:2 * D], ACT.Copy).then_inc(s["up_high"], 1)

                    def split_down_high(act, it, j):
                        wait(act, s["down_multiplied"], it * RING + j - 1)
                        act.activation(dh[j % 2][:, :], raw[j][:, 2 * D:3 * D], ACT.Copy).then_inc(s["down_high"], 1)

                    def following(it, j):
                        return (it, j + 1) if j + 1 < RING else (it + 1, 0)

                    def split_up_low(dve, it, j):
                        dve.wait_ge(s["up_high"], it * RING + j + 1)
                        dve.tensor_tensor(ul[j % 2][:, :, :, :].rearrange("p a k f -> p (a k f)"), raw[j][:, 0:2 * D],
                                          uh[j % 2][:, :, :, :].rearrange("p a k f -> p (a k f)").bitcast(F32), ALU.subtract).then_inc(s["up_low"], 1)

                    def split_down_low(dve, it, j):
                        dve.wait_ge(s["down_high"], it * RING + j + 1)
                        dve.tensor_tensor(dl[j % 2][:, :], raw[j][:, 2 * D:3 * D], dh[j % 2][:, :].bitcast(F32), ALU.subtract).then_inc(s["down_low"], 1)

                    with nc.Block() as block:
                        @block.sync
                        def _(sp):
                            sp.dma_start(rw[:, :, :], t["router_w"][l].rearrange("(p k) e -> p k e", k=KD)).then_inc(s["router_landed"], 16)
                            sp.dma_start(rb[:, :], t["router_bias"][l:l + 1, :].partition_broadcast(P)).then_inc(s["router_landed"], 16)
                            norm.sync(sp)
                            sp.wait_ge(s["gatesT"], 1)
                            sp.dma_start(gate_rows[l], gT[:, :]).then_inc(s["gates_stored"], 16)
                            sp.wait_ge(s["gates_stored"], 16)

                            def load(it, j):
                                i = it * RING + j
                                if not (isinstance(it, int) and it == 0):
                                    sp.wait_ge(s["down_low"], i - RING + 1)
                                    self.load_weights(sp, it, j)
                                    wait(sp, s["gated"], i - RING)
                                sp.dma_start(gb[j][:, :], gate_rows[l, bass.ds(i - 1, 1), :].partition_broadcast(P)).then_inc(self.gate_landed[j], 16)
                            items(sp, 1, load)
                            for j in range(RING):
                                sp.wait_ge(s["down_low"], NE + 1)
                                if prefetch:
                                    prefetch(sp, j)
                            if final:
                                for r in range(REQ):
                                    sp.wait_ge(norm.done, r + 1)
                                    store(sp, y_out[r][0], X[:, r, :])
                                sp.wait_ge(s_out, n_out[0])

                        @block.scalar
                        def _(act):
                            mod.scalar(act)
                            act.wait_ge(s["router_landed"], 32)
                            act.activation(rwh[:, :, :], rw[:, :, :], ACT.Copy).then_inc(s["router_high"], 1)
                            act.wait_ge(s["router_multiplied"], 1)
                            act.activation(sc[:, :, :], PS[:, 0, 0:REQ * NE].rearrange("p (r e) -> p r e", r=REQ), ACT.Sigmoid).then_inc(s["router_scores"], 1)
                            act.wait_ge(s["gates_turned"], 1)
                            act.activation(gT[:, :], PS[0:NE, 0, 0:REQ * TOK], ACT.Copy).then_inc(s["gatesT"], 1)
                            split_up_high(act, 0, 0)
                            split_down_high(act, 0, 0)

                            def item(it, j, last=False):
                                i = it * RING + j
                                if not last:
                                    split_up_high(act, *following(it, j))
                                act.wait_ge(s["up_multiplied"], i + 1)
                                wait(act, s["product"], i - 1)
                                act.activation(sg[j % 2][:, :], PS[:, j % 2, 0:REQ * TOK], ACT.Silu).then_inc(s["silu"], 1)
                                if not last:
                                    split_down_high(act, *following(it, j))
                            for j in range(RING):
                                item(0, j)
                            with act.Fori(1, 1 + GRPS) as it:
                                for j in range(RING):
                                    item(it, j)
                            item(1 + GRPS, 0, last=True)
                            norm.scalar(act)

                        @block.vector
                        def _(dve):
                            mod.vector(dve)
                            dve.wait_ge(s["router_high"], 1)
                            dve.tensor_tensor(rwl[:, :, :], rw[:, :, :], rwh[:, :, :].bitcast(F32), ALU.subtract).then_inc(s["router_low"], 1)
                            split_up_first = split_up_low
                            dve.wait_ge(s["router_scores"], 1)
                            dve_step(dve, dve.tensor_tensor(sel[:, :, :], sc[:, :, :], rb[:, :].unsqueeze(1).to_broadcast([P, REQ, NE]), ALU.add))
                            for r in range(REQ):
                                dve_step(dve, dve.max(m8[:, r, :], sel[:, r, :]))
                                dve_step(dve, dve.max_index(i8[:, r, :], m8[:, r, :], sel[:, r, :]))
                            dve_step(dve, dve.tensor_copy(f8[:, :, :], i8[:, :, :]))
                            for r in range(REQ):
                                dve_step(dve, dve.tensor_scalar(mask[:, r, :], table[:, T_IO:T_MK], f8[:, r, 0:1], None, ALU.is_equal))
                                for j in range(1, TOPK):
                                    dve_step(dve, dve.scalar_tensor_tensor(mask[:, r, :], table[:, T_IO:T_MK], f8[:, r, j:j + 1], mask[:, r, :],
                                                                           ALU.is_equal, ALU.add))
                            dve_step(dve, dve.tensor_tensor(gt[:, :, :], mask[:, :, :], sc[:, :, :], ALU.mult))
                            dve_step(dve, dve.tensor_reduce(sm[:, :, 0], gt[:, :, :], AX_X, ALU.add))
                            dve_step(dve, dve.reciprocal(sm[:, :, 1], sm[:, :, 0]))
                            for r in range(REQ):
                                i = dve.tensor_scalar(gt[:, r, :], gt[:, r, :], sm[:, r, 1:2], ROUTED, ALU.mult, ALU.mult)
                                i.then_inc(s["gates"], 1)
                            split_up_low(dve, 0, 0)
                            split_down_low(dve, 0, 0)

                            def item(it, j, last=False, shared=False):
                                i = it * RING + j
                                b = j % 2
                                if not last:
                                    split_up_low(dve, *following(it, j))
                                dve.wait_ge(s["silu"], i + 1)
                                wait(dve, s["hidden_low"], i - 1)
                                up = PS[:, b, REQ * TOK:2 * REQ * TOK]
                                if shared:
                                    dve.tensor_tensor(hg[b][:, :], sg[b][:, :], up, ALU.mult).then_inc(s["product"], 1)
                                    dve.wait_ge(s["product"], 1)
                                else:
                                    dve.tensor_tensor(pr[b][:, :], sg[b][:, :], up, ALU.mult).then_inc(s["product"], 1)
                                    dve.wait_ge(s["product"], i + 1)
                                    dve.wait_ge(self.gate_landed[j], it * 16 + (16 if j else 0))
                                    dve.tensor_tensor(hg[b][:, :], pr[b][:, :], gb[j][:, :], ALU.mult).then_inc(s["gated"], 1)
                                    dve.wait_ge(s["gated"], i)
                                wait(dve, s["down_multiplied"], i - 1)
                                dve.tensor_copy(hh[b][:, :], hg[b][:, :]).then_inc(s["hidden_high"], 1)
                                dve.wait_ge(s["hidden_high"], i + 1)
                                dve.tensor_tensor(hl[b][:, :], hg[b][:, :], hh[b][:, :].bitcast(F32), ALU.subtract).then_inc(s["hidden_low"], 1)
                                if not last:
                                    split_down_low(dve, *following(it, j))
                            for j in range(RING):
                                item(0, j, shared=(j == 0))
                            with dve.Fori(1, 1 + GRPS) as it:
                                for j in range(RING):
                                    item(it, j)
                            item(1 + GRPS, 0, last=True)
                            norm.vector(dve)

                        @block.tensor
                        def _(pe):
                            mod.tensor(pe)
                            pe.wait_ge(mod.lo, 2)
                            pe.wait_ge(s["router_low"], 1)
                            for r in range(REQ):
                                at = slice(r * TOK, r * TOK + TOK)
                                for k in range(KD):
                                    mm = three(pe, PS[:, 0, r * NE:(r + 1) * NE], HTh[:, k, at], HTl[:, k, at], rwh[:, k, :], rwl[:, k, :],
                                               start=(k == 0), stop=(k == KD - 1))
                            mm.then_inc(s["router_multiplied"], 1)
                            pe.wait_ge(s["gates"], 2)
                            for r in range(REQ):
                                mm = pe.transpose(PS[0:NE, 0, r * TOK:(r + 1) * TOK], gt[:, r, :], ident)
                            mm.then_inc(s["gates_turned"], 1)
                            pe.wait_ge(s["gatesT"], 1)

                            def up(it, j):
                                i = it * RING + j
                                b = j % 2
                                pe.wait_ge(s["up_low"], i + 1)
                                wait(pe, s["product"], i - 1)
                                for a in range(2):
                                    for k in range(KD):
                                        mm = three(pe, PS[:, b, a * REQ * TOK:(a + 1) * REQ * TOK], uh[b][:, a, k, :], ul[b][:, a, k, :],
                                                   HTh[:, k, :], HTl[:, k, :], start=(k == 0), stop=(k == KD - 1))
                                mm.then_inc(s["up_multiplied"], 1)

                            def down(it, j, first=False, last=False):
                                i = it * RING + j
                                b = j % 2
                                pe.wait_ge(s["hidden_low"], i + 1)
                                pe.wait_ge(s["down_low"], i + 1)
                                for r in range(REQ):
                                    at = slice(r * TOK, r * TOK + TOK)
                                    for c in range(2):
                                        cols = slice(c * 512, c * 512 + 512)
                                        mm = three(pe, PS[:, 4 + 2 * r + c, :], hh[b][:, at], hl[b][:, at], dh[b][:, cols], dl[b][:, cols],
                                                   start=first, stop=last)
                                mm.then_inc(s["down_multiplied"], 1)
                            up(0, 0)
                            for j in range(1, RING):
                                up(0, j)
                                down(0, j - 1, first=(j == 1))
                            with pe.Fori(1, 1 + GRPS) as it:
                                for j in range(RING):
                                    up(it, j)
                                    if j:
                                        down(it, j - 1)
                                    else:
                                        down(it - 1, RING - 1)
                            up(1 + GRPS, 0)
                            down(GRPS, RING - 1)
                            down(1 + GRPS, 0, last=True)

        NG2 = G5 // 2
        NS = 2 * NG2
        RJ = REQ * NC5
        TG = 4
        UNITS = [(tile, d) for tile in range(NG2 // TG) for d in range(2)]
        u_d = nc.dram_tensor("u_saved", [P, KD * CH * RJ], F32, kind="Internal").ap()

        def run_layer1():
            with ExitStack() as outer:
                w_in = LateProject("w_in_c", t["w_in_c"][0], 256, 4, None, None, None, None)
                w_out = LateProject("w_out_c", t["w_out_c"][0], 256, 8,
                                    lambda b, r: PS[:, 4 * r + b // 2, b % 2 * 256:b % 2 * 256 + 256], None, None, None)
                w_out.view = t["w_out_c"][0].rearrange("(k p) n -> p k n", p=P)
                ada(1, lambda sp, j: w_in.load(sp, j))
                PW = sb("powers", [P, 12, 2, NS], F32, outer)
                PR = sb("powers_down", [P, 9, 2, NS], F32, outer)
                X0 = sb("s5_start", [P, P], F32, outer)
                u_stored = sem("u_stored")
                b_landed, c_landed = sem("s5_b_landed"), sem("s5_c_landed")
                pw_ready = sem("powers_ready")
                Braw = raw[0][:, 0:2048].rearrange("n (i p c) -> n i p c", i=2, c=C5)
                Craw = raw[1][:, 0:2048].rearrange("n (i c p) -> n i c p", i=2, c=C5)
                U = [raw[i][:, 2048:3072].rearrange("p (g n) -> p g n", g=G5 // 2) for i in range(2)]

                with ExitStack() as scope:
                    mod = Modulate("mix1_mod", 0, scope)
                    w_in.alloc(scope)
                    uT = sb("uT", [P, KD, CH, RJ], F32, scope)
                    q = sb("s5_pre", [NS, 24, P], F32, scope)
                    S6 = sb("s5_turned", [P, 6, NS], F32, scope)
                    ldt = sb("s5_log_dt_sb", [NS, 2, 2], F32, scope)
                    sraw = sb("s5_state_raw", [P, P], F32, scope)
                    lam_landed, st_landed = sem("lambda_landed"), sem("state_landed")
                    dt_e, angles, exps, sins = sem("dt_ready"), sem("angles_ready"), sem("magnitudes_ready"), sem("sines_ready")
                    pre = sem("discretised")
                    turned, s6_ready = sem("s5_params_turned"), sem("s5_params_ready")
                    V = sb("u_rows", [RJ, G5, CC], F32, scope)
                    v_mm, v_ready = sem("u_rows_turned"), [sem("u_rows_act"), sem("u_rows_dve")]
                    u_mm, u_ready = sem("u_chunks_turned"), [sem("u_chunks_act"), sem("u_chunks_dve")]

                    def u_copies(eng, me):
                        copy = (lambda o, i: eng.activation(o, i, ACT.Copy)) if me == 0 else eng.tensor_copy
                        for k in range(KD):
                            f = 2 * k + me
                            eng.wait_ge(v_mm, f + 1)
                            copy(V[:, 8 * k:8 * k + 8, me * 64:me * 64 + 64].rearrange("n g (s c) -> n s g c", s=4),
                                 PS[0:RJ, f % 4, :].rearrange("n (s g c) -> n s g c", s=4, g=8)).then_inc(v_ready[me], 1)
                            if k and (k - 1) % 2 == me:
                                chunk_copy(eng, copy, k - 1, me)
                        if me == (KD - 1) % 2:
                            chunk_copy(eng, copy, KD - 1, me)

                    def chunk_copy(eng, copy, k, me):
                        eng.wait_ge(u_mm, k + 1)
                        copy(U[k // 4][:, k % 4 * 8:k % 4 * 8 + 8, :], PS[:, 4 + k % 4, 0:8 * RJ].rearrange("p (g n) -> p g n", g=8)).then_inc(u_ready[me], 1)
                    pt_tmp = sb("s5_pt", [P, 2, 2, 2, NS], F32, scope)

                    def evac(eng, b, a):
                        i = 2 * b + a
                        src = PS[:, i, 0:REQ * TOK].rearrange("p (r j s) -> p s r j", r=REQ, s=CH)
                        dst = uT[:, i, :, :].rearrange("p s (r j) -> p s r j", r=REQ)
                        return eng.activation(dst, src, ACT.Copy) if a == 0 else eng.tensor_copy(dst, src)
                    w_in.evac = evac
                    v2 = lambda ap: ap.rearrange("n (g p) -> n g p", g=2)
                    with nc.Block() as block:
                        @block.sync
                        def _(sp):
                            sp.dma_start(q[:, 0, :], t["s5_lam_re"][0].rearrange("d (n g) p -> (d n) (g p)", g=2)).then_inc(lam_landed, 16)
                            sp.dma_start(q[:, 1, :], t["s5_lam_im"][0].rearrange("d (n g) p -> (d n) (g p)", g=2)).then_inc(lam_landed, 16)
                            sp.dma_start(ldt[:, 0, :], t["s5_log_dt"][0].rearrange("d (n g) -> (d n) g", g=2)).then_inc(lam_landed, 16)
                            sp.dma_start(sraw[:, :], t["state_ssm"][0, 0].rearrange("d i (n g) p -> (d i n) (g p)", g=2)).then_inc(st_landed, 16)
                            sp.wait_ge(w_in.lo, 1)
                            for i, key in enumerate(("s5_b_re", "s5_b_im")):
                                sp.dma_start(Braw[:, i, :, :], t[key][0].rearrange("d g p c -> (d g) p c")).then_inc(b_landed, 16)
                            sp.wait_ge(w_in.lo, 2)
                            for i, key in enumerate(("s5_c_re", "s5_c_im")):
                                sp.dma_start(Craw[:, i, :, :], t[key][0].rearrange("d g c p -> (d g) c p")).then_inc(c_landed, 16)
                            sp.wait_ge(w_in.ready[0], 4)
                            sp.wait_ge(w_in.ready[1], 4)
                            sp.dma_start(u_d, uT[:, :, :, :].rearrange("p k s n -> p (k s n)")).then_inc(u_stored, 16)
                            sp.wait_ge(u_stored, 16)

                        @block.tensor
                        def _(pe):
                            mod.tensor(pe)
                            pe.wait_ge(mod.lo, 2)
                            for b in range(4):
                                pe.wait_ge(w_in.lo, b + 1)
                                for a in range(2):
                                    for k in range(KD):
                                        at = slice(a * P, a * P + P)
                                        mm = three(pe, PS[:, 2 * b + a, 0:REQ * TOK], w_in.wh[b % 2][:, k, at], w_in.wl[b % 2][:, k, at],
                                                   HTh[:, k, :], HTl[:, k, :], start=(k == 0), stop=(k == KD - 1))
                                    mm.then_inc(w_in.mm, 1)
                            pe.wait_ge(w_in.ready[0], 4)
                            pe.wait_ge(w_in.ready[1], 4)

                            def rows(f):
                                wait(pe, v_ready[f % 2], f // 2 - 1)
                                for i in range(4):
                                    mm = pe.transpose(PS[0:RJ, f % 4, i * P:i * P + P], uT[:, f // 2, f % 2 * 4 + i, :], ident)
                                mm.then_inc(v_mm, 1)

                            def columns(k):
                                pe.wait_ge(v_ready[0], k + 1)
                                pe.wait_ge(v_ready[1], k + 1)
                                if k >= 4:
                                    pe.wait_ge(u_ready[k % 2], k // 2 - 1)
                                for g in range(8):
                                    mm = pe.transpose(PS[:, 4 + k % 4, g * RJ:(g + 1) * RJ], V[:, 8 * k + g, :], ident[0:RJ, 0:RJ])
                                mm.then_inc(u_mm, 1)
                            for k in range(KD):
                                rows(2 * k)
                                rows(2 * k + 1)
                                if k:
                                    columns(k - 1)
                            columns(KD - 1)
                            pe.wait_ge(v_ready[0], KD)
                            pe.wait_ge(v_ready[1], KD)
                            pe.wait_ge(pre, 1)
                            for i in range(6):
                                mm = pe.transpose(PS[:, 0, i * NS:(i + 1) * NS], q[:, 18 + i, :], ident[0:NS, 0:NS])
                            mm.then_inc(turned, 1)
                            pe.wait_ge(st_landed, 16)
                            pe.transpose(PS[:, 1, 0:P], sraw[:, :], ident).then_inc(turned, 1)

                        @block.scalar
                        def _(act):
                            mod.scalar(act)
                            w_in.scalar(act)
                            act.wait_ge(w_in.ready[0], 4)
                            u_copies(act, 0)
                            act.wait_ge(u_ready[0], KD // 2)
                            act.wait_ge(lam_landed, 48)
                            act.activation(ldt[:, 1, :], ldt[:, 0, :], ACT.Exp).then_inc(dt_e, 1)
                            act.wait_ge(angles, 1)
                            act.activation(q[:, 4, :], q[:, 2, :], ACT.Exp).then_inc(exps, 1)
                            act.activation(q[:, 5, :], q[:, 2, :], ACT.Exp, scale=-1.0).then_inc(exps, 1)
                            act.wait_ge(angles, 2)
                            act.activation(q[:, 8, :], q[:, 6, :], ACT.Sin).then_inc(sins, 1)
                            act.activation(q[:, 9, :], q[:, 7, :], ACT.Sin).then_inc(sins, 1)
                            act.wait_ge(turned, 2)
                            act.activation(X0[:, :], PS[:, 1, 0:P], ACT.Copy).then_inc(s6_ready, 1)
                            act.wait_ge(s6_ready, 1)

                        @block.vector
                        def _(dve):
                            mod.vector(dve)
                            w_in.vector(dve)
                            u_copies(dve, 1)
                            dve.wait_ge(u_ready[1], KD // 2)
                            S = lambda i: q[:, i, :]
                            step = lambda ins: dve_step(dve, ins)
                            dve.wait_ge(dt_e, 1)
                            for g in range(2):
                                at = slice(g * P5, g * P5 + P5)
                                dve.tensor_scalar(q[:, 2, at], q[:, 0, at], ldt[:, 1, g:g + 1], None, ALU.mult)
                                i = dve.tensor_scalar(q[:, 3, at], q[:, 1, at], ldt[:, 1, g:g + 1], None, ALU.mult)
                            i.then_inc(angles, 1)
                            dve.wait_ge(angles, 1)
                            BIG, C1 = 12582912.0, 6.28125
                            C2 = 2 * math.pi - C1
                            PI = 3.1415925
                            step(dve.tensor_scalar(S(10), S(3), 1 / (2 * math.pi), BIG, ALU.mult, ALU.add))
                            step(dve.tensor_scalar(S(11), S(10), -BIG, None, ALU.add))
                            step(dve.scalar_tensor_tensor(S(10), S(11), -C1, S(3), ALU.mult, ALU.add))
                            step(dve.scalar_tensor_tensor(S(12), S(11), -C2, S(10), ALU.mult, ALU.add))
                            step(dve.tensor_scalar(S(6), S(12), PI, -PI, ALU.min, ALU.max))
                            step(dve.tensor_scalar(S(13), S(6), math.pi / 2, None, ALU.add))
                            step(dve.tensor_scalar(S(14), S(13), PI, -2 * math.pi, ALU.is_gt, ALU.mult))
                            step(dve.tensor_tensor(S(15), S(13), S(14), ALU.add))
                            dve.tensor_scalar(S(7), S(15), PI, -PI, ALU.min, ALU.max).then_inc(angles, 1)
                            dve.wait_ge(sins, 2)
                            dve.wait_ge(exps, 2)
                            dve.tensor_tensor(S(18), S(4), S(9), ALU.mult)
                            dve.tensor_tensor(S(19), S(4), S(8), ALU.mult)
                            dve.tensor_tensor(S(20), S(5), S(9), ALU.mult)
                            step(dve.scalar_tensor_tensor(S(21), S(8), -1.0, S(5), ALU.mult, ALU.mult))
                            dve.tensor_scalar(S(10), S(18), -1.0, None, ALU.add)
                            dve.tensor_tensor(S(11), S(0), S(0), ALU.mult)
                            step(dve.tensor_tensor(S(12), S(1), S(1), ALU.mult))
                            step(dve.tensor_tensor(S(13), S(11), S(12), ALU.add))
                            dve.reciprocal(S(14), S(13))
                            dve.tensor_tensor(S(15), S(10), S(0), ALU.mult)
                            dve.tensor_tensor(S(16), S(19), S(1), ALU.mult)
                            dve.tensor_tensor(S(17), S(19), S(0), ALU.mult)
                            step(dve.tensor_tensor(S(2), S(10), S(1), ALU.mult))
                            dve.tensor_tensor(S(12), S(15), S(16), ALU.add)
                            step(dve.tensor_tensor(S(13), S(17), S(2), ALU.subtract))
                            dve.tensor_tensor(S(22), S(12), S(14), ALU.mult)
                            dve.tensor_tensor(S(23), S(13), S(14), ALU.mult).then_inc(pre, 1)
                            dve.wait_ge(turned, 1)
                            step(dve.tensor_copy(S6[:, :, :], PS[:, 0, 0:6 * NS].rearrange("p (i n) -> p i n", i=6)))

                            def cmul(dst, n, a, b):
                                br = PW[:, b, 0, :].unsqueeze(1).to_broadcast([P, n, NS])
                                bi = PW[:, b, 1, :].unsqueeze(1).to_broadcast([P, n, NS])
                                ar, ai = PW[:, a:a + n, 0, :], PW[:, a:a + n, 1, :]
                                T = [pt_tmp[:, i // 2, i % 2, 0:n, :] for i in range(4)]
                                dve.tensor_tensor(T[0], ar, br, ALU.mult)
                                dve.tensor_tensor(T[1], ai, bi, ALU.mult)
                                dve.tensor_tensor(T[2], ar, bi, ALU.mult)
                                step(dve.tensor_tensor(T[3], ai, br, ALU.mult))
                                dve.tensor_tensor(PW[:, dst:dst + n, 0, :], T[0], T[1], ALU.subtract)
                                step(dve.tensor_tensor(PW[:, dst:dst + n, 1, :], T[2], T[3], ALU.add))
                            dve.memset(PW[:, 4, 0, :], 1.0)
                            dve.memset(PW[:, 4, 1, :], 0.0)
                            dve.tensor_copy(PW[:, 11, :, :], S6[:, 4:6, :])
                            dve.tensor_copy(PW[:, 5, :, :], S6[:, 0:2, :])
                            step(dve.tensor_copy(PW[:, 3, :, :], S6[:, 2:4, :]))
                            cmul(6, 1, 5, 5)
                            cmul(7, 2, 5, 6)
                            cmul(2, 1, 3, 3)
                            cmul(1, 1, 2, 3)
                            cmul(0, 1, 2, 2)
                            cmul(9, 1, 8, 5)
                            cmul(10, 1, 8, 8)
                            for i in range(9):
                                ins = dve.tensor_copy(PR[:, i, :, :], PW[:, 8 - i, :, :])
                            ins.then_inc(pw_ready, 1)
                            dve.wait_ge(pw_ready, 1)
                            dve.wait_ge(w_in.ready[1], 4)

                with ExitStack() as scope:
                    F = sb("F", [P, 2, NG2, 2, CC], F32, scope)
                    E = sb("E", [P, 2, TG, 2, CC], F32, scope)
                    ZX = sb("ZX", [P, 2, NG2, 2, REQ, NC5 + 1], F32, scope)
                    Et = sb("E_turned", [P, 2048], F32, scope)
                    tmpE = sb("tmpE", [P, 1024], F32, scope)
                    tmpF = sb("tmpF", [P, 1024], F32, scope)
                    A = [m[:, 0:3 * NG2 * 2 * REQ].rearrange("p (a n i r) -> p a n i r", a=3, i=2, r=REQ) for m in (tmpE, tmpF)]
                    HS = tmpE[:, 512:640].rearrange("p (d i n) -> p d i n", d=2, i=2)
                    HSt = tmpF[:, 512:640]
                    Bb = raw[1][:, 0:2048].rearrange("p (n i c) -> p n i c", n=NS, i=2)
                    B2 = raw[0][:, 0:2048].rearrange("p (n i c) -> p n i c", n=NS, i=2)
                    Ct = raw[2][:, 0:2048].rearrange("p (n i c) -> p n i c", n=NS, i=2)
                    C2 = raw[3][:, 0:2048].rearrange("p (n i c) -> p n i c", n=NS, i=2)
                    Ms = [raw[2 + i][:, 2048:3072] for i in range(2)]
                    t1 = Et[:, :].rearrange("p (n i c) -> p n i c", n=NS, i=2)
                    t2 = E[:, :, :, :, :].rearrange("p d g i x -> p (d g i x)").rearrange("p (n i c) -> p n i c", n=NS, i=2)
                    c_turned, c_ready, bb, b_ready = sem("C_turned"), sem("C_ready"), sem("B_step"), sem("B_ready")
                    e_p, e_ready, f_p, f_ready = sem("E_step"), sem("E_ready"), sem("F_step"), sem("F_ready")
                    et_mm, et_ready = sem("E_turned_pe"), sem("E_turned_ready")
                    m_mm, m_ready = sem("M_multiplied"), sem("M_ready")
                    z_mm, z_ready, ym_mm = sem("z_multiplied"), sem("z_ready"), sem("y_inside_multiplied")
                    zero = sem("scan_start_zeroed")
                    scan = [sem("scan_forward_step"), sem("scan_backward_step")]
                    scanned = [sem("scan_forward_done"), sem("scan_backward_done")]
                    ends = [sem("end_states_forward"), sem("end_states_backward")]
                    end_t, end_s = sem("end_states_turned"), sem("end_states_sb")
                    y_mm = sem("y_multiplied")

                    def build_matrix(eng, s1, s2, tmp, out, v, base, other, table_):
                        tile, d = UNITS[v]
                        n0 = d * NG2 + tile * TG
                        shape = [P, TG, CH, C5]
                        pr = table_[:, :, 0, n0:n0 + TG].rearrange("p s n -> p n s").unsqueeze(3).to_broadcast(shape)
                        pi = table_[:, :, 1, n0:n0 + TG].rearrange("p s n -> p n s").unsqueeze(3).to_broadcast(shape)
                        tm = tmp[:, :].rearrange("p (g i s c) -> p g i s c", g=TG, i=2, s=CH)
                        for i in range(2):
                            o = out[:, :, i, :].rearrange("p g (s c) -> p g s c", s=CH)
                            eng.tensor_tensor(o, base[:, n0:n0 + TG, i, :].unsqueeze(2).to_broadcast(shape), pr, ALU.mult)
                            ins = eng.tensor_tensor(tm[:, :, i, :, :], other[:, n0:n0 + TG, i, :].unsqueeze(2).to_broadcast(shape), pi, ALU.mult)
                        ins.then_inc(s1, 1)
                        eng.wait_ge(s1, v + 1)
                        eng.tensor_tensor(out.rearrange("p g i x -> p (g i x)"), out.rearrange("p g i x -> p (g i x)"), tmp[:, :], ALU.add).then_inc(s2, 1)

                    def y_at(g):
                        return PS[:, 2 * (g % 2) + g // 32, g // 2 % 16 * RJ:g // 2 % 16 * RJ + RJ]
                    YB = [0, 2, 1, 3]

                    def scan_dir(eng, d):
                        lr = PW[:, 10, 0, d * NG2:(d + 1) * NG2].unsqueeze(2).to_broadcast([P, NG2, 4])
                        li = PW[:, 10, 1, d * NG2:(d + 1) * NG2].unsqueeze(2).to_broadcast([P, NG2, 4])
                        a, p1, p2 = (A[d][:, i, :, :, :] for i in range(3))
                        fl = lambda x: x.rearrange("p n i r -> p n (i r)")
                        n = [0]

                        def then(ins):
                            n[0] += 1
                            ins.then_inc(scan[d], 1)
                            eng.wait_ge(scan[d], n[0])
                        s0 = 0 if d == 0 else NC5
                        x0 = ZX[:, d, :, :, :, s0]
                        h = X0[:, :].rearrange("p (d i n) -> p d i n", d=2, i=2)
                        w = [PW[:, 9, i, d * NG2:(d + 1) * NG2] for i in range(2)]
                        eng.memset(x0[:, :, :, 0], 0.0)
                        eng.tensor_tensor(p1[:, :, 0, 0], h[:, d, 0, :], w[0], ALU.mult)
                        eng.tensor_tensor(p1[:, :, 1, 0], h[:, d, 1, :], w[0], ALU.mult)
                        eng.tensor_tensor(p2[:, :, 0, 0], h[:, d, 0, :], w[1], ALU.mult)
                        then(eng.tensor_tensor(p2[:, :, 1, 0], h[:, d, 1, :], w[1], ALU.mult))
                        eng.tensor_tensor(x0[:, :, 0, 1], p1[:, :, 0, 0], p2[:, :, 1, 0], ALU.subtract)
                        then(eng.tensor_tensor(x0[:, :, 1, 1], p1[:, :, 1, 0], p2[:, :, 0, 0], ALU.add))
                        for j in range(NC5):
                            cur, nxt = (j, j + 1) if d == 0 else (NC5 - j, NC5 - j - 1)
                            then(eng.tensor_tensor(a, ZX[:, d, :, :, :, cur], ZX[:, d, :, :, :, nxt], ALU.add))
                            if j == NC5 - 1:
                                break
                            eng.tensor_tensor(fl(p1), fl(a), lr, ALU.mult)
                            then(eng.tensor_tensor(fl(p2), fl(a), li, ALU.mult))
                            eng.tensor_tensor(ZX[:, d, :, 0, :, nxt], p1[:, :, 0, :], p2[:, :, 1, :], ALU.subtract)
                            ins = eng.tensor_tensor(ZX[:, d, :, 1, :, nxt], p1[:, :, 1, :], p2[:, :, 0, :], ALU.add)
                            if j == NC5 - 2:
                                ins.then_inc(scanned[d], 1)
                                eng.wait_ge(scanned[d], 1)
                            else:
                                then(ins)
                        w = [PW[:, 7, i, d * NG2:(d + 1) * NG2] for i in range(2)]
                        eng.tensor_tensor(p1[:, :, 0, 0], a[:, :, 0, 0], w[0], ALU.mult)
                        eng.tensor_tensor(p1[:, :, 1, 0], a[:, :, 1, 0], w[0], ALU.mult)
                        eng.tensor_tensor(p2[:, :, 0, 0], a[:, :, 0, 0], w[1], ALU.mult)
                        then(eng.tensor_tensor(p2[:, :, 1, 0], a[:, :, 1, 0], w[1], ALU.mult))
                        eng.tensor_tensor(HS[:, d, 0, :], p1[:, :, 0, 0], p2[:, :, 1, 0], ALU.subtract).then_inc(ends[d], 1)
                        eng.tensor_tensor(HS[:, d, 1, :], p1[:, :, 1, 0], p2[:, :, 0, 0], ALU.add).then_inc(ends[d], 1)

                    with nc.Block() as block:
                        @block.tensor
                        def _(pe):
                            pe.wait_ge(b_landed, 32)
                            pe.wait_ge(c_landed, 32)
                            for m in range(2):
                                for i in range(2):
                                    for c in range(C5):
                                        src = Craw[:, i, c, :] if m == 0 else Braw[:, i, :, c]
                                        for g in range(2):
                                            mm = pe.matmul(PS[g * P5:(g + 1) * P5, (0 if m else 4) + 2 * i + c // 8, c % 8 * NS:c % 8 * NS + NS],
                                                           src, ident[:, g:P:2], start=True, stop=True)
                                mm.then_inc(c_turned, 1)
                            pe.wait_ge(c_ready, 4)
                            pe.wait_ge(b_ready, 3)

                            def inside(v):
                                tile, d = UNITS[v]
                                for x in range(8):
                                    g = 2 * (tile * TG + x % TG) + x // TG
                                    pe.wait_ge(m_ready, 2 * v + 1 + x // TG)
                                    mm = pe.matmul(y_at(g), Ms[v % 2][:, x * P:(x + 1) * P],
                                                   U[g // 32][:, g % 32, :], start=(d == 0 and g // 2 % 16 == 0), stop=False, skip_group_check=True)
                                mm.then_inc(ym_mm, 1)
                            for v, (tile, d) in enumerate(UNITS):
                                pe.wait_ge(e_ready, v + 1)
                                wait(pe, z_ready, 2 * v)
                                for n in range(TG):
                                    for i in range(2):
                                        x = 2 * n + i
                                        mm = pe.transpose(PS[:, 6 + x // 4, x % 4 * P:x % 4 * P + P],
                                                          E[:, d, n, i, :], ident)
                                    if n % 2:
                                        mm.then_inc(et_mm, 1)
                                pe.wait_ge(f_ready, v + 1)
                                wait(pe, m_ready, 2 * v)
                                for x in range(8):
                                    n, g = x // 2, x % 2
                                    rows = slice(g * P5, (g + 1) * P5)
                                    for i in range(2):
                                        mm = pe.matmul(PS[:, 4 + g, n * P:n * P + P], E[rows, d, n, i, :],
                                                       F[rows, d, tile * TG + n, i, :], start=(i == 0), stop=(i == 1))
                                    if x >= 6:
                                        mm.then_inc(m_mm, 1)
                                pe.wait_ge(et_ready, 2 * v + 2)
                                for x in range(8):
                                    n = x // 2
                                    g = (tile * TG + n) * 2
                                    mm = pe.matmul(PS[:, 6, x * 64:x * 64 + 64], Et[:, x * P:(x + 1) * P], U[g // 32][:, g % 32:g % 32 + 2, :],
                                                   start=True, stop=True)
                                mm.then_inc(z_mm, 1)
                                if v:
                                    inside(v - 1)
                            inside(len(UNITS) - 1)
                            for d in range(2):
                                pe.wait_ge(scanned[d], 1)
                                for g in range(G5):
                                    rows = slice(g % 2 * P5, g % 2 * P5 + P5)
                                    for i in range(2):
                                        mm = pe.matmul(y_at(g), F[rows, d, g // 2, i, :],
                                                       ZX[rows, d, g // 2, i, :, d:d + NC5], start=False,
                                                       stop=(d == 1 and i == 1 and g // 2 % 16 == 15), skip_group_check=True)
                                    if d == 1 and g // 2 % 16 == 15:
                                        mm.then_inc(y_mm, 1)
                            pe.wait_ge(ends[0], 2)
                            pe.wait_ge(ends[1], 2)
                            pe.transpose(PS[:, 7, 0:P], HS[:, :, :, :].rearrange("p d i n -> p (d i n)"), ident).then_inc(end_t, 1)

                        @block.scalar
                        def _(act):
                            act.wait_ge(c_turned, 1)
                            cp = lambda i: PS[:, 4 + 2 * i:6 + 2 * i, :].rearrange("p b (c n) -> p n (b c)", n=NS)
                            act.activation(Ct[:, :, 0, :], cp(0), ACT.Copy).then_inc(c_ready, 1)
                            act.activation(C2[:, :, 1, :], cp(0), ACT.Copy, scale=-1.0).then_inc(c_ready, 1)
                            act.activation(Ct[:, :, 1, :], cp(1), ACT.Copy, scale=-1.0).then_inc(c_ready, 1)
                            act.activation(C2[:, :, 0, :], cp(1), ACT.Copy, scale=-1.0).then_inc(c_ready, 1)
                            act.wait_ge(b_ready, 3)
                            for v, (tile, d) in enumerate(UNITS):
                                for half in range(2):
                                    act.wait_ge(et_mm, 2 * v + half + 1)
                                    wait(act, z_mm, v)
                                    act.activation(Et[:, half * 512:half * 512 + 512], PS[:, 6 + half, :], ACT.Copy).then_inc(et_ready, 1)
                                act.wait_ge(z_mm, v + 1)
                                for g in range(2):
                                    rows = slice(g * P5, (g + 1) * P5)
                                    src = PS[rows, 6, :].rearrange("p (x g r j) -> p x g r j", g=2, r=REQ, j=NC5)[:, :, g, :, :]
                                    dst = ZX[rows, d, tile * TG:(tile + 1) * TG, :, :, 1 - d:1 - d + NC5].rearrange("p n i r j -> p (n i) r j")
                                    act.activation(dst, src, ACT.Copy).then_inc(z_ready, 1)
                            act.wait_ge(end_t, 1)
                            act.activation(HSt, PS[:, 7, 0:P], ACT.Copy).then_inc(end_s, 1)

                        @block.vector
                        def _(dve):
                            dve.wait_ge(c_turned, 2)
                            for i in range(2):
                                bp = PS[:, 2 * i:2 * i + 2, :].rearrange("p b (c n) -> p n (b c)", n=NS)
                                for out, part in ((t1, 0), (t2, 1)):
                                    dve.tensor_tensor(out[:, :, i, :], bp, PW[:, 11, part, :].unsqueeze(2).to_broadcast([P, NS, C5]), ALU.mult).then_inc(bb, 1)
                            dve.wait_ge(bb, 4)
                            dve.tensor_tensor(Bb[:, :, 0, :], t1[:, :, 0, :], t2[:, :, 1, :], ALU.subtract).then_inc(b_ready, 1)
                            dve.tensor_tensor(Bb[:, :, 1, :], t1[:, :, 1, :], t2[:, :, 0, :], ALU.add).then_inc(b_ready, 1)
                            dve.wait_ge(b_ready, 2)
                            dve.tensor_copy(B2[:, :, 1, :], Bb[:, :, 0, :]).then_inc(bb, 1)
                            dve.tensor_scalar(B2[:, :, 0, :], Bb[:, :, 1, :], -1.0, None, ALU.mult).then_inc(b_ready, 1)
                            dve.wait_ge(b_ready, 3)
                            dve.wait_ge(bb, 5)

                            def masked(v):
                                d = UNITS[v][1]
                                mk = table[:, T_MK + d * P:T_MK + (d + 1) * P].unsqueeze(1).to_broadcast([P, 4, P])
                                for half in range(2):
                                    dve.wait_ge(m_mm, 2 * v + half + 1)
                                    wait(dve, ym_mm, v - 1)
                                    dve.tensor_tensor(Ms[v % 2][:, half * 512:half * 512 + 512].rearrange("p (x q) -> p x q", x=4),
                                                      PS[:, 4 + half, :].rearrange("p (x q) -> p x q", x=4), mk, ALU.mult).then_inc(m_ready, 1)
                            for v, (tile, d) in enumerate(UNITS):
                                if v >= 2:
                                    dve.wait_ge(m_mm, 2 * (v - 1))
                                build_matrix(dve, e_p, e_ready, tmpE, E[:, d, :, :, :], v, Bb, B2, PR[:, 0:8] if d == 0 else PW[:, 1:9])
                                dve.wait_ge(e_ready, v + 1)
                                if v:
                                    masked(v - 1)
                            masked(len(UNITS) - 1)
                            dve.wait_ge(z_ready, 2 * len(UNITS))
                            scan_dir(dve, 0)
                            
                        @block.gpsimd
                        def _(pool):
                            pool.wait_ge(c_ready, 4)
                            for v, (tile, d) in enumerate(UNITS):
                                build_matrix(pool, f_p, f_ready, tmpF, F[:, d, tile * TG:(tile + 1) * TG, :, :], v, Ct, C2,
                                             PW[:, 0:8] if d == 0 else PR[:, 1:9])
                                pool.wait_ge(f_ready, v + 1)
                            pool.wait_ge(z_ready, 2 * len(UNITS))
                            scan_dir(pool, 1)

                        @block.sync
                        def _(sp):
                            sp.wait_ge(end_s, 1)
                            store(sp, ssm_out[0, 0].rearrange("d i (n g) p -> (d i n) (g p)", g=2), HSt)
                            for j in range(RING):
                                w_out.load(sp, j)
                            sp.wait_ge(y_mm, 4)

                Yt = sb("Yt", [P, KD, CH, RJ], F32, outer)
                with ExitStack() as scope:
                    Ys = sb("y_columns", [P, 4, 16, RJ], F32, scope)
                    V = sb("y_rows", [RJ, CH, D], F32, scope)
                    uT = sb("uT_again", [P, KD, CH, RJ], F32, scope)
                    dcol = sb("s5_d_col", [P, KD], F32, scope)
                    back, ys = sem("u_back_landed"), [sem("y_columns_act"), sem("y_columns_dve")]
                    v_mm, v_ready = sem("y_rows_turned"), [sem("y_rows_act"), sem("y_rows_dve")]
                    y_mm2, y_done = sem("y_channels_turned"), sem("y_plus_du")

                    def y_copies(eng, me):
                        copy = (lambda o, i: eng.activation(o, i, ACT.Copy)) if me == 0 else eng.tensor_copy
                        for b in range(me, 4, 2):
                            copy(Ys[:, b, :, :], PS[:, b, :].rearrange("p (n x) -> p n x", n=16)).then_inc(ys[me], 1)
                        for f in range(me, 16, 2):
                            eng.wait_ge(v_mm, f + 1)
                            copy(V[:, :, 64 * f:64 * f + 64].rearrange("n s (g c) -> n g s c", g=4),
                                 PS[0:RJ, 4 + f % 4, :].rearrange("n (g s c) -> n g s c", g=4, s=CH)).then_inc(v_ready[me], 1)
                    with nc.Block() as block:
                        @block.sync
                        def _(sp):
                            sp.dma_start(uT[:, :, :, :].rearrange("p k s n -> p (k s n)"), u_d).then_inc(back, 16)
                            sp.dma_start(dcol[:, :], t["s5_d"][0].rearrange("(k p) -> p k", p=P), allow_slow_non_contiguous=True).then_inc(back, 16)

                        @block.tensor
                        def _(pe):
                            pe.wait_ge(ys[0], 2)
                            pe.wait_ge(ys[1], 2)
                            for f in range(16):
                                wait(pe, v_ready[f % 2], f // 2 - 1)
                                for i in range(4):
                                    g = 4 * f + i
                                    mm = pe.transpose(PS[0:RJ, 4 + f % 4, i * P:i * P + P], Ys[:, 2 * (g % 2) + g // 32, g // 2 % 16, :], ident)
                                mm.then_inc(v_mm, 1)
                            for k in range(KD):
                                for e in range(2):
                                    pe.wait_ge(v_ready[e], k + 1)
                                wait(pe, y_done, k - 3)
                                for s in range(CH):
                                    mm = pe.transpose(PS[:, k % 4, s * RJ:(s + 1) * RJ], V[:, s, k * P:(k + 1) * P], ident[0:RJ, 0:RJ])
                                mm.then_inc(y_mm2, 1)

                        @block.scalar
                        def _(act):
                            y_copies(act, 0)
                            act.wait_ge(v_ready[0], 8)

                        @block.vector
                        def _(dve):
                            y_copies(dve, 1)
                            dve.wait_ge(back, 32)
                            for k in range(KD):
                                dve.wait_ge(y_mm2, k + 1)
                                dve.scalar_tensor_tensor(Yt[:, k, :, :].rearrange("p s n -> p (s n)"), uT[:, k, :, :].rearrange("p s n -> p (s n)"),
                                                         dcol[:, k:k + 1], PS[:, k % 4, 0:CH * RJ], ALU.mult, ALU.add).then_inc(y_done, 1)
                            dve.wait_ge(y_done, KD)

                with ExitStack() as scope:
                    Gf = sb("gelu", [P, KD, REQ * TOK], F32, scope)
                    Gh = sb("gelu_h", [P, KD, REQ * TOK], F32R, scope)
                    Gl = sb("gelu_l", [P, KD, REQ * TOK], F32R, scope)
                    w_out.lh, w_out.ll = Gh, Gl
                    w_out.alloc(scope)
                    sig = Gf[:, :, :].rearrange("p k t -> p (k t)").rearrange("p (r n) -> p r n", r=REQ)
                    gelu, g_hi, g_lo = sem("gelu_ready"), sem("gelu_high"), sem("gelu_low")
                    sigm, glu = sem("gate_sigmoid"), sem("glu_ready")
                    norm = Norm("ln_mix1", 1, 0, [0, 1, 4, 5], lambda e, r: e.wait_ge(glu, 2 * r + 2), scope, t["ln_mix_g"][1:2, :], t["ln_mix_b"][1:2, :])
                    glu_sb = Yt[:, :, :, :].rearrange("p k s n -> p (k s n)").rearrange("p (r n) -> p r n", r=REQ)
                    norm.source = lambda r, n: glu_sb[:, r, n * 512:n * 512 + 512]
                    with nc.Block() as block:
                        @block.sync
                        def _(sp):
                            norm.sync(sp)
                            w_out.sync(sp)
                            for j in range(RING):
                                sp.wait_ge(w_out.lo, 5 + j)
                                moes[1].load_weights(sp, 0, j)

                        @block.tensor
                        def _(pe):
                            pe.wait_ge(g_lo, 2)
                            w_out.tensor(pe)

                        @block.scalar
                        def _(act):
                            for k in range(KD):
                                act.activation(Gf[:, k, :].rearrange("p (r j s) -> p s r j", r=REQ, s=CH),
                                               Yt[:, k, :, :].rearrange("p s (r j) -> p s r j", r=REQ), ACT.Gelu_apprx_tanh).then_inc(gelu, 1)
                            for half in range(2):
                                act.wait_ge(gelu, 4 * half + 4)
                                act.activation(Gh[:, 4 * half:4 * half + 4, :], Gf[:, 4 * half:4 * half + 4, :], ACT.Copy).then_inc(g_hi, 1)
                            w_out.scalar(act)
                            act.wait_ge(w_out.mm, 16)
                            act.wait_ge(g_lo, 2)
                            for r in range(REQ):
                                for n in range(2):
                                    act.activation(sig[:, r, n * 512:n * 512 + 512], PS[:, 4 * r + 2 + n, :], ACT.Sigmoid).then_inc(sigm, 1)
                            norm.scalar(act)

                        @block.vector
                        def _(dve):
                            for half in range(2):
                                dve.wait_ge(g_hi, half + 1)
                                at = slice(4 * half, 4 * half + 4)
                                dve.tensor_tensor(Gl[:, at, :], Gf[:, at, :], Gh[:, at, :].bitcast(F32), ALU.subtract).then_inc(g_lo, 1)
                            w_out.vector(dve)
                            for r in range(REQ):
                                for n in range(2):
                                    dve.wait_ge(sigm, 2 * r + n + 1)
                                    dve.tensor_tensor(glu_sb[:, r, n * 512:n * 512 + 512], PS[:, 4 * r + n, :], sig[:, r, n * 512:n * 512 + 512],
                                                      ALU.mult).then_inc(glu, 1)
                            norm.vector(dve)

        moes = [Moe(0)]
        run_layer0()
        if LAYERS == 1:
            moes[0].run(None, True)
        else:
            moes[0].run(None, False)
            nc.clear_and_free_semaphores(layer_sems)
            nc.all_engine_barrier()
            moes.append(Moe(1))
            run_layer1()
            moes[1].run(None, True)


_INS = ['x_prompt', 'x_sample', 'c', 'cache_attn_k', 'cache_attn_v', 'cache_mla_ckv', 'cache_mla_krope', 'state_ssm', 'c_ctx',
        'ada_w', 'ada_b', 'ln_mix_g', 'ln_mix_b', 'ln_ffn_g', 'ln_ffn_b', 'w_in_ab', 'attn_sink', 'mla_q_norm', 'mla_kv_norm',
        'mla_w_uq', 'mla_w_ukv', 'w_out_ab', 'w_in_c', 's5_lam_re', 's5_lam_im', 's5_log_dt', 's5_b_re', 's5_b_im', 's5_c_re',
        's5_c_im', 's5_d', 'w_out_c', 'router_w', 'router_bias', 'exp_w_gate', 'exp_w_up', 'exp_w_down', 'sh_w_gate', 'sh_w_up',
        'sh_w_down']
_OUTS = [(1, 128, 1024), (1, 128, 1024), (1, 1, 128, 2, 64), (1, 1, 128, 2, 64), (1, 1, 128, 128), (1, 1, 128, 32), (1, 1, 2, 2, 64, 64)]


def kernel(**inputs):
    import concourse.bacc as bacc
    from concourse.bass_utils import run_bass_kernel_spmd

    nc = bacc.Bacc("TRN2", target_bir_lowering=False, num_devices=1)
    arrays, aps = {}, {}
    given = {name: inputs[name] for name in _INS}
    given["table"], given["pick"] = shape_constants()
    for name, value in given.items():
        a = np.ascontiguousarray(value)
        arrays[f"in_{name}"] = a
        aps[name] = nc.dram_tensor(f"in_{name}", a.shape, mybir.dt.from_np(a.dtype), kind="ExternalInput").ap()
    n_outs = 7 if LAYERS == 2 else 6
    outs = [nc.dram_tensor(f"out_{i}", shape, F32, kind="ExternalOutput").ap() for i, shape in enumerate(_OUTS[:n_outs])]
    build(nc, aps, outs + [None] * (7 - n_outs))
    r = run_bass_kernel_spmd(nc, [arrays], core_ids=[0])
    return tuple(r.results[0][f"out_{i}"] for i in range(n_outs))
```

```python
import math
from contextlib import ExitStack

import numpy as np

import concourse.bass as bass
from concourse import mybir

F32 = mybir.dt.float32
F32R = mybir.dt.float32r
U32 = mybir.dt.uint32
ALU = mybir.AluOpType
ACT = mybir.ActivationFunctionType
AX_X = mybir.AxisListType.X

P = 128
D = 1024
KD = D // P
TOK = 128
REQ = 2
DEPTH = 2
LAYERS = 2
H, KV, HD = 8, 2, 64
GRP = H // KV
RQ, RKV, NOPE, ROPE, VD = 256, 128, 64, 32, 64
QK = NOPE + ROPE
A_Q, A_K, A_V = 0, H * HD, (H + KV) * HD
A_CQ = (H + 2 * KV) * HD
A_CKV = A_CQ + RQ
A_KR = A_CKV + RKV
W_AB = A_KR + ROPE
SC_A = HD ** -0.5
SC_M = QK ** -0.5
NE, TOPK, FF = 64, 6, 128
ROUTED = 2.5
ALPHA = (2.0 * DEPTH) ** 0.25
LN_EPS, RMS_EPS = 1e-5, 1e-6
RING = 4
SLOT = 3 * KD * FF
NADA = 24
GRID_W, ROPE_BASE = 64, 10000.0

G5, C5, P5 = 64, 16, 64
CH = 8
NC5 = TOK // CH
CC = CH * C5


def wait(eng, sem, value):
    if not isinstance(value, int) or value > 0:
        eng.wait_ge(sem, value)


def shape_constants():
    ident = np.eye(P, dtype=np.float32)
    pick = np.zeros((4, 2 + 2 * P), np.float32)
    for row in range(4):
        pick[row, row % 2] = 1.0
        pick[row, 2 + P * (row % 2):2 + P * (row % 2) + P] = 1.0
    tok = np.arange(TOK)
    pos = np.stack([tok // GRID_W, tok % GRID_W], 1).astype(np.float32)

    def rope(width):
        quarter = width // 4
        inv = (np.float32(ROPE_BASE) ** (-np.arange(quarter, dtype=np.float32) / np.float32(quarter))).astype(np.float32)
        ang = (pos[:, :, None] * inv[None, None, :]).astype(np.float32)
        return np.stack([np.cos(ang), np.sin(ang)], 1).astype(np.float32).reshape(TOK, -1)

    table = np.concatenate([ident, rope(HD), rope(ROPE), np.tile(np.arange(NE, dtype=np.float32), (P, 1))], 1)
    step = np.arange(P) // C5
    later = (step[None, :] >= step[:, None]).astype(np.float32)
    masks = np.stack([later, later.T], 1).reshape(P, 2 * P)
    half = P // 2
    swap = np.zeros((P, P), np.float32)
    swap[np.arange(half) + half, np.arange(half)] = -1.0
    swap[np.arange(half), np.arange(half) + half] = 1.0
    return (np.ascontiguousarray(np.concatenate([table, masks, swap], 1)), np.ascontiguousarray(pick))


T_ID = 0
T_RA = P
T_RM = T_RA + HD
T_IO = T_RM + ROPE
T_MK = T_IO + NE
T_SW = T_MK + 2 * P
T_W = T_SW + P


def build(nc, t, outs):
    y_out = outs[0:2]
    k_out, v_out, ckv_out, kr_out, ssm_out = outs[2:7]

    top = ExitStack()
    with top:
        def sb(name, shape, dt=F32, scope=top):
            return scope.enter_context(nc.sbuf_tensor(name, shape, dt))

        layer_sems = []

        def sem(name):
            layer_sems.append(nc.alloc_semaphore(name=name))
            return layer_sems[-1]

        def lasting_sem(name):
            return nc.alloc_semaphore(name=name)

        PS = top.enter_context(nc.psum_tensor("PS", [P, 8, 512], F32))
        table = sb("table", [P, T_W])
        pick = sb("pick", [4, 2 + 2 * P])
        ident = table[:, T_ID:T_ID + P]
        X = sb("X", [P, REQ, D])
        G = sb("G", [P, 2, REQ, D])
        COL = sb("COL", [P, 4, KD, REQ])
        stat = sb("stat", [P, 64])
        eps = sb("eps", [P, 2])
        raw = [sb(f"raw{i}", [P, SLOT]) for i in range(RING)]
        gate_rows = nc.dram_tensor("gate_rows", [DEPTH, NE, REQ * TOK], F32, kind="Internal").ap()

        s_const = lasting_sem("constants_landed")
        s_x = lasting_sem("x_landed")
        s_eps = lasting_sem("eps_ready")
        s_out = lasting_sem("outputs_stored")
        n_out = [0]
        act_link = lasting_sem("act_step_done")
        dve_link = lasting_sem("dve_step_done")
        links = {"act": 0, "dve": 0}

        def act_step(act, ins):
            links["act"] += 1
            ins.then_inc(act_link, 1)
            act.wait_ge(act_link, links["act"])

        def dve_step(dve, ins):
            links["dve"] += 1
            ins.then_inc(dve_link, 1)
            dve.wait_ge(dve_link, links["dve"])

        def store(eng, out, in_):
            n_out[0] += 16
            eng.dma_start(out, in_).then_inc(s_out, 16)

        class Stream:
            def __init__(self, name, sources):
                self.src = sources
                self.landed = [sem(f"{name}_landed{i}") for i in range(RING)]
                self.hi = sem(f"{name}_high_parts")
                self.lo = sem(f"{name}_low_parts")
                self.used = sem(f"{name}_multiplied")

            def load(self, sp, b):
                src = self.src(b)
                width = 1
                for n in src.shape[1:]:
                    width *= n
                dst = raw[b % RING][:, 0:width]
                if len(src.shape) == 3:
                    dst = dst.rearrange("p (k n) -> p k n", k=src.shape[1])
                sp.dma_start(dst, src).then_inc(self.landed[b % RING], 16)

        def colblocks(name, w, width, count):
            view = w.rearrange("(p k) n -> p k n", k=KD)
            return Stream(name, lambda b: view[:, :, b * width:(b + 1) * width]), count, width

        ada_landed = [[named(f"ada{l}_weights_landed{i}") for i in range(RING)] for l, named in enumerate((sem, lasting_sem))]

        def ada_columns(it, j):
            return (NADA - RING + j) * 256 if isinstance(it, int) and it == 0 else ((it - 1) * RING + j) * 256

        def ada_load(sp, l, it, j):
            sp.dma_start(raw[j][:, 0:KD * 256].rearrange("p (k n) -> p k n", k=KD),
                         t["ada_w"][l].rearrange("(p k) n -> p k n", k=KD)[:, :, bass.ds(ada_columns(it, j), 256)]).then_inc(ada_landed[l][j], 16)

        def ada(l, prefetch):
            with ExitStack() as scope:
                wh = [sb(f"ada{l}_wh{i}", [P, KD, 256], F32R, scope) for i in range(2)]
                wl = [sb(f"ada{l}_wl{i}", [P, KD, 256], F32R, scope) for i in range(2)]
                row4 = sb(f"ada{l}_row4", [4, 6 * D], F32, scope)
                bias4 = sb(f"ada{l}_bias4", [4, 6 * D], F32, scope)
                craw = sb(f"ada{l}_c", [P, REQ, KD], F32, scope)
                csil = sb(f"ada{l}_silu", [P, KD, REQ], F32, scope)
                cs = sb(f"ada{l}_cs", [P, KD, 4], F32R, scope)
                n = f"ada{l}_"
                landed = ada_landed[l]
                c_landed, b_landed, b_zero = sem(n + "c_landed"), sem(n + "bias_landed"), sem(n + "bias_zeroed")
                c_silu, c_hi, c_lo = sem(n + "c_silu"), sem(n + "c_high"), sem(n + "c_low")
                w_hi, w_lo = sem(n + "weights_high"), sem(n + "weights_low")
                rows_mm, rows = sem(n + "rows_multiplied"), sem(n + "rows_ready")
                cols_mm, cols = sem(n + "columns_multiplied"), sem(n + "columns_ready")
                gates_mm, gates_ready = sem(n + "gates_multiplied"), sem(n + "gates_ready")
                ROUNDS = NADA // RING
                GATES = [4, 5, 6, 7, 0, 1, 2, 3]
                MID = ROUNDS - 8 // RING
                gbank = lambda g: 3 + g % 5
                with nc.Block() as block:
                    @block.sync
                    def _(sp):
                        if l == 0:
                            ada_load(sp, l, 0, 0)
                        sp.dma_start(craw[:, 0, :], t["c_ctx"].rearrange("(p k) -> p k", k=KD)).then_inc(c_landed, 16)
                        sp.dma_start(craw[:, 1, :], t["c"][0].rearrange("(p k) -> p k", k=KD)).then_inc(c_landed, 16)
                        if l == 0:
                            for j in range(1, RING):
                                ada_load(sp, l, 0, j)
                            sp.dma_start(table[:, :], t["table"]).then_inc(s_const, 16)
                            sp.dma_start(pick[:, :], t["pick"]).then_inc(s_const, 16)
                            sp.dma_start(X[:, 0, :], t["x_prompt"][0]).then_inc(s_x, 16)
                            sp.dma_start(X[:, 1, :], t["x_sample"][0]).then_inc(s_x, 16)
                        with sp.Fori(1, ROUNDS) as it:
                            for j in range(RING):
                                sp.wait_ge(w_lo, (it - 1) * RING + j + 1)
                                ada_load(sp, l, it, j)
                        for j in range(RING):
                            sp.wait_ge(w_lo, NADA - RING + j + 1)
                            prefetch(sp, j)

                    @block.gpsimd
                    def _(pool):
                        pool.memset(bias4[:, :], 0.0).then_inc(b_zero, 1)
                        pool.wait_ge(b_zero, 1)
                        pool.dma_start(bias4[0:2, :], t["ada_b"][l:l + 1, :].partition_broadcast(2)).then_inc(b_landed, 16)

                    @block.scalar
                    def _(act):
                        act.wait_ge(c_landed, 32)
                        act.activation(csil[:, :, :], craw[:, :, :].rearrange("p r k -> p k r"), ACT.Silu).then_inc(c_silu, 1)
                        act.wait_ge(c_silu, 1)
                        act.activation(cs[:, :, 0:2], csil[:, :, :], ACT.Copy).then_inc(c_hi, 1)

                        def high(it, j):
                            b = it * RING + j
                            act.wait_ge(landed[j], it * 16 + 16)
                            wait(act, rows_mm, b - 1)
                            act.activation(wh[j % 2][:, :, :], raw[j][:, 0:KD * 256].rearrange("p (k n) -> p k n", k=KD),
                                           ACT.Copy).then_inc(w_hi, 1)
                        for j in range(RING):
                            high(0, j)
                        with act.Fori(1, MID) as it:
                            for j in range(RING):
                                high(it, j)
                        high(MID, 0)
                        for g, i in enumerate(GATES):
                            if g < 7:
                                high(MID + (g + 1) // RING, (g + 1) % RING)
                            act.wait_ge(gates_mm, g + 1)
                            act.activation(G[:, i // 4, i // 2 % 2, i % 2 * 512:i % 2 * 512 + 512], PS[:, gbank(g), :],
                                           ACT.Copy).then_inc(gates_ready, 1)
                        act.wait_ge(gates_ready, 8)

                    @block.vector
                    def _(dve):
                        if l == 0:
                            dve.memset(eps[:, 0:1], LN_EPS)
                            dve.memset(eps[:, 1:2], RMS_EPS).then_inc(s_eps, 1)
                        dve.wait_ge(c_hi, 1)
                        dve.tensor_tensor(cs[:, :, 2:4], csil[:, :, :], cs[:, :, 0:2].bitcast(F32), ALU.subtract).then_inc(c_lo, 1)

                        def low(it, j):
                            b = it * RING + j
                            dve.wait_ge(w_hi, b + 1)
                            wait(dve, rows_mm, b - 1)
                            dve.tensor_tensor(wl[j % 2][:, :, :], raw[j][:, 0:KD * 256].rearrange("p (k n) -> p k n", k=KD),
                                              wh[j % 2][:, :, :].bitcast(F32), ALU.subtract).then_inc(w_lo, 1)

                        def row(it, j):
                            b = it * RING + j
                            dve.wait_ge(rows_mm, b + 1)
                            at = bass.ds(ada_columns(it, j), 256)
                            dve.tensor_tensor(row4[:, at], PS[0:4, j % 2, 0:256], bias4[:, at], ALU.add).then_inc(rows, 1)
                        low(0, 0)
                        dve.wait_ge(b_landed, 16)
                        for j in range(1, RING):
                            low(0, j)
                            row(0, j - 1)
                        def columns(s):
                            c4 = PS[:, 2, 0:4 * KD * REQ].rearrange("p (s k r) -> p s k r", s=4, k=KD)
                            dve.tensor_scalar(COL[:, s, :, :], c4[:, s, :, :], float(s % 2), None, ALU.add).then_inc(cols, 1)

                        def round_of(it, j):
                            low(it, j)
                            if j:
                                row(it, j - 1)
                            else:
                                row(it - 1, RING - 1)
                        low(1, 0)
                        row(0, RING - 1)
                        for j in range(1, RING):
                            round_of(1, j)
                        with dve.Fori(2, MID) as it:
                            for j in range(RING):
                                round_of(it, j)
                        round_of(MID, 0)
                        dve.wait_ge(cols_mm, 1)
                        for s in range(2):
                            columns(s)
                        for b in range(MID * RING + 1, NADA):
                            round_of(b // RING, b % RING)
                        row(ROUNDS - 1, RING - 1)
                        dve.wait_ge(cols_mm, 2)
                        for s in range(2, 4):
                            columns(s)
                        dve.wait_ge(cols, 4)

                    @block.tensor
                    def _(pe):
                        pe.wait_ge(c_lo, 1)

                        def rows_product(it, j):
                            b = it * RING + j
                            pe.wait_ge(w_lo, b + 1)
                            wait(pe, rows, b - 1)
                            for k in range(KD):
                                pe.matmul(PS[0:4, j % 2, 0:256], cs[:, k, :], wh[j % 2][:, k, :], start=(k == 0), stop=False)
                                mm = pe.matmul(PS[0:4, j % 2, 0:256], cs[:, k, :], wl[j % 2][:, k, :], start=False, stop=(k == KD - 1))
                            mm.then_inc(rows_mm, 1)
                        for j in range(RING):
                            rows_product(0, j)
                        with pe.Fori(1, MID) as it:
                            for j in range(RING):
                                rows_product(it, j)

                        def columns(first):
                            for s in range(first, first + 2):
                                which = (0, 1, 3, 4)[s]
                                for k in range(KD):
                                    at = (s * KD + k) * REQ
                                    mm = pe.matmul(PS[:, 2, at:at + REQ], row4[:, which * D + k:which * D + D:KD], pick[:, 0:2],
                                                   start=True, stop=True)
                            mm.then_inc(cols_mm, 1)

                        pe.wait_ge(s_const, 32)
                        pe.wait_ge(rows, 3 * RING)
                        columns(0)
                        for g, i in enumerate(GATES):
                            rows_product(MID + g // RING, g % RING)
                            pe.wait_ge(rows, 4 * RING)
                            wait(pe, gates_ready, g - 4)
                            src = (2 if i < 4 else 5) * D + i % 2 * 512
                            pe.matmul(PS[:, gbank(g), :], pick[:, 2 + P * (i // 2 % 2):2 + P * (i // 2 % 2) + P], row4[:, src:src + 512],
                                      start=True, stop=True).then_inc(gates_mm, 1)
                        pe.wait_ge(rows, NADA)
                        pe.wait_ge(cols, 2)
                        columns(2)

        class Modulate:
            def __init__(self, name, s, scope):
                self.s = s
                self.HT = sb(name + "_HT", [P, KD, REQ * TOK], F32, scope)
                self.h = sb(name + "_HTh", [P, KD, REQ * TOK], F32R, scope)
                self.l = sb(name + "_HTl", [P, KD, REQ * TOK], F32R, scope)
                self.turned = sem(name + "_turned")
                self.mod = [sem(f"{name}_modulated{r}") for r in range(REQ)]
                self.hi = sem(name + "_high")
                self.lo = sem(name + "_low")

            def tensor(self, pe):
                for r in range(REQ):
                    for half in range(2):
                        for i in range(4):
                            k = half * 4 + i
                            mm = pe.transpose(PS[:, 2 * r + half, i * P:(i + 1) * P], X[:, r, k:D:KD], ident)
                        mm.then_inc(self.turned, 1)

            def scalar(self, act):
                act.wait_ge(self.turned, 2)
                for k in range(KD):
                    act.activation(self.HT[:, k, 0:TOK], PS[:, k // 4, k % 4 * P:k % 4 * P + P], ACT.Identity,
                                   bias=COL[:, self.s, k, 0:1], scale=COL[:, self.s + 1, k, 0:1]).then_inc(self.mod[0], 1)
                act.wait_ge(self.mod[0], KD)
                act.activation(self.h[:, :, 0:TOK], self.HT[:, :, 0:TOK], ACT.Copy).then_inc(self.hi, 1)
                act.wait_ge(self.mod[1], KD)
                act.activation(self.h[:, :, TOK:], self.HT[:, :, TOK:], ACT.Copy).then_inc(self.hi, 1)

            def vector(self, dve):
                dve.wait_ge(self.turned, 4)
                for k in range(KD):
                    dve.tensor_scalar(self.HT[:, k, TOK:], PS[:, 2 + k // 4, k % 4 * P:k % 4 * P + P],
                                      COL[:, self.s + 1, k, 1:2], COL[:, self.s, k, 1:2], ALU.mult, ALU.add).then_inc(self.mod[1], 1)
                for r in range(REQ):
                    dve.wait_ge(self.hi, r + 1)
                    at = slice(r * TOK, (r + 1) * TOK)
                    dve.tensor_tensor(self.l[:, :, at], self.HT[:, :, at], self.h[:, :, at].bitcast(F32), ALU.subtract).then_inc(self.lo, 1)

        def three(pe, out, ah, al, bh, bl, start, stop):
            pe.matmul(out, ah, bh, start=start, stop=False, skip_group_check=True)
            pe.matmul(out, ah, bl, start=False, stop=False, skip_group_check=True)
            return pe.matmul(out, al, bh, start=False, stop=stop, skip_group_check=True)

        class Norm:
            def __init__(self, name, l, ffn, banks, out_ready, scope, g_ap, b_ap):
                self.name, self.l, self.ffn, self.banks, self.out_ready = name, l, ffn, banks, out_ready
                self.gb = sb(name + "_gain_bias", [P, 2, D], F32, scope)
                self.tmp = sb(name + "_tmp", [P, REQ, D], F32, scope)
                self.st = sb(name + "_stats", [P, REQ, 2, 6], F32, scope)
                self.mv = sb(name + "_mean_var", [P, REQ, 2], F32, scope)
                self.rs = sb(name + "_rstd", [P, REQ, 4], F32, scope)
                self.landed = sem(name + "_gain_landed")
                self.var = sem(name + "_variance")
                self.std = sem(name + "_std")
                self.coef = sem(name + "_coefficients")
                self.unit = sem(name + "_unit")
                self.done = [sem(f"{name}_done{r}") for r in range(REQ)]
                self.g_ap, self.b_ap = g_ap, b_ap
                self.source = lambda r, n: PS[:, self.banks[2 * r + n], :]

            def sync(self, sp):
                sp.dma_start(self.gb[:, 0, :], self.g_ap.partition_broadcast(P)).then_inc(self.landed, 16)
                sp.dma_start(self.gb[:, 1, :], self.b_ap.partition_broadcast(P)).then_inc(self.landed, 16)

            def vector(self, dve):
                def gated(r):
                    self.out_ready(dve, r)
                    for n in range(2):
                        at = slice(n * 512, n * 512 + 512)
                        i = dve.tensor_tensor(self.tmp[:, r, at], self.source(r, n), G[:, self.ffn, r, at], ALU.mult)
                    dve_step(dve, i)

                def statistics(r):
                    dve_step(dve, dve.scalar_tensor_tensor(self.tmp[:, r, :], X[:, r, :], ALPHA, self.tmp[:, r, :], ALU.mult, ALU.add))
                    for n in range(2):
                        i = dve.bn_stats(self.st[:, r, n, :], self.tmp[:, r, n * 512:n * 512 + 512])
                    dve_step(dve, i)
                    dve.bn_aggr(self.mv[:, r, :], self.st[:, r, :, :]).then_inc(self.var, 1)

                def rstd(r):
                    dve.wait_ge(self.std, r + 1)
                    dve_step(dve, dve.reciprocal(self.rs[:, r, 1:2], self.rs[:, r, 0:1]))
                gated(0)
                statistics(0)
                gated(1)
                rstd(0)
                dve.scalar_tensor_tensor(self.rs[:, 0, 2:3], self.mv[:, 0, 0:1], -1.0, self.rs[:, 0, 1:2],
                                         ALU.mult, ALU.mult).then_inc(self.coef, 1)
                statistics(1)
                dve.wait_ge(self.landed, 32)
                dve.wait_ge(self.var, 2)
                dve_step(dve, dve.scalar_tensor_tensor(X[:, 1, :], self.tmp[:, 1, :], self.mv[:, 1, 0:1], self.gb[:, 0, :],
                                                       ALU.subtract, ALU.mult))
                rstd(1)
                dve.scalar_tensor_tensor(X[:, 1, :], X[:, 1, :], self.rs[:, 1, 1:2], self.gb[:, 1, :],
                                         ALU.mult, ALU.add).then_inc(self.done[1], 1)
                dve.wait_ge(self.done[1], 1)

            def scalar(self, act):
                act.wait_ge(s_eps, 1)
                act_step(act, act.activation(self.rs[:, 0, 3:4], eps[:, 0:1], ACT.Sqrt))
                for r in range(REQ):
                    act.wait_ge(self.var, r + 1)
                    act.activation(self.rs[:, r, 0:1], self.mv[:, r, 1:2], ACT.Sqrt, bias=eps[:, 0:1]).then_inc(self.std, 1)
                    if r == 0:
                        act.wait_ge(self.coef, 1)
                        act.activation(self.tmp[:, r, :], self.tmp[:, r, :], ACT.Identity, bias=self.rs[:, r, 2:3],
                                       scale=self.rs[:, r, 1:2]).then_inc(self.unit, 1)

            def gpsimd(self, pool):
                pool.wait_ge(self.landed, 32)
                pool.wait_ge(self.unit, 1)
                pool.tensor_tensor(X[:, 0, :], self.tmp[:, 0, :], self.gb[:, 0, :], ALU.mult).then_inc(self.done[0], 1)
                pool.wait_ge(self.done[0], 1)
                pool.tensor_tensor(X[:, 0, :], X[:, 0, :], self.gb[:, 1, :], ALU.add).then_inc(self.done[0], 1)
                pool.wait_ge(self.done[0], 2)

        class Project:
            def __init__(self, name, w, width, count, bank, lh, ll, scope, evac):
                self.name, self.width, self.count, self.bank, self.lh, self.ll, self.evac = name, width, count, bank, lh, ll, evac
                self.view = w.rearrange("(p k) n -> p k n", k=KD)
                self.wh = [sb(f"{name}_wh{i}", [P, KD, width], F32R, scope) for i in range(2)]
                self.wl = [sb(f"{name}_wl{i}", [P, KD, width], F32R, scope) for i in range(2)]
                self.landed = [sem(f"{name}_landed{i}") for i in range(RING)]
                self.hi, self.lo = sem(name + "_high"), sem(name + "_low")
                self.mm = sem(name + "_multiplied")
                self.ready = [sem(f"{name}_out{r}") for r in range(REQ)]

            def raw(self, b):
                return raw[b % RING][:, 0:KD * self.width].rearrange("p (k n) -> p k n", k=KD)

            def load(self, sp, b):
                sp.dma_start(self.raw(b), self.view[:, :, b * self.width:(b + 1) * self.width]).then_inc(self.landed[b % RING], 16)

            def sync(self, sp):
                for b in range(RING, self.count):
                    sp.wait_ge(self.lo, b - RING + 1)
                    self.load(sp, b)

            def scalar(self, act):
                for b in range(self.count + 1):
                    if b < self.count:
                        act.wait_ge(self.landed[b % RING], 16 * (b // RING + 1))
                        wait(act, self.mm, 2 * (b - 1))
                        act.activation(self.wh[b % 2][:, :, :], self.raw(b), ACT.Copy).then_inc(self.hi, 1)
                    if b and self.evac:
                        act.wait_ge(self.mm, 2 * b - 1)
                        self.evac(act, b - 1, 0).then_inc(self.ready[0], 1)

            def vector(self, dve):
                for b in range(self.count + 1):
                    if b < self.count:
                        dve.wait_ge(self.hi, b + 1)
                        dve.tensor_tensor(self.wl[b % 2][:, :, :], self.raw(b), self.wh[b % 2][:, :, :].bitcast(F32),
                                          ALU.subtract).then_inc(self.lo, 1)
                    if b and self.evac:
                        dve.wait_ge(self.mm, 2 * b)
                        self.evac(dve, b - 1, 1).then_inc(self.ready[1], 1)

            def tensor(self, pe):
                for b in range(self.count):
                    pe.wait_ge(self.lo, b + 1)
                    for r in range(REQ):
                        out = self.bank(b, r)
                        for k in range(KD):
                            at = slice(r * TOK, r * TOK + TOK)
                            mm = three(pe, out, self.lh[:, k, at], self.ll[:, k, at], self.wh[b % 2][:, k, :], self.wl[b % 2][:, k, :],
                                       start=(k == 0), stop=(k == KD - 1))
                        mm.then_inc(self.mm, 1)

        class Turn:
            def __init__(self, name, src, oh, ol):
                self.src, self.oh, self.ol = src, oh, ol
                self.turned, self.hi, self.lo = sem(name + "_turned"), sem(name + "_high"), sem(name + "_low")

            def tensor(self, pe):
                for r in range(REQ):
                    for half in range(2):
                        for i in range(4):
                            k = half * 4 + i
                            mm = pe.transpose(PS[:, 2 * r + half, i * P:(i + 1) * P], self.src[:, r, k:D:KD], ident)
                        mm.then_inc(self.turned, 1)

            def scalar(self, act):
                for q in range(4):
                    act.wait_ge(self.turned, q + 1)
                    act.activation(self.oh[:, q % 2 * 4:q % 2 * 4 + 4, q // 2 * TOK:q // 2 * TOK + TOK],
                                   PS[:, q, :].rearrange("p (k t) -> p k t", k=4), ACT.Copy).then_inc(self.hi, 1)

            def vector(self, dve):
                for q in range(4):
                    dve.wait_ge(self.hi, q + 1)
                    at = (slice(None), slice(q % 2 * 4, q % 2 * 4 + 4), slice(q // 2 * TOK, q // 2 * TOK + TOK))
                    dve.tensor_tensor(self.ol[at], PS[:, q, :].rearrange("p (k t) -> p k t", k=4), self.oh[at].bitcast(F32),
                                      ALU.subtract).then_inc(self.lo, 1)

        class Attend:
            def __init__(self, name, QT, KT, V, dim, scale, sink, merged, at, bufs):
                self.n, self.QT, self.KT, self.V, self.dim, self.scale, self.sink, self.merged, self.at = \
                    name, QT, KT, V, dim, scale, sink, merged, at
                self.Pb, self.PT = bufs
                self.st = sb(name + "_softmax", [P, 8, REQ, H], F32, mix_scope[0])
                self.scores, self.maxed = sem(name + "_scores"), sem(name + "_negmax")
                self.probs, self.tot, self.es = sem(name + "_probs"), sem(name + "_rowsums"), sem(name + "_sink_exp")
                self.pturn, self.pt = sem(name + "_probs_turned"), [sem(f"{name}_probsT{i}") for i in range(2)]
                self.pv, self.done = sem(name + "_values"), sem(name + "_merged")

            def sbank(self, r):
                if r == 0:
                    return PS[:, 0:2, :].rearrange("p b (h k) -> p (b h) k", k=TOK)
                return PS[:, 2:6, :].rearrange("p b (h k) -> p (b h) k", k=2 * TOK)

            def tensor(self, pe):
                for r in range(REQ):
                    for h in range(H):
                        mm = pe.matmul(self.sbank(r)[:, h, :], self.QT[0:self.dim, r, h, :],
                                       self.KT(h, r, 1 + r), start=True, stop=True)
                    mm.then_inc(self.scores, 1)
                for c in range(6):
                    if c < 2:
                        pe.wait_ge(self.probs, 4 * c + 4)
                        if c == 0:
                            pe.wait_ge(self.probs, 8)
                    else:
                        pe.wait_ge(self.probs, 8 + 2 * (c - 1))
                        if c == 2:
                            pe.wait_ge(self.probs, 16)
                    bank = [6, 7, 0, 1, 2, 3][c]
                    if c >= 2:
                        pe.wait_ge(self.probs, 16)
                    for i in range(4):
                        mm = pe.transpose(PS[:, bank, i * P:(i + 1) * P], self.Pb[:, (4 * c + i) * P:(4 * c + i + 1) * P], ident)
                    mm.then_inc(self.pturn, 1)
                for r in range(REQ):
                    pe.wait_ge(self.pt[0], 1 if r == 0 else 3)
                    pe.wait_ge(self.pt[1], 1 if r == 0 else 3)
                    for h in range(H):
                        out = PS[:, 4 + r, h * VD:(h + 1) * VD]
                        if r == 0:
                            mm = pe.matmul(out, self.PT[:, h * P:(h + 1) * P], self.V(h, 0), start=True, stop=True)
                        else:
                            for s in range(2):
                                c = H + 2 * h + s
                                mm = pe.matmul(out, self.PT[:, c * P:(c + 1) * P], self.V(h, 1 + s), start=(s == 0), stop=(s == 1))
                    mm.then_inc(self.pv, 1)

            def vector(self, dve):
                st = self.st
                for r in range(REQ):
                    dve.wait_ge(self.scores, r + 1)
                    dve_step(dve, dve.tensor_reduce(st[:, 0, r, :], self.sbank(r), AX_X, ALU.max))
                    if self.sink is None:
                        dve.tensor_scalar(st[:, 1, r, :], st[:, 0, r, :], -self.scale, None, ALU.mult).then_inc(self.maxed, 1)
                    else:
                        dve_step(dve, dve.scalar_tensor_tensor(st[:, 2, r, :], st[:, 0, r, :], self.scale, self.sink, ALU.mult, ALU.max))
                        dve_step(dve, dve.tensor_scalar(st[:, 1, r, :], st[:, 2, r, :], -1.0, None, ALU.mult))
                        dve.tensor_tensor(st[:, 3, r, :], self.sink, st[:, 1, r, :], ALU.add).then_inc(self.maxed, 1)
                for c in (1, 3, 5):
                    dve.wait_ge(self.pturn, c + 1)
                    bank = [6, 7, 0, 1, 2, 3][c]
                    dve.tensor_copy(self.PT[:, 4 * c * P:4 * (c + 1) * P], PS[:, bank, :]).then_inc(self.pt[1], 1)
                for r in range(REQ):
                    if self.sink is None:
                        dve.wait_ge(self.probs, 16)
                        dve_step(dve, dve.reciprocal(st[:, 6, r, :], st[:, 4, r, :]))
                    else:
                        dve.wait_ge(self.es, r + 1)
                        dve_step(dve, dve.tensor_tensor(st[:, 7, r, :], st[:, 4, r, :], st[:, 5, r, :], ALU.add))
                        dve_step(dve, dve.reciprocal(st[:, 6, r, :], st[:, 7, r, :]))
                    dve.wait_ge(self.pv, r + 1)
                    dve.tensor_tensor(self.merged[:, r, self.at:self.at + H * VD].rearrange("p (h e) -> p h e", h=H),
                                      PS[:, 4 + r, :].rearrange("p (h e) -> p h e", h=H),
                                      st[:, 6, r, :].unsqueeze(2).to_broadcast([P, H, VD]), ALU.mult).then_inc(self.done, 1)

            def scalar(self, act):
                st = self.st
                for r in range(REQ):
                    act.wait_ge(self.maxed, r + 1)
                    for h in range(H):
                        w = TOK * (1 + r)
                        base = h * TOK if r == 0 else H * TOK + 2 * h * TOK
                        act.activation(self.Pb[:, base:base + w], self.sbank(r)[:, h, :], ACT.Exp, bias=st[:, 1, r, h:h + 1],
                                       scale=self.scale, accum_out=st[:, 4, r, h:h + 1]).then_inc(self.probs, 1)
                    if self.sink is not None:
                        act.activation(st[:, 5, r, :], st[:, 3, r, :], ACT.Exp).then_inc(self.es, 1)
                for c in (0, 2, 4):
                    act.wait_ge(self.pturn, c + 1)
                    bank = [6, 7, 0, 1, 2, 3][c]
                    act.activation(self.PT[:, 4 * c * P:4 * (c + 1) * P], PS[:, bank, :], ACT.Copy).then_inc(self.pt[0], 1)

        mix_scope = [None]

        def mixer0(project_in, project_out_holder, prefetch_next):
            proj, merged = project_in.proj, project_in.merged
            with ExitStack() as scope:
                mod = Modulate("mix0_mod", 0, scope)
                pr = project_in
                pr.alloc(scope)
                pr.p.lh, pr.p.ll = mod.h, mod.l
                with nc.Block() as block:
                    @block.sync
                    def _(sp):
                        sp.wait_ge(pr.p.lo, 1)
                        sp.dma_start(raw[0][:, 0:2 * H * QK].rearrange("p (k n) -> p k n", k=2),
                                     t["mla_w_uq"][0].rearrange("(p k) n -> p k n", k=2)).then_inc(pr.uq_landed, 16)
                        sp.dma_start(raw[0][:, 2 * H * QK:2 * H * QK + H * (NOPE + VD)], t["mla_w_ukv"][0]).then_inc(pr.uq_landed, 16)

                    @block.tensor
                    def _(pe):
                        pe.wait_ge(s_x, 32)
                        mod.tensor(pe)
                        pe.wait_ge(mod.lo, 2)
                        pr.p.tensor(pe)

                    @block.scalar
                    def _(act):
                        mod.scalar(act)
                        pr.p.scalar(act)
                        act.wait_ge(pr.p.ready[0], pr.p.count)

                    @block.vector
                    def _(dve):
                        mod.vector(dve)
                        pr.p.vector(dve)
                        dve.wait_ge(pr.p.ready[1], pr.p.count)
            with ExitStack() as scope:
                mix_scope[0] = scope
                Pb = sb("probs", [P, 3 * H * TOK], F32, scope)
                PT = sb("probsT", [P, 3 * H * TOK], F32, scope)
                QT = sb("QT", [QK, REQ, H, TOK], F32, scope)
                KT = sb("KT", [QK, H, 3, TOK], F32, scope)
                cq = sb("cq_n", [P, REQ, RQ], F32, scope)
                ckv = sb("ckv_n", [P, 3, RKV], F32, scope)
                cqT = sb("cqT", [P, 2, REQ, TOK], F32, scope)
                ckvT = sb("ckvT", [P, 3, TOK], F32, scope)
                QM = sb("QM", [P, REQ, H, QK], F32, scope)
                KM = sb("KM", [P, 3, H, QK], F32, scope)
                VM = sb("VM", [P, 3, H, VD], F32, scope)
                kcv = sb("cache_kv", [P, 2, KV * HD], F32, scope)
                krc = sb("cache_kr", [P, ROPE], F32, scope)
                norms = sb("norm_gains", [P, RQ + RKV], F32, scope)
                sink = sb("sink_b", [P, H], F32, scope)
                rt = sb("rope_tmp", [P, 4, 10 * 32], F32, scope)
                rms = sb("rms", [P, 3, 4], F32, scope)
                junk = sb("junk", [P, RQ], F32, scope)
                landed = sem("attn_inputs_landed")
                roped, kr_roped = sem("rope_done"), sem("mla_k_rope_done")
                a_turn, a_t = sem("a_turned"), [sem("a_turned_act"), sem("a_turned_dve")]
                sq, msq, std, rmsed = sem("rms_squares"), sem("rms_mean"), sem("rms_root"), sem("rms_done")
                c_turn, cT = sem("c_turned"), sem("cT_ready")
                qm_mm, qm = sem("qm_multiplied"), sem("qm_ready")
                kv_mm, kv_e = sem("kv_multiplied"), [sem("kv_act"), sem("kv_dve")]
                qroped = sem("qm_roped")
                m_turn, m_t = sem("m_turned"), [sem("m_turned_act"), sem("m_turned_dve")]
                kfill = sem("k_rope_filled")
                proj_v = proj
                atA = Attend("attA", QT, lambda h, s, n: KT[0:HD, h // GRP, s:s + n, :],
                             lambda h, s: (proj[:, s, A_V + h // GRP * HD:A_V + (h // GRP + 1) * HD] if s < 2
                                           else kcv[:, 1, h // GRP * HD:(h // GRP + 1) * HD]),
                             HD, SC_A, sink[:, :], merged, 0, (Pb, PT))
                atM = Attend("attM", QT, lambda h, s, n: KT[0:QK, h, s:s + n, :], lambda h, s: VM[:, s, h, :],
                             QK, SC_M, None, merged, H * HD, (Pb, PT))

                def rotate(dve, src, heads, quarter, tab):
                    x = src.rearrange("p h (a b w) -> p h a b w", a=2, b=2)
                    x1, x2 = x[:, :, :, 0, :], x[:, :, :, 1, :]
                    cs = tab.rearrange("p (s a w) -> p s a w", s=2, a=2)
                    shape = [P, heads, 2, quarter]
                    co = cs[:, 0, :, :].unsqueeze(1).to_broadcast(shape)
                    si = cs[:, 1, :, :].unsqueeze(1).to_broadcast(shape)
                    tm = [rt[:, i, 0:heads * 2 * quarter].rearrange("p (h a w) -> p h a w", h=heads, a=2) for i in range(4)]
                    dve.tensor_tensor(tm[0], x1, co, ALU.mult)
                    dve.tensor_tensor(tm[1], x2, si, ALU.mult)
                    dve.tensor_tensor(tm[2], x1, si, ALU.mult)
                    dve_step(dve, dve.tensor_tensor(tm[3], x2, co, ALU.mult))
                    dve_step(dve, dve.tensor_tensor(x1, tm[0], tm[1], ALU.subtract))
                    return dve.tensor_tensor(x2, tm[2], tm[3], ALU.add)

                def a_copy(eng, q):
                    src = PS[0:HD, q, :]
                    if q < 4:
                        dst = QT[0:HD, q // 2, q % 2 * 4:q % 2 * 4 + 4, :]
                        src = src.rearrange("p (h t) -> p h t", h=4)
                    else:
                        src = src[:, 0:3 * TOK].rearrange("p (h t) -> p h t", h=3)
                        dst = KT[0:HD, q - 4, :, :]
                    if q % 2 == 0:
                        eng.activation(dst, src, ACT.Copy).then_inc(a_t[0], 1)
                    else:
                        eng.tensor_copy(dst, src).then_inc(a_t[1], 1)

                def kv_copy(eng, i):
                    eng.wait_ge(kv_mm, i + 1)
                    bank = [4, 5, 6, 7, 0, 1][i]
                    v = PS[:, bank, :].rearrange("p (h e) -> p h e", h=4)
                    hs = slice(i % 2 * 4, i % 2 * 4 + 4)
                    if i % 2 == 0:
                        eng.activation(KM[:, i // 2, hs, 0:NOPE], v[:, :, 0:NOPE], ACT.Copy)
                        eng.activation(VM[:, i // 2, hs, :], v[:, :, NOPE:], ACT.Copy).then_inc(kv_e[0], 1)
                    else:
                        eng.tensor_copy(KM[:, i // 2, hs, 0:NOPE], v[:, :, 0:NOPE])
                        eng.tensor_copy(VM[:, i // 2, hs, :], v[:, :, NOPE:]).then_inc(kv_e[1], 1)

                MB = [2, 3, 4, 5, 6, 7, 0, 1, 2, 3]

                def m_copy(eng, q):
                    src = PS[0:QK, MB[q], :].rearrange("p (h t) -> p h t", h=4)
                    hs = slice(q % 2 * 4, q % 2 * 4 + 4)
                    dst = QT[:, q // 2, hs, :] if q < 4 else KT[:, hs, (q - 4) // 2, :]
                    if q % 2 == 0:
                        eng.activation(dst, src, ACT.Copy).then_inc(m_t[0], 1)
                    else:
                        eng.tensor_copy(dst, src).then_inc(m_t[1], 1)

                with nc.Block() as block:
                    @block.sync
                    def _(sp):
                        sp.dma_start(kcv[:, 0, :], t["cache_attn_k"][0, 0].rearrange("k h d -> k (h d)")).then_inc(landed, 16)
                        sp.dma_start(kcv[:, 1, :], t["cache_attn_v"][0, 0].rearrange("k h d -> k (h d)")).then_inc(landed, 16)
                        sp.dma_start(krc[:, :], t["cache_mla_krope"][0, 0]).then_inc(landed, 16)
                        sp.dma_start(ckv[:, 2, :], t["cache_mla_ckv"][0, 0]).then_inc(landed, 16)
                        sp.dma_start(sink[:, :], t["attn_sink"].partition_broadcast(P)).then_inc(landed, 16)
                        sp.dma_start(norms[:, 0:RQ], t["mla_q_norm"].partition_broadcast(P)).then_inc(landed, 16)
                        sp.dma_start(norms[:, RQ:], t["mla_kv_norm"].partition_broadcast(P)).then_inc(landed, 16)
                        store(sp, k_out[0, 0].rearrange("k h d -> k (h d)"), proj[:, 0, A_K:A_V])
                        store(sp, v_out[0, 0].rearrange("k h d -> k (h d)"), proj[:, 0, A_V:A_CQ])
                        store(sp, kr_out[0, 0], proj[:, 0, A_KR:W_AB])
                        sp.wait_ge(rmsed, 4)
                        store(sp, ckv_out[0, 0], ckv[:, 0, :])
                        for b in range(1, RING):
                            project_out_holder.load(sp, b)
                        sp.wait_ge(kv_mm, 6)
                        project_out_holder.load(sp, 0)
                        sp.wait_ge(s_out, n_out[0])

                    @block.scalar
                    def _(act):
                        for r in range(REQ):
                            act.activation(junk[:, 0:RQ], proj[:, r, A_CQ:A_CKV], ACT.Square, accum_out=rms[:, 0, 2 * r:2 * r + 1]).then_inc(sq, 1)
                            act.wait_ge(sq, 2 * r + 1)
                            act.activation(junk[:, 0:RKV], proj[:, r, A_CKV:A_KR], ACT.Square, accum_out=rms[:, 0, 2 * r + 1:2 * r + 2]).then_inc(sq, 1)
                            act.wait_ge(sq, 2 * r + 2)
                        act.wait_ge(msq, 2)
                        act.activation(rms[:, 2, :], rms[:, 1, :], ACT.Sqrt).then_inc(std, 1)
                        for q in (0, 2, 4):
                            act.wait_ge(a_turn, q + 1)
                            a_copy(act, q)
                        atA.scalar(act)
                        for q in range(2):
                            act.wait_ge(c_turn, q + 1)
                            if q == 0:
                                act.activation(cqT[:, :, :, :], PS[:, 6, :].rearrange("p (k r t) -> p k r t", k=2, r=2), ACT.Copy).then_inc(cT, 1)
                            else:
                                act.activation(ckvT[:, :, :], PS[:, 7, 0:3 * TOK].rearrange("p (s t) -> p s t", s=3), ACT.Copy).then_inc(cT, 1)
                        for i in range(4):
                            act.wait_ge(qm_mm, i + 1)
                            act.activation(QM[:, i // 2, i % 2 * 4:i % 2 * 4 + 4, :], PS[:, i, 0:4 * QK].rearrange("p (h d) -> p h d", h=4),
                                           ACT.Copy).then_inc(qm, 1)
                        for i in (0, 2, 4):
                            kv_copy(act, i)
                        for q in range(0, 10, 2):
                            act.wait_ge(m_turn, q + 1)
                            m_copy(act, q)
                        atM.scalar(act)

                    @block.vector
                    def _(dve):
                        rotate(dve, proj[:, 1, 0:A_V].rearrange("p (h d) -> p h d", d=HD), H + KV, HD // 4, table[:, T_RA:T_RM]).then_inc(roped, 1)
                        dve.wait_ge(roped, 1)
                        rotate(dve, proj[:, 1, A_KR:W_AB].unsqueeze(1), 1, ROPE // 4, table[:, T_RM:T_IO]).then_inc(kr_roped, 1)
                        dve.wait_ge(sq, 4)
                        for j, n in enumerate((RQ, RKV)):
                            dve.tensor_scalar(rms[:, 1, j:4:2], rms[:, 0, j:4:2], 1.0 / n, RMS_EPS, ALU.mult, ALU.add).then_inc(msq, 1)
                        dve.wait_ge(std, 1)
                        dve_step(dve, dve.reciprocal(rms[:, 0, :], rms[:, 2, :]))
                        dve.wait_ge(landed, 7 * 16)
                        for r in range(REQ):
                            dve.scalar_tensor_tensor(cq[:, r, :], proj[:, r, A_CQ:A_CKV], rms[:, 0, 2 * r:2 * r + 1], norms[:, 0:RQ],
                                                     ALU.mult, ALU.mult).then_inc(rmsed, 1)
                            dve.scalar_tensor_tensor(ckv[:, r, :], proj[:, r, A_CKV:A_KR], rms[:, 0, 2 * r + 1:2 * r + 2], norms[:, RQ:],
                                                     ALU.mult, ALU.mult).then_inc(rmsed, 1)
                        dve.wait_ge(kr_roped, 1)
                        for s in range(3):
                            src = krc[:, :] if s == 2 else proj[:, s, A_KR:W_AB]
                            dve.tensor_copy(KM[:, s, :, NOPE:], src.unsqueeze(1).to_broadcast([P, H, ROPE])).then_inc(kfill, 1)
                        for q in (1, 3, 5):
                            dve.wait_ge(a_turn, q + 1)
                            a_copy(dve, q)
                        atA.vector(dve)
                        dve.wait_ge(qm, 4)
                        rotate(dve, QM[:, 1, :, NOPE:], H, ROPE // 4, table[:, T_RM:T_IO]).then_inc(qroped, 1)
                        for i in (1, 3, 5):
                            kv_copy(dve, i)
                        for q in range(1, 10, 2):
                            dve.wait_ge(m_turn, q + 1)
                            m_copy(dve, q)
                        atM.vector(dve)
                        dve.wait_ge(atM.done, 2)

                    @block.tensor
                    def _(pe):
                        pe.wait_ge(landed, 7 * 16)
                        pe.wait_ge(roped, 1)
                        for q in range(4):
                            for i in range(4):
                                h = q % 2 * 4 + i
                                mm = pe.transpose(PS[0:HD, q, i * P:(i + 1) * P], proj[:, q // 2, h * HD:(h + 1) * HD], ident)
                            mm.then_inc(a_turn, 1)
                        for g in range(KV):
                            for s in range(3):
                                src = kcv[:, 0, g * HD:(g + 1) * HD] if s == 2 else proj[:, s, A_K + g * HD:A_K + (g + 1) * HD]
                                mm = pe.transpose(PS[0:HD, 4 + g, s * P:(s + 1) * P], src, ident)
                            mm.then_inc(a_turn, 1)
                        pe.wait_ge(a_t[0], 3)
                        pe.wait_ge(a_t[1], 3)
                        atA.tensor(pe)
                        pe.wait_ge(rmsed, 4)
                        for k in range(2):
                            for r in range(REQ):
                                mm = pe.transpose(PS[:, 6, (2 * k + r) * P:(2 * k + r + 1) * P], cq[:, r, k:RQ:2], ident)
                        mm.then_inc(c_turn, 1)
                        for s in range(3):
                            mm = pe.transpose(PS[:, 7, s * P:(s + 1) * P], ckv[:, s, :], ident)
                        mm.then_inc(c_turn, 1)
                        pe.wait_ge(cT, 2)
                        pe.wait_ge(project_in.uq_landed, 32)
                        uq = raw[0][:, 0:2 * H * QK].rearrange("p (k n) -> p k n", k=2)
                        for i in range(4):
                            for k in range(2):
                                mm = pe.matmul(PS[:, i, 0:4 * QK], cqT[:, k, i // 2, :], uq[:, k, i % 2 * 4 * QK:i % 2 * 4 * QK + 4 * QK],
                                               start=(k == 0), stop=(k == 1))
                            mm.then_inc(qm_mm, 1)
                        pe.wait_ge(atA.done, 2)
                        for i in range(6):
                            if i == 4:
                                pe.wait_ge(qm, 2)
                            bank = [4, 5, 6, 7, 0, 1][i]
                            w0 = 2 * H * QK + i % 2 * 512
                            pe.matmul(PS[:, bank, :], ckvT[:, i // 2, :], raw[0][:, w0:w0 + 512], start=True, stop=True).then_inc(kv_mm, 1)
                        pe.wait_ge(qm, 4)
                        pe.wait_ge(qroped, 1)
                        pe.wait_ge(kfill, 3)
                        pe.wait_ge(kv_e[0], 3)
                        pe.wait_ge(kv_e[1], 3)
                        for q in range(10):
                            if q >= 8:
                                pe.wait_ge(m_t[q % 2], (q - 8) // 2 + 1)
                            for i in range(4):
                                h = q % 2 * 4 + i
                                src = QM[:, q // 2, h, :] if q < 4 else KM[:, (q - 4) // 2, h, :]
                                mm = pe.transpose(PS[0:QK, MB[q], i * P:(i + 1) * P], src, ident)
                            mm.then_inc(m_turn, 1)
                        pe.wait_ge(m_t[0], 5)
                        pe.wait_ge(m_t[1], 5)
                        atM.tensor(pe)

        class In0:
            def __init__(self, scope):
                self.proj = sb("proj", [P, REQ, W_AB], F32, scope)
                self.merged = sb("merged", [P, REQ, D], F32, scope)
                self.uq_landed = sem("uq_landed")

            def alloc(self, scope):
                pass

        def ab_width():
            return W_AB // 4

        def run_layer0():
            with ExitStack() as outer:
                in0 = In0(outer)
                wi = ab_width()

                def evac_in(eng, b, r):
                    src = PS[:, (2 * b + r) % 8, 0:wi]
                    dst = in0.proj[:, r, b * wi:(b + 1) * wi]
                    return eng.activation(dst, src, ACT.Copy) if r == 0 else eng.tensor_copy(dst, src)
                w_in_holder = LateProject("w_in_ab", t["w_in_ab"][0], wi, 4, lambda b, r: PS[:, (2 * b + r) % 8, 0:wi], None, None, evac_in)
                ada(0, lambda sp, j: w_in_holder.load(sp, j))
                in0.p = w_in_holder
                in0.alloc = w_in_holder.alloc
                w_out = LateProject("w_out_ab", t["w_out_ab"][0], 256, 4,
                                    lambda b, r: PS[:, 4 + 2 * r + b // 2, b % 2 * 256:b % 2 * 256 + 256], None, None, None)
                mixer0(in0, w_out, None)
                with ExitStack() as scope:
                    MTh = sb("mergedT_h", [P, KD, REQ * TOK], F32R, scope)
                    MTl = sb("mergedT_l", [P, KD, REQ * TOK], F32R, scope)
                    w_out.lh, w_out.ll = MTh, MTl
                    w_out.alloc(scope)
                    turn = Turn("merged", in0.merged, MTh, MTl)
                    norm = Norm("ln_mix0", 0, 0, [4, 5, 6, 7], lambda e, r: e.wait_ge(w_out.mm, 8), scope, t["ln_mix_g"][0:1, :], t["ln_mix_b"][0:1, :])
                    with nc.Block() as block:
                        @block.sync
                        def _(sp):
                            norm.sync(sp)
                            for j in range(RING):
                                sp.wait_ge(w_out.lo, j + 1)
                                moes[0].load_weights(sp, 0, j)

                        @block.tensor
                        def _(pe):
                            turn.tensor(pe)
                            pe.wait_ge(turn.lo, 4)
                            w_out.tensor(pe)

                        @block.scalar
                        def _(act):
                            turn.scalar(act)
                            w_out.scalar(act)
                            norm.scalar(act)

                        @block.gpsimd
                        def _(pool):
                            norm.gpsimd(pool)

                        @block.vector
                        def _(dve):
                            turn.vector(dve)
                            w_out.vector(dve)
                            norm.vector(dve)

        class LateProject(Project):
            def __init__(self, name, w, width, count, bank, lh, ll, evac):
                self.name, self.width, self.count, self.bank, self.lh, self.ll, self.evac = name, width, count, bank, lh, ll, evac
                self.view = w.rearrange("(p k) n -> p k n", k=KD)
                self.landed = [sem(f"{name}_landed{i}") for i in range(RING)]
                self.hi, self.lo = sem(name + "_high"), sem(name + "_low")
                self.mm = sem(name + "_multiplied")
                self.ready = [sem(f"{name}_out{r}") for r in range(REQ)]

            def alloc(self, scope):
                self.wh = [sb(f"{self.name}_wh{i}", [P, KD, self.width], F32R, scope) for i in range(2)]
                self.wl = [sb(f"{self.name}_wl{i}", [P, KD, self.width], F32R, scope) for i in range(2)]

        class Moe:
            def __init__(self, l):
                self.l = l
                n = f"moe{l}_"
                self.landed = [sem(f"{n}weights_landed{i}") for i in range(RING)]
                self.gate_landed = [sem(f"{n}gate_landed{i}") for i in range(RING)]
                names = ("up_high", "up_low", "down_high", "down_low", "up_multiplied", "down_multiplied",
                         "silu", "product", "gated", "hidden_high", "hidden_low",
                         "router_landed", "router_high", "router_low", "router_multiplied", "router_scores",
                         "scores_turned", "gates", "gates_turned", "gatesT", "gates_stored", "first_request_done")
                self.s = {k: sem(n + k) for k in names}

            def load_weights(self, sp, it, j):
                l, e = self.l, it * RING + j - 1
                if isinstance(e, int) and e < 0:
                    src = (t["sh_w_gate"][l], t["sh_w_up"][l], t["sh_w_down"][l])
                else:
                    src = [t[k][l, bass.ds(e, 1)].rearrange("o a b -> (o a) b") for k in ("exp_w_gate", "exp_w_up", "exp_w_down")]
                for i in range(2):
                    sp.dma_start(raw[j][:, i * D:(i + 1) * D], src[i].rearrange("(p k) f -> p (k f)", k=KD)).then_inc(self.landed[j], 16)
                sp.dma_start(raw[j][:, 2 * D:3 * D], src[2]).then_inc(self.landed[j], 16)

            def run(self, prefetch, final):
                l, s = self.l, self.s
                n = f"moe{l}_"
                GRPS = (NE - RING) // RING
                with ExitStack() as scope:
                    mod = Modulate(n + "mod", 2, scope)
                    uh = [sb(f"{n}up_h{i}", [P, 2, KD, FF], F32R, scope) for i in range(2)]
                    ul = [sb(f"{n}up_l{i}", [P, 2, KD, FF], F32R, scope) for i in range(2)]
                    dh = [sb(f"{n}down_h{i}", [P, D], F32R, scope) for i in range(2)]
                    dl = [sb(f"{n}down_l{i}", [P, D], F32R, scope) for i in range(2)]
                    gb = [sb(f"{n}gate_b{i}", [P, REQ * TOK], F32, scope) for i in range(RING)]
                    sg = [sb(f"{n}silu{i}", [P, REQ * TOK], F32, scope) for i in range(2)]
                    pr = [sb(f"{n}prod{i}", [P, REQ * TOK], F32, scope) for i in range(2)]
                    hg = [sb(f"{n}hid{i}", [P, REQ * TOK], F32, scope) for i in range(2)]
                    hh = [sb(f"{n}hid_h{i}", [P, REQ * TOK], F32R, scope) for i in range(2)]
                    hl = [sb(f"{n}hid_l{i}", [P, REQ * TOK], F32R, scope) for i in range(2)]
                    rw = sb(n + "router", [P, KD, NE], F32, scope)
                    rwh = sb(n + "router_h", [P, KD, NE], F32R, scope)
                    rwl = sb(n + "router_l", [P, KD, NE], F32R, scope)
                    rb = sb(n + "router_b", [P, NE], F32, scope)
                    scT = sb(n + "scoresT", [NE, REQ * TOK], F32, scope)
                    sc = PS[:, 3, 0:REQ * NE].rearrange("p (r e) -> p r e", r=REQ)
                    sel = sb(n + "biased", [P, REQ, NE], F32, scope)
                    m8 = sb(n + "top8", [P, REQ, 8], F32, scope)
                    i8 = sb(n + "top8_at", [P, REQ, 8], U32, scope)
                    f8 = sb(n + "top8_f", [P, REQ, 8], F32, scope)
                    mask = sb(n + "mask", [P, REQ, NE], F32, scope)
                    gt = sb(n + "gates_t", [P, REQ, NE], F32, scope)
                    sm = sb(n + "gate_sum", [P, REQ, 2], F32, scope)
                    gT = sb(n + "gatesT_sb", [NE, REQ * TOK], F32, scope)
                    norm = Norm(f"ln_ffn{l}", l, 1, [4, 5, 6, 7], lambda e, r: e.wait_ge(*((s["down_multiplied"], NE + 1) if r else (s["first_request_done"], 1))), scope,
                                t["ln_ffn_g"][l:l + 1, :], t["ln_ffn_b"][l:l + 1, :])

                    def items(eng, first, body):
                        for j in range(first, RING):
                            body(0, j)
                        with eng.Fori(1, 1 + GRPS) as it:
                            for j in range(RING):
                                body(it, j)
                        body(1 + GRPS, 0)

                    def split_up_high(act, it, j):
                        act.wait_ge(self.landed[j], it * 48 + 48)
                        wait(act, s["up_multiplied"], it * RING + j - 1)
                        act.activation(uh[j % 2][:, :, :, :].rearrange("p a k f -> p (a k f)"), raw[j][:, 0:2 * D], ACT.Copy).then_inc(s["up_high"], 1)

                    def split_down_high(act, it, j):
                        wait(act, s["down_multiplied"], it * RING + j - 1)
                        act.activation(dh[j % 2][:, :], raw[j][:, 2 * D:3 * D], ACT.Copy).then_inc(s["down_high"], 1)

                    def following(it, j):
                        return (it, j + 1) if j + 1 < RING else (it + 1, 0)

                    def split_up_low(dve, it, j):
                        dve.wait_ge(s["up_high"], it * RING + j + 1)
                        dve.tensor_tensor(ul[j % 2][:, :, :, :].rearrange("p a k f -> p (a k f)"), raw[j][:, 0:2 * D],
                                          uh[j % 2][:, :, :, :].rearrange("p a k f -> p (a k f)").bitcast(F32), ALU.subtract).then_inc(s["up_low"], 1)

                    def split_down_low(dve, it, j):
                        dve.wait_ge(s["down_high"], it * RING + j + 1)
                        dve.tensor_tensor(dl[j % 2][:, :], raw[j][:, 2 * D:3 * D], dh[j % 2][:, :].bitcast(F32), ALU.subtract).then_inc(s["down_low"], 1)

                    with nc.Block() as block:
                        @block.sync
                        def _(sp):
                            sp.dma_start(rw[:, :, :], t["router_w"][l].rearrange("(p k) e -> p k e", k=KD)).then_inc(s["router_landed"], 16)
                            sp.dma_start(rb[:, :], t["router_bias"][l:l + 1, :].partition_broadcast(P)).then_inc(s["router_landed"], 16)
                            norm.sync(sp)
                            sp.wait_ge(s["gatesT"], 1)
                            sp.dma_start(gate_rows[l], gT[:, :]).then_inc(s["gates_stored"], 16)
                            sp.wait_ge(s["gates_stored"], 16)

                            def load(it, j):
                                i = it * RING + j
                                if not (isinstance(it, int) and it == 0):
                                    sp.wait_ge(s["down_low"], i - RING + 1)
                                    self.load_weights(sp, it, j)
                                    wait(sp, s["gated"], i - RING)
                                sp.dma_start(gb[j][:, :], gate_rows[l, bass.ds(i - 1, 1), :].partition_broadcast(P)).then_inc(self.gate_landed[j], 16)
                            items(sp, 1, load)
                            if prefetch:
                                for n in range(1, RING + 1):
                                    sp.wait_ge(s["down_low"], NE - RING + n + 1)
                                    prefetch(sp, n % RING)
                            if final:
                                for r in range(REQ):
                                    sp.wait_ge(norm.done[r], 2 - r)
                                    store(sp, y_out[r][0], X[:, r, :])
                                sp.wait_ge(s_out, n_out[0])

                        @block.scalar
                        def _(act):
                            split_up_high(act, 0, 0)
                            act.wait_ge(s["router_landed"], 32)
                            act.activation(rwh[:, :, :], rw[:, :, :], ACT.Copy).then_inc(s["router_high"], 1)
                            mod.scalar(act)
                            split_up_high(act, 0, 1)
                            split_down_high(act, 0, 0)
                            act.wait_ge(s["router_multiplied"], 1)
                            act.activation(scT[:, :], PS[0:NE, 2, 0:REQ * TOK], ACT.Sigmoid).then_inc(s["router_scores"], 1)

                            def item(it, j, first=False, last=False):
                                i = it * RING + j
                                if not last and not first:
                                    split_up_high(act, *following(it, j))
                                act.wait_ge(s["up_multiplied"], i + 1)
                                wait(act, s["product"], i - 1)
                                act.activation(sg[j % 2][:, :], PS[:, j % 2, 0:REQ * TOK], ACT.Silu).then_inc(s["silu"], 1)
                                if not last:
                                    split_down_high(act, *following(it, j))
                            item(0, 0, first=True)
                            act.wait_ge(s["gates_turned"], 1)
                            act.activation(gT[:, :], PS[0:NE, 2, 0:REQ * TOK], ACT.Copy).then_inc(s["gatesT"], 1)
                            for j in range(1, RING):
                                item(0, j)
                            with act.Fori(1, 1 + GRPS) as it:
                                for j in range(RING):
                                    item(it, j)
                            item(1 + GRPS, 0, last=True)
                            norm.scalar(act)

                        @block.gpsimd
                        def _(pool):
                            norm.gpsimd(pool)

                        @block.vector
                        def _(dve):
                            split_up_low(dve, 0, 0)
                            dve.wait_ge(s["router_high"], 1)
                            dve.tensor_tensor(rwl[:, :, :], rw[:, :, :], rwh[:, :, :].bitcast(F32), ALU.subtract).then_inc(s["router_low"], 1)
                            mod.vector(dve)
                            split_up_low(dve, 0, 1)
                            split_down_low(dve, 0, 0)
                            dve.wait_ge(s["scores_turned"], 1)
                            dve_step(dve, dve.tensor_tensor(sel[:, :, :], sc[:, :, :], rb[:, :].unsqueeze(1).to_broadcast([P, REQ, NE]), ALU.add))
                            for r in range(REQ):
                                dve_step(dve, dve.max(m8[:, r, :], sel[:, r, :]))
                                dve_step(dve, dve.max_index(i8[:, r, :], m8[:, r, :], sel[:, r, :]))
                            dve_step(dve, dve.tensor_copy(f8[:, :, :], i8[:, :, :]))
                            for r in range(REQ):
                                dve_step(dve, dve.tensor_scalar(mask[:, r, :], table[:, T_IO:T_MK], f8[:, r, 0:1], None, ALU.is_equal))
                                for j in range(1, TOPK):
                                    dve_step(dve, dve.scalar_tensor_tensor(mask[:, r, :], table[:, T_IO:T_MK], f8[:, r, j:j + 1], mask[:, r, :],
                                                                           ALU.is_equal, ALU.add))
                            dve_step(dve, dve.tensor_tensor(gt[:, :, :], mask[:, :, :], sc[:, :, :], ALU.mult))
                            dve_step(dve, dve.tensor_reduce(sm[:, :, 0], gt[:, :, :], AX_X, ALU.add))
                            dve_step(dve, dve.reciprocal(sm[:, :, 1], sm[:, :, 0]))
                            for r in range(REQ):
                                i = dve.tensor_scalar(gt[:, r, :], gt[:, r, :], sm[:, r, 1:2], ROUTED, ALU.mult, ALU.mult)
                                i.then_inc(s["gates"], 1)

                            def item(it, j, last=False, shared=False):
                                i = it * RING + j
                                b = j % 2
                                if not last and not shared:
                                    split_up_low(dve, *following(it, j))
                                dve.wait_ge(s["silu"], i + 1)
                                wait(dve, s["hidden_low"], i - 1)
                                up = PS[:, b, REQ * TOK:2 * REQ * TOK]
                                if shared:
                                    dve.tensor_tensor(hg[b][:, :], sg[b][:, :], up, ALU.mult).then_inc(s["product"], 1)
                                    dve.wait_ge(s["product"], 1)
                                else:
                                    dve.tensor_tensor(pr[b][:, :], sg[b][:, :], up, ALU.mult).then_inc(s["product"], 1)
                                    dve.wait_ge(s["product"], i + 1)
                                    dve.wait_ge(self.gate_landed[j], it * 16 + (16 if j else 0))
                                    dve.tensor_tensor(hg[b][:, :], pr[b][:, :], gb[j][:, :], ALU.mult).then_inc(s["gated"], 1)
                                    dve.wait_ge(s["gated"], i)
                                wait(dve, s["down_multiplied"], i - 1)
                                dve.tensor_copy(hh[b][:, :], hg[b][:, :]).then_inc(s["hidden_high"], 1)
                                dve.wait_ge(s["hidden_high"], i + 1)
                                dve.tensor_tensor(hl[b][:, :], hg[b][:, :], hh[b][:, :].bitcast(F32), ALU.subtract).then_inc(s["hidden_low"], 1)
                                if not last:
                                    split_down_low(dve, *following(it, j))
                            for j in range(RING):
                                item(0, j, shared=(j == 0))
                            with dve.Fori(1, 1 + GRPS) as it:
                                for j in range(RING):
                                    item(it, j)
                            item(1 + GRPS, 0, last=True)
                            norm.vector(dve)

                        @block.tensor
                        def _(pe):
                            mod.tensor(pe)
                            pe.wait_ge(mod.lo, 2)
                            pe.wait_ge(s["router_low"], 1)
                            for k in range(KD):
                                mm = three(pe, PS[0:NE, 2, 0:REQ * TOK], rwh[:, k, :], rwl[:, k, :], mod.h[:, k, :], mod.l[:, k, :],
                                           start=(k == 0), stop=(k == KD - 1))
                            mm.then_inc(s["router_multiplied"], 1)

                            def turn_scores():
                                pe.wait_ge(s["router_scores"], 1)
                                for r in range(REQ):
                                    mm = pe.transpose(PS[:, 3, r * NE:(r + 1) * NE], scT[:, r * TOK:(r + 1) * TOK], ident[0:NE, 0:NE])
                                mm.then_inc(s["scores_turned"], 1)

                            def up(it, j, between=None):
                                i = it * RING + j
                                b = j % 2
                                pe.wait_ge(s["up_low"], i + 1)
                                wait(pe, s["product"], i - 1)
                                for a in range(2):
                                    if a and between:
                                        between()
                                    for k in range(KD):
                                        mm = three(pe, PS[:, b, a * REQ * TOK:(a + 1) * REQ * TOK], uh[b][:, a, k, :], ul[b][:, a, k, :],
                                                   mod.h[:, k, :], mod.l[:, k, :], start=(k == 0), stop=(k == KD - 1))
                                mm.then_inc(s["up_multiplied"], 1)

                            def down(it, j, first=False, last=False):
                                i = it * RING + j
                                b = j % 2
                                pe.wait_ge(s["hidden_low"], i + 1)
                                pe.wait_ge(s["down_low"], i + 1)
                                for r in range(REQ):
                                    at = slice(r * TOK, r * TOK + TOK)
                                    for c in range(2):
                                        cols = slice(c * 512, c * 512 + 512)
                                        mm = three(pe, PS[:, 4 + 2 * r + c, :], hh[b][:, at], hl[b][:, at], dh[b][:, cols], dl[b][:, cols],
                                                   start=first, stop=last)
                                    if last and r == 0:
                                        mm.then_inc(s["first_request_done"], 1)
                                mm.then_inc(s["down_multiplied"], 1)
                            up(0, 0, between=turn_scores)
                            up(0, 1)
                            down(0, 0, first=True)
                            pe.wait_ge(s["gates"], 2)
                            for r in range(REQ):
                                mm = pe.transpose(PS[0:NE, 2, r * TOK:(r + 1) * TOK], gt[:, r, :], ident)
                            mm.then_inc(s["gates_turned"], 1)
                            for j in range(2, RING):
                                up(0, j)
                                down(0, j - 1)
                            with pe.Fori(1, 1 + GRPS) as it:
                                for j in range(RING):
                                    up(it, j)
                                    if j:
                                        down(it, j - 1)
                                    else:
                                        down(it - 1, RING - 1)
                            up(1 + GRPS, 0)
                            down(GRPS, RING - 1)
                            down(1 + GRPS, 0, last=True)

        NS = 2 * G5
        RJ = REQ * NC5
        TG = 8
        UNITS = [(tile, d) for tile in range(G5 // TG) for d in range(2)]
        swap = table[:, T_SW:T_SW + P]
        u_d = nc.dram_tensor("u_saved", [P, KD * CH * RJ], F32, kind="Internal").ap()

        def run_layer1():
            with ExitStack() as outer:
                w_in = LateProject("w_in_c", t["w_in_c"][0], 256, 4, None, None, None, None)
                w_out = LateProject("w_out_c", t["w_out_c"][0], 256, 8,
                                    lambda b, r: PS[:, 4 * r + b // 2, b % 2 * 256:b % 2 * 256 + 256], None, None, None)
                w_out.view = t["w_out_c"][0].rearrange("(k p) n -> p k n", p=P)
                ada(1, lambda sp, j: w_in.load(sp, j))
                PW = sb("powers", [P, 12, 2, NS], F32, outer)
                X0 = sb("s5_start", [P, P], F32, outer)
                u_stored = sem("u_stored")
                b_landed, c_landed = sem("s5_b_landed"), sem("s5_c_landed")
                pw_ready = sem("powers_ready")
                Braw = raw[0][:, 0:2048].rearrange("n (i p c) -> n i p c", i=2, c=C5)
                Craw = raw[1][:, 0:2048].rearrange("n (i c p) -> n i c p", i=2, c=C5)
                U = [raw[i][:, 2048:3072].rearrange("p (g n) -> p g n", g=G5 // 2) for i in range(2)]

                with ExitStack() as scope:
                    mod = Modulate("mix1_mod", 0, scope)
                    w_in.alloc(scope)
                    uT = sb("uT", [P, KD, CH, RJ], F32, scope)
                    q = sb("s5_pre", [P, 24, P5], F32, scope)
                    q2 = sb("s5_twice", [P, 6, 2, P5], F32, scope)
                    x0s = sb("s5_start_turned", [P, 3, NS], F32, scope)
                    ldt = sb("s5_log_dt_sb", [P, 2], F32, scope)
                    sraw = sb("s5_state_raw", [G5, 2, 2, P5], F32, scope)
                    lam_landed, st_landed = sem("lambda_landed"), sem("state_landed")
                    dt_e, angles, exps, sins = sem("dt_ready"), sem("angles_ready"), sem("magnitudes_ready"), sem("sines_ready")
                    pre = sem("discretised")
                    turned, s6_ready = sem("s5_params_turned"), sem("s5_params_ready")
                    V = sb("u_rows", [RJ, G5, CC], F32, scope)
                    v_mm, v_ready = sem("u_rows_turned"), [sem("u_rows_act"), sem("u_rows_dve")]
                    u_mm, u_ready = sem("u_chunks_turned"), [sem("u_chunks_act"), sem("u_chunks_dve")]

                    def u_copies(eng, me):
                        copy = (lambda o, i: eng.activation(o, i, ACT.Copy)) if me == 0 else eng.tensor_copy
                        for k in range(KD):
                            f = 2 * k + me
                            eng.wait_ge(v_mm, f + 1)
                            copy(V[:, 8 * k:8 * k + 8, me * 64:me * 64 + 64].rearrange("n g (s c) -> n s g c", s=4),
                                 PS[0:RJ, f % 4, :].rearrange("n (s g c) -> n s g c", s=4, g=8)).then_inc(v_ready[me], 1)
                            if k and (k - 1) % 2 == me:
                                chunk_copy(eng, copy, k - 1, me)
                        if me == (KD - 1) % 2:
                            chunk_copy(eng, copy, KD - 1, me)

                    def chunk_copy(eng, copy, k, me):
                        eng.wait_ge(u_mm, k + 1)
                        copy(U[k // 4][:, k % 4 * 8:k % 4 * 8 + 8, :], PS[:, 4 + k % 4, 0:8 * RJ].rearrange("p (g n) -> p g n", g=8)).then_inc(u_ready[me], 1)
                    pt_tmp = sb("s5_pt", [P, 4, 2, NS], F32, scope)

                    def evac(eng, b, a):
                        i = 2 * b + a
                        src = PS[:, i, 0:REQ * TOK].rearrange("p (r j s) -> p s r j", r=REQ, s=CH)
                        dst = uT[:, i, :, :].rearrange("p s (r j) -> p s r j", r=REQ)
                        return eng.activation(dst, src, ACT.Copy) if a == 0 else eng.tensor_copy(dst, src)
                    w_in.evac = evac
                    with nc.Block() as block:
                        @block.sync
                        def _(sp):
                            sp.dma_start(q[:, 0, :], t["s5_lam_re"][0].rearrange("d g p -> (d g) p")).then_inc(lam_landed, 16)
                            sp.dma_start(q[:, 1, :], t["s5_lam_im"][0].rearrange("d g p -> (d g) p")).then_inc(lam_landed, 16)
                            sp.dma_start(ldt[:, 0:1], t["s5_log_dt"][0].rearrange("d (g o) -> (d g) o", o=1)).then_inc(lam_landed, 16)
                            for d in range(2):
                                sp.dma_start(sraw[:, d, :, :], t["state_ssm"][0, 0, d].rearrange("i g p -> g i p")).then_inc(st_landed, 16)
                            sp.wait_ge(w_in.lo, 1)
                            for i, key in enumerate(("s5_b_re", "s5_b_im")):
                                sp.dma_start(Braw[:, i, :, :], t[key][0].rearrange("d g p c -> (d g) p c")).then_inc(b_landed, 16)
                            sp.wait_ge(w_in.lo, 2)
                            for i, key in enumerate(("s5_c_re", "s5_c_im")):
                                sp.dma_start(Craw[:, i, :, :], t[key][0].rearrange("d g c p -> (d g) c p")).then_inc(c_landed, 16)
                            sp.wait_ge(w_in.ready[0], 4)
                            sp.wait_ge(w_in.ready[1], 4)
                            sp.dma_start(u_d, uT[:, :, :, :].rearrange("p k s n -> p (k s n)")).then_inc(u_stored, 16)
                            sp.wait_ge(u_stored, 16)

                        @block.tensor
                        def _(pe):
                            mod.tensor(pe)
                            pe.wait_ge(mod.lo, 2)
                            for b in range(4):
                                pe.wait_ge(w_in.lo, b + 1)
                                for a in range(2):
                                    for k in range(KD):
                                        at = slice(a * P, a * P + P)
                                        mm = three(pe, PS[:, 2 * b + a, 0:REQ * TOK], w_in.wh[b % 2][:, k, at], w_in.wl[b % 2][:, k, at],
                                                   mod.h[:, k, :], mod.l[:, k, :], start=(k == 0), stop=(k == KD - 1))
                                    mm.then_inc(w_in.mm, 1)
                            pe.wait_ge(w_in.ready[0], 4)
                            pe.wait_ge(w_in.ready[1], 4)

                            def rows(f):
                                wait(pe, v_ready[f % 2], f // 2 - 1)
                                for i in range(4):
                                    mm = pe.transpose(PS[0:RJ, f % 4, i * P:i * P + P], uT[:, f // 2, f % 2 * 4 + i, :], ident)
                                mm.then_inc(v_mm, 1)

                            def columns(k):
                                pe.wait_ge(v_ready[0], k + 1)
                                pe.wait_ge(v_ready[1], k + 1)
                                if k >= 4:
                                    pe.wait_ge(u_ready[k % 2], k // 2 - 1)
                                for g in range(8):
                                    mm = pe.transpose(PS[:, 4 + k % 4, g * RJ:(g + 1) * RJ], V[:, 8 * k + g, :], ident[0:RJ, 0:RJ])
                                mm.then_inc(u_mm, 1)
                            for k in range(KD):
                                rows(2 * k)
                                rows(2 * k + 1)
                                if k:
                                    columns(k - 1)
                            columns(KD - 1)
                            pe.wait_ge(v_ready[0], KD)
                            pe.wait_ge(v_ready[1], KD)
                            pe.wait_ge(pre, 1)
                            for i in range(6):
                                mm = pe.transpose(PS[:, i // 4, i % 4 * NS:(i % 4 + 1) * NS], q2[:, i, :, :].rearrange("n a p -> n (a p)"), ident)
                            mm.then_inc(turned, 1)
                            pe.wait_ge(st_landed, 32)
                            for d in range(2):
                                mm = pe.transpose(PS[:, 2, d * G5:(d + 1) * G5], sraw[:, d, :, :].rearrange("g i p -> g (i p)"), ident[0:G5, 0:G5])
                            mm.then_inc(turned, 1)
                            pe.wait_ge(s6_ready, 1)
                            pe.matmul(PS[:, 3, 0:NS], swap, x0s[:, 0, :], start=True, stop=True).then_inc(turned, 1)

                        @block.scalar
                        def _(act):
                            mod.scalar(act)
                            w_in.scalar(act)
                            act.wait_ge(w_in.ready[0], 4)
                            u_copies(act, 0)
                            act.wait_ge(u_ready[0], KD // 2)
                            act.wait_ge(lam_landed, 48)
                            act.activation(ldt[:, 1:2], ldt[:, 0:1], ACT.Exp).then_inc(dt_e, 1)
                            act.wait_ge(angles, 1)
                            act.activation(q[:, 4, :], q[:, 2, :], ACT.Exp).then_inc(exps, 1)
                            act.activation(q[:, 5, :], q[:, 2, :], ACT.Exp, scale=-1.0).then_inc(exps, 1)
                            act.wait_ge(angles, 2)
                            act.activation(q[:, 8, :], q[:, 6, :], ACT.Sin).then_inc(sins, 1)
                            act.activation(q[:, 9, :], q[:, 7, :], ACT.Sin).then_inc(sins, 1)
                            act.wait_ge(turned, 2)
                            act.activation(x0s[:, 0, :], PS[:, 2, 0:NS], ACT.Copy).then_inc(s6_ready, 1)
                            act.wait_ge(s6_ready, 1)

                        @block.vector
                        def _(dve):
                            mod.vector(dve)
                            w_in.vector(dve)
                            u_copies(dve, 1)
                            dve.wait_ge(u_ready[1], KD // 2)
                            S = lambda i: q[:, i, :]
                            step = lambda ins: dve_step(dve, ins)
                            dve.wait_ge(dt_e, 1)
                            dve.tensor_scalar(S(2), S(0), ldt[:, 1:2], None, ALU.mult)
                            i = dve.tensor_scalar(S(3), S(1), ldt[:, 1:2], None, ALU.mult)
                            i.then_inc(angles, 1)
                            dve.wait_ge(angles, 1)
                            BIG, C1 = 12582912.0, 6.28125
                            C2 = 2 * math.pi - C1
                            PI = 3.1415925
                            step(dve.tensor_scalar(S(10), S(3), 1 / (2 * math.pi), BIG, ALU.mult, ALU.add))
                            step(dve.tensor_scalar(S(11), S(10), -BIG, None, ALU.add))
                            step(dve.scalar_tensor_tensor(S(10), S(11), -C1, S(3), ALU.mult, ALU.add))
                            step(dve.scalar_tensor_tensor(S(12), S(11), -C2, S(10), ALU.mult, ALU.add))
                            step(dve.tensor_scalar(S(6), S(12), PI, -PI, ALU.min, ALU.max))
                            step(dve.tensor_scalar(S(13), S(6), math.pi / 2, None, ALU.add))
                            step(dve.tensor_scalar(S(14), S(13), PI, -2 * math.pi, ALU.is_gt, ALU.mult))
                            step(dve.tensor_tensor(S(15), S(13), S(14), ALU.add))
                            dve.tensor_scalar(S(7), S(15), PI, -PI, ALU.min, ALU.max).then_inc(angles, 1)
                            dve.wait_ge(sins, 2)
                            dve.wait_ge(exps, 2)
                            dve.tensor_tensor(S(18), S(4), S(9), ALU.mult)
                            dve.tensor_tensor(S(19), S(4), S(8), ALU.mult)
                            dve.tensor_tensor(S(20), S(5), S(9), ALU.mult)
                            step(dve.scalar_tensor_tensor(S(21), S(8), -1.0, S(5), ALU.mult, ALU.mult))
                            dve.tensor_scalar(S(10), S(18), -1.0, None, ALU.add)
                            dve.tensor_tensor(S(11), S(0), S(0), ALU.mult)
                            step(dve.tensor_tensor(S(12), S(1), S(1), ALU.mult))
                            step(dve.tensor_tensor(S(13), S(11), S(12), ALU.add))
                            dve.reciprocal(S(14), S(13))
                            dve.tensor_tensor(S(15), S(10), S(0), ALU.mult)
                            dve.tensor_tensor(S(16), S(19), S(1), ALU.mult)
                            dve.tensor_tensor(S(17), S(19), S(0), ALU.mult)
                            step(dve.tensor_tensor(S(2), S(10), S(1), ALU.mult))
                            dve.tensor_tensor(S(12), S(15), S(16), ALU.add)
                            step(dve.tensor_tensor(S(13), S(17), S(2), ALU.subtract))
                            dve.tensor_tensor(S(22), S(12), S(14), ALU.mult)
                            step(dve.tensor_tensor(S(23), S(13), S(14), ALU.mult))
                            dve.tensor_copy(q2[:, :, 0, :], q[:, 18:24, :])
                            dve.tensor_copy(q2[:, :, 1, :], q[:, 18:24, :]).then_inc(pre, 1)
                            dve.wait_ge(turned, 1)

                            def cmul(dst, n, a, b):
                                br = PW[:, b, 0, :].unsqueeze(1).to_broadcast([P, n, NS])
                                bi = PW[:, b, 1, :].unsqueeze(1).to_broadcast([P, n, NS])
                                ar, ai = PW[:, a:a + n, 0, :], PW[:, a:a + n, 1, :]
                                T = [pt_tmp[:, i, 0:n, :] for i in range(4)]
                                dve.tensor_tensor(T[0], ar, br, ALU.mult)
                                dve.tensor_tensor(T[1], ai, bi, ALU.mult)
                                dve.tensor_tensor(T[2], ar, bi, ALU.mult)
                                step(dve.tensor_tensor(T[3], ai, br, ALU.mult))
                                dve.tensor_tensor(PW[:, dst:dst + n, 0, :], T[0], T[1], ALU.subtract)
                                step(dve.tensor_tensor(PW[:, dst:dst + n, 1, :], T[2], T[3], ALU.add))
                            dve.memset(PW[:, 4, 0, :], 1.0)
                            dve.memset(PW[:, 4, 1, :], 0.0)
                            dve.tensor_copy(PW[:, 5, :, :], PS[:, 0, 0:2 * NS].rearrange("p (i n) -> p i n", i=2))
                            dve.tensor_copy(PW[:, 3, :, :], PS[:, 0, 2 * NS:4 * NS].rearrange("p (i n) -> p i n", i=2))
                            step(dve.tensor_copy(PW[:, 11, :, :], PS[:, 1, 0:2 * NS].rearrange("p (i n) -> p i n", i=2)))
                            cmul(6, 1, 5, 5)
                            cmul(7, 2, 5, 6)
                            cmul(2, 1, 3, 3)
                            cmul(1, 1, 2, 3)
                            cmul(0, 1, 2, 2)
                            cmul(9, 1, 8, 5)
                            cmul(10, 1, 8, 8)
                            dve.wait_ge(turned, 3)
                            dve.wait_ge(s6_ready, 1)
                            dve.tensor_tensor(x0s[:, 1, :], x0s[:, 0, :], PW[:, 9, 0, :], ALU.mult)
                            step(dve.tensor_tensor(x0s[:, 2, :], PS[:, 3, 0:NS], PW[:, 9, 1, :], ALU.mult))
                            dve.tensor_tensor(X0[:, :], x0s[:, 1, :], x0s[:, 2, :], ALU.add).then_inc(pw_ready, 1)
                            dve.wait_ge(pw_ready, 1)

                with ExitStack() as scope:
                    F = sb("F", [P, 2, G5, CC], F32, scope)
                    E = sb("E", [P, 2, TG, CC], F32, scope)
                    ZX = sb("ZX", [P, 2, G5, REQ, NC5 + 1], F32, scope)
                    Et = sb("E_turned", [P, TG * P], F32, scope)
                    tmpE = sb("tmpE", [P, TG * CC], F32, scope)
                    tmpF = sb("tmpF", [P, TG * CC], F32, scope)
                    A = sb("scan_sums", [P, 3, 2, G5, REQ], F32, scope)
                    HS = sb("s5_end", [P, 2, G5], F32, scope)
                    HSt = sb("s5_end_t", [G5, 2, P], F32, scope)
                    cols = lambda ap: ap.rearrange("p (n c) -> p n c", n=NS)
                    flat = lambda ap: ap.rearrange("p n c -> p (n c)")
                    B2 = cols(raw[0][:, 0:2048])
                    Bb = cols(raw[1][:, 0:2048])
                    Ct = cols(raw[2][:, 0:2048])
                    C2 = cols(raw[3][:, 0:2048])
                    Ms = [raw[2 + i][:, 2048:3072] for i in range(2)]
                    Bs = cols(E[:, :, :, :].rearrange("p d g x -> p (d g x)"))
                    scr = cols(F[:, 1, G5 - 16:G5, :].rearrange("p g x -> p (g x)"))
                    c_turned, c_ready, bb, b_ready = sem("BC_turned"), sem("C_ready"), sem("B_step"), sem("B_ready")
                    swapped, bs_ready = sem("BC_swapped"), sem("B_columns_ready")
                    e_p, e_ready, f_p, f_ready = sem("E_step"), sem("E_ready"), sem("F_step"), sem("F_ready")
                    et_mm, et_ready = sem("E_turned_pe"), sem("E_turned_ready")
                    m_mm, m_ready = sem("M_multiplied"), sem("M_ready")
                    z_mm, z_ready, ym_mm = sem("z_multiplied"), sem("z_ready"), sem("y_inside_multiplied")
                    started = sem("scan_start_ready")
                    scan_a = [sem("scan_sum_forward"), sem("scan_sum_backward")]
                    scan_j = [sem("scan_swapped_forward"), sem("scan_swapped_backward")]
                    scanned = [sem("scan_forward_done"), sem("scan_backward_done")]
                    ends, end_t, end_s = sem("end_states"), sem("end_states_turned"), sem("end_states_sb")
                    y_mm = sem("y_multiplied")

                    def build_matrix(eng, s1, s2, tmp, out, v, base, other, slots):
                        tile, d = UNITS[v]
                        n0 = d * G5 + tile * TG
                        shape = [P, TG, CH, C5]
                        pr = PW[:, slots, 0, n0:n0 + TG].rearrange("p s n -> p n s").unsqueeze(3).to_broadcast(shape)
                        pi = PW[:, slots, 1, n0:n0 + TG].rearrange("p s n -> p n s").unsqueeze(3).to_broadcast(shape)
                        o = out.rearrange("p g (s c) -> p g s c", s=CH)
                        tm = tmp[:, :].rearrange("p (g s c) -> p g s c", g=TG, s=CH)
                        eng.tensor_tensor(o, base[:, n0:n0 + TG, :].unsqueeze(2).to_broadcast(shape), pr, ALU.mult)
                        eng.tensor_tensor(tm, other[:, n0:n0 + TG, :].unsqueeze(2).to_broadcast(shape), pi, ALU.mult).then_inc(s1, 1)
                        eng.wait_ge(s1, v + 1)
                        eng.tensor_tensor(out.rearrange("p g x -> p (g x)"), out.rearrange("p g x -> p (g x)"), tmp[:, :], ALU.add).then_inc(s2, 1)

                    def y_at(g):
                        return PS[:, g // 16, g % 16 * RJ:(g % 16 + 1) * RJ]

                    with nc.Block() as block:
                        @block.tensor
                        def _(pe):
                            pe.wait_ge(b_landed, 32)
                            pe.wait_ge(c_landed, 32)
                            for m in range(2):
                                for c in range(C5):
                                    for i in range(2):
                                        src = Craw[:, i, c, :] if m == 0 else Braw[:, i, :, c]
                                        mm = pe.matmul(PS[i * P5:(i + 1) * P5, (0 if m else 4) + c // 4, c % 4 * NS:(c % 4 + 1) * NS],
                                                       src, ident, start=True, stop=True)
                                mm.then_inc(c_turned, 1)
                            pe.wait_ge(c_ready, 2)
                            for b in range(4):
                                mm = pe.matmul(PS[:, 4 + b, :], swap, flat(Ct)[:, b * 512:(b + 1) * 512], start=True, stop=True)
                            mm.then_inc(swapped, 1)
                            pe.wait_ge(bs_ready, 1)
                            for b in range(4):
                                mm = pe.matmul(PS[:, b, :], swap, flat(Bs)[:, b * 512:(b + 1) * 512], start=True, stop=True)
                            mm.then_inc(swapped, 1)
                            pe.wait_ge(c_ready, 3)
                            pe.wait_ge(b_ready, 2)

                            def inside(v):
                                tile, d = UNITS[v]
                                for x in range(TG):
                                    g = tile * TG + x
                                    pe.wait_ge(m_ready, 2 * v + 1 + x // 4)
                                    mm = pe.matmul(y_at(g), Ms[v % 2][:, x * P:(x + 1) * P],
                                                   U[g // 32][:, g % 32, :], start=(d == 0 and g % 16 == 0), stop=False, skip_group_check=True)
                                mm.then_inc(ym_mm, 1)
                            for v, (tile, d) in enumerate(UNITS):
                                pe.wait_ge(e_ready, v + 1)
                                wait(pe, z_ready, v)
                                for x in range(TG):
                                    mm = pe.transpose(PS[:, 6 + x // 4, x % 4 * P:x % 4 * P + P], E[:, d, x, :], ident)
                                    if x % 4 == 3:
                                        mm.then_inc(et_mm, 1)
                                pe.wait_ge(f_ready, v + 1)
                                wait(pe, m_ready, 2 * v)
                                for x in range(TG):
                                    mm = pe.matmul(PS[:, 4 + x // 4, x % 4 * P:x % 4 * P + P], E[:, d, x, :],
                                                   F[:, d, tile * TG + x, :], start=True, stop=True)
                                    if x % 4 == 3:
                                        mm.then_inc(m_mm, 1)
                                pe.wait_ge(et_ready, 2 * v + 2)
                                for x in range(TG):
                                    g = tile * TG + x
                                    mm = pe.matmul(PS[:, 6, x * RJ:(x + 1) * RJ], Et[:, x * P:(x + 1) * P], U[g // 32][:, g % 32, :],
                                                   start=True, stop=True)
                                mm.then_inc(z_mm, 1)
                                if v:
                                    inside(v - 1)
                            inside(len(UNITS) - 1)
                            for j in range(NC5):
                                for d in range(2):
                                    pe.wait_ge(scan_a[d], j + 1)
                                    pe.matmul(PS[:, 6 + d, 0:G5 * REQ], swap, A[:, 0, d, :, :].rearrange("p g r -> p (g r)"),
                                              start=True, stop=True).then_inc(scan_j[d], 1)
                            for g in range(G5):
                                for d in range(2):
                                    pe.wait_ge(scanned[d], 1)
                                    mm = pe.matmul(y_at(g), F[:, d, g, :], ZX[:, d, g, :, d:d + NC5], start=False,
                                                   stop=(d == 1 and g % 16 == 15), skip_group_check=True)
                                if g % 16 == 15:
                                    mm.then_inc(y_mm, 1)
                            pe.wait_ge(ends, 2)
                            for d in range(2):
                                mm = pe.transpose(PS[0:G5, 7, d * P:(d + 1) * P], HS[:, d, :], ident)
                            mm.then_inc(end_t, 1)

                        @block.scalar
                        def _(act):
                            act.wait_ge(c_turned, 1)
                            for h, sign in ((0, 1.0), (1, -1.0)):
                                rows = slice(h * P5, (h + 1) * P5)
                                act.activation(Ct[rows, :, :], PS[rows, 4:8, :].rearrange("p b (c n) -> p n (b c)", n=NS), ACT.Copy, scale=sign).then_inc(c_ready, 1)
                            act.wait_ge(swapped, 1)
                            act.activation(flat(C2), PS[:, 4:8, :].rearrange("p b x -> p (b x)"), ACT.Copy, scale=-1.0).then_inc(c_ready, 1)
                            for v, (tile, d) in enumerate(UNITS):
                                for half in range(2):
                                    act.wait_ge(et_mm, 2 * v + half + 1)
                                    wait(act, z_mm, v)
                                    act.activation(Et[:, half * 512:half * 512 + 512], PS[:, 6 + half, :], ACT.Copy).then_inc(et_ready, 1)
                                act.wait_ge(z_mm, v + 1)
                                act.activation(ZX[:, d, tile * TG:(tile + 1) * TG, :, 1 - d:1 - d + NC5].rearrange("p g r j -> p (g r) j"),
                                               PS[:, 6, 0:TG * RJ].rearrange("p (n j) -> p n j", j=NC5), ACT.Copy).then_inc(z_ready, 1)
                            act.wait_ge(end_t, 1)
                            act.activation(HSt[:, :, :], PS[0:G5, 7, 0:2 * P].rearrange("g (d x) -> g d x", d=2), ACT.Copy).then_inc(end_s, 1)

                        @block.vector
                        def _(dve):
                            dve.wait_ge(c_turned, 2)
                            dve.tensor_copy(Bs, PS[:, 0:4, :].rearrange("p b (c n) -> p n (b c)", n=NS)).then_inc(bs_ready, 1)
                            cr = PW[:, 11, 0, :].unsqueeze(2).to_broadcast([P, NS, C5])
                            ci = PW[:, 11, 1, :].unsqueeze(2).to_broadcast([P, NS, C5])
                            Bp = cols(PS[:, 0:4, :].rearrange("p b x -> p (b x)"))
                            dve.wait_ge(bs_ready, 1)
                            dve.tensor_tensor(Bb, Bs, cr, ALU.mult)
                            dve.wait_ge(swapped, 2)
                            dve.tensor_tensor(scr, Bp, ci, ALU.mult).then_inc(bb, 1)
                            dve.tensor_tensor(B2, Bp, cr, ALU.mult)
                            dve.wait_ge(bb, 1)
                            dve.tensor_tensor(Bb, Bb, scr, ALU.add).then_inc(b_ready, 1)
                            dve.wait_ge(b_ready, 1)
                            dve.tensor_tensor(scr, Bs, ci, ALU.mult).then_inc(bb, 1)
                            dve.wait_ge(bb, 2)
                            dve.tensor_tensor(B2, B2, scr, ALU.subtract).then_inc(b_ready, 1)
                            dve.wait_ge(b_ready, 2)

                            def masked(v):
                                d = UNITS[v][1]
                                mk = table[:, T_MK + d * P:T_MK + (d + 1) * P].unsqueeze(1).to_broadcast([P, 4, P])
                                for half in range(2):
                                    dve.wait_ge(m_mm, 2 * v + half + 1)
                                    wait(dve, ym_mm, v - 1)
                                    dve.tensor_tensor(Ms[v % 2][:, half * 512:half * 512 + 512].rearrange("p (x q) -> p x q", x=4),
                                                      PS[:, 4 + half, :].rearrange("p (x q) -> p x q", x=4), mk, ALU.mult).then_inc(m_ready, 1)
                            for v, (tile, d) in enumerate(UNITS):
                                if v >= 2:
                                    dve.wait_ge(m_mm, 2 * (v - 1))
                                build_matrix(dve, e_p, e_ready, tmpE, E[:, d, :, :], v, Bb, B2, slice(8, 0, -1) if d == 0 else slice(1, 9))
                                dve.wait_ge(e_ready, v + 1)
                                if v:
                                    masked(v - 1)
                            masked(len(UNITS) - 1)
                            dve.wait_ge(z_ready, len(UNITS))
                            gr = lambda x: x.rearrange("p g r -> p (g r)")
                            slot = lambda d, j: ZX[:, d, :, :, j]
                            power = lambda m, i, d: PW[:, m, i, d * G5:(d + 1) * G5]
                            both = lambda ap: ap.unsqueeze(2).to_broadcast([P, G5, REQ])
                            for d in range(2):
                                x0 = slot(d, 0 if d == 0 else NC5)
                                dve.memset(x0[:, :, 0], 0.0)
                                i = dve.tensor_copy(x0[:, :, 1], X0[:, d * G5:(d + 1) * G5])
                            dve_step(dve, i)
                            for j in range(NC5):
                                last = j == NC5 - 1
                                for d in range(2):
                                    cur, nxt = (j, j + 1) if d == 0 else (NC5 - j, NC5 - j - 1)
                                    dve.tensor_tensor(gr(A[:, 0, d, :, :]), gr(slot(d, cur)), gr(slot(d, nxt)), ALU.add).then_inc(scan_a[d], 1)
                                for d in range(2):
                                    dve.wait_ge(scan_a[d], j + 1)
                                    if last:
                                        i = dve.tensor_tensor(A[:, 1, d, :, 0], A[:, 0, d, :, 0], power(7, 0, d), ALU.mult)
                                    else:
                                        i = dve.tensor_tensor(A[:, 1, d, :, :], A[:, 0, d, :, :], both(power(10, 0, d)), ALU.mult)
                                for d in range(2):
                                    nxt = j + 1 if d == 0 else NC5 - j - 1
                                    dve.wait_ge(scan_j[d], j + 1)
                                    pj = PS[:, 6 + d, 0:G5 * REQ].rearrange("p (g r) -> p g r", r=REQ)
                                    if last:
                                        dve_step(dve, dve.tensor_tensor(A[:, 2, d, :, 0], pj[:, :, 0], power(7, 1, d), ALU.mult))
                                        dve.tensor_tensor(HS[:, d, :], A[:, 1, d, :, 0], A[:, 2, d, :, 0], ALU.add).then_inc(ends, 1)
                                    else:
                                        dve_step(dve, dve.tensor_tensor(A[:, 2, d, :, :], pj, both(power(10, 1, d)), ALU.mult))
                                        i = dve.tensor_tensor(gr(slot(d, nxt)), gr(A[:, 1, d, :, :]), gr(A[:, 2, d, :, :]), ALU.add)
                                        if j == NC5 - 2:
                                            i.then_inc(scanned[d], 1)
                                            dve.wait_ge(scanned[d], 1)
                                        else:
                                            dve_step(dve, i)

                        @block.gpsimd
                        def _(pool):
                            pool.wait_ge(c_ready, 3)
                            for v, (tile, d) in enumerate(UNITS):
                                if v == len(UNITS) - 4:
                                    pool.wait_ge(b_ready, 2)
                                build_matrix(pool, f_p, f_ready, tmpF, F[:, d, tile * TG:(tile + 1) * TG, :], v, Ct, C2,
                                             slice(0, 8) if d == 0 else slice(7, None, -1))
                                pool.wait_ge(f_ready, v + 1)

                        @block.sync
                        def _(sp):
                            sp.wait_ge(end_s, 1)
                            store(sp, ssm_out[0, 0].rearrange("d i g p -> g d i p"), HSt[:, :, :].rearrange("g d (i p) -> g d i p", i=2))
                            for j in range(RING):
                                w_out.load(sp, j)
                            sp.wait_ge(y_mm, 4)

                Yt = sb("Yt", [P, KD, CH, RJ], F32, outer)
                with ExitStack() as scope:
                    Ys = sb("y_columns", [P, 4, 16, RJ], F32, scope)
                    V = sb("y_rows", [RJ, CH, D], F32, scope)
                    uT = sb("uT_again", [P, KD, CH, RJ], F32, scope)
                    dcol = sb("s5_d_col", [P, KD], F32, scope)
                    back, ys = sem("u_back_landed"), [sem("y_columns_act"), sem("y_columns_dve")]
                    v_mm, v_ready = sem("y_rows_turned"), [sem("y_rows_act"), sem("y_rows_dve")]
                    y_mm2, y_done = sem("y_channels_turned"), sem("y_plus_du")

                    def y_copies(eng, me):
                        copy = (lambda o, i: eng.activation(o, i, ACT.Copy)) if me == 0 else eng.tensor_copy
                        for b in range(me, 4, 2):
                            copy(Ys[:, b, :, :], PS[:, b, :].rearrange("p (n x) -> p n x", n=16)).then_inc(ys[me], 1)
                        for f in range(me, 16, 2):
                            eng.wait_ge(v_mm, f + 1)
                            copy(V[:, :, 64 * f:64 * f + 64].rearrange("n s (g c) -> n g s c", g=4),
                                 PS[0:RJ, 4 + f % 4, :].rearrange("n (g s c) -> n g s c", g=4, s=CH)).then_inc(v_ready[me], 1)
                    with nc.Block() as block:
                        @block.sync
                        def _(sp):
                            sp.dma_start(uT[:, :, :, :].rearrange("p k s n -> p (k s n)"), u_d).then_inc(back, 16)
                            sp.dma_start(dcol[:, :], t["s5_d"][0].rearrange("(k p) -> p k", p=P), allow_slow_non_contiguous=True).then_inc(back, 16)

                        @block.tensor
                        def _(pe):
                            pe.wait_ge(ys[0], 2)
                            pe.wait_ge(ys[1], 2)
                            for f in range(16):
                                wait(pe, v_ready[f % 2], f // 2 - 1)
                                for i in range(4):
                                    g = 4 * f + i
                                    mm = pe.transpose(PS[0:RJ, 4 + f % 4, i * P:i * P + P], Ys[:, g // 16, g % 16, :], ident)
                                mm.then_inc(v_mm, 1)
                            for k in range(KD):
                                for e in range(2):
                                    pe.wait_ge(v_ready[e], k + 1)
                                wait(pe, y_done, k - 3)
                                for s in range(CH):
                                    mm = pe.transpose(PS[:, k % 4, s * RJ:(s + 1) * RJ], V[:, s, k * P:(k + 1) * P], ident[0:RJ, 0:RJ])
                                mm.then_inc(y_mm2, 1)

                        @block.scalar
                        def _(act):
                            y_copies(act, 0)
                            act.wait_ge(v_ready[0], 8)

                        @block.vector
                        def _(dve):
                            y_copies(dve, 1)
                            dve.wait_ge(back, 32)
                            for k in range(KD):
                                dve.wait_ge(y_mm2, k + 1)
                                dve.scalar_tensor_tensor(Yt[:, k, :, :].rearrange("p s n -> p (s n)"), uT[:, k, :, :].rearrange("p s n -> p (s n)"),
                                                         dcol[:, k:k + 1], PS[:, k % 4, 0:CH * RJ], ALU.mult, ALU.add).then_inc(y_done, 1)
                            dve.wait_ge(y_done, KD)

                with ExitStack() as scope:
                    Gf = sb("gelu", [P, KD, REQ * TOK], F32, scope)
                    Gh = sb("gelu_h", [P, KD, REQ * TOK], F32R, scope)
                    Gl = sb("gelu_l", [P, KD, REQ * TOK], F32R, scope)
                    w_out.lh, w_out.ll = Gh, Gl
                    w_out.alloc(scope)
                    sig = Gf[:, :, :].rearrange("p k t -> p (k t)").rearrange("p (r n) -> p r n", r=REQ)
                    gelu, g_hi, g_lo = sem("gelu_ready"), sem("gelu_high"), sem("gelu_low")
                    sigm, glu = sem("gate_sigmoid"), sem("glu_ready")
                    norm = Norm("ln_mix1", 1, 0, [0, 1, 4, 5], lambda e, r: e.wait_ge(glu, 2 * r + 2), scope, t["ln_mix_g"][1:2, :], t["ln_mix_b"][1:2, :])
                    glu_sb = Yt[:, :, :, :].rearrange("p k s n -> p (k s n)").rearrange("p (r n) -> p r n", r=REQ)
                    norm.source = lambda r, n: glu_sb[:, r, n * 512:n * 512 + 512]
                    with nc.Block() as block:
                        @block.sync
                        def _(sp):
                            norm.sync(sp)
                            w_out.sync(sp)
                            for j in range(RING):
                                sp.wait_ge(w_out.lo, 5 + j)
                                moes[1].load_weights(sp, 0, j)

                        @block.tensor
                        def _(pe):
                            pe.wait_ge(g_lo, 2)
                            w_out.tensor(pe)

                        @block.scalar
                        def _(act):
                            for k in range(KD):
                                act.activation(Gf[:, k, :].rearrange("p (r j s) -> p s r j", r=REQ, s=CH),
                                               Yt[:, k, :, :].rearrange("p s (r j) -> p s r j", r=REQ), ACT.Gelu_apprx_tanh).then_inc(gelu, 1)
                            for half in range(2):
                                act.wait_ge(gelu, 4 * half + 4)
                                act.activation(Gh[:, 4 * half:4 * half + 4, :], Gf[:, 4 * half:4 * half + 4, :], ACT.Copy).then_inc(g_hi, 1)
                            w_out.scalar(act)
                            act.wait_ge(w_out.mm, 16)
                            act.wait_ge(g_lo, 2)
                            for r in range(REQ):
                                for n in range(2):
                                    act.activation(sig[:, r, n * 512:n * 512 + 512], PS[:, 4 * r + 2 + n, :], ACT.Sigmoid).then_inc(sigm, 1)
                            norm.scalar(act)

                        @block.gpsimd
                        def _(pool):
                            norm.gpsimd(pool)

                        @block.vector
                        def _(dve):
                            for half in range(2):
                                dve.wait_ge(g_hi, half + 1)
                                at = slice(4 * half, 4 * half + 4)
                                dve.tensor_tensor(Gl[:, at, :], Gf[:, at, :], Gh[:, at, :].bitcast(F32), ALU.subtract).then_inc(g_lo, 1)
                            w_out.vector(dve)
                            for r in range(REQ):
                                for n in range(2):
                                    dve.wait_ge(sigm, 2 * r + n + 1)
                                    dve.tensor_tensor(glu_sb[:, r, n * 512:n * 512 + 512], PS[:, 4 * r + n, :], sig[:, r, n * 512:n * 512 + 512],
                                                      ALU.mult).then_inc(glu, 1)
                            norm.vector(dve)

        moes = [Moe(0)]
        run_layer0()
        if LAYERS == 1:
            moes[0].run(None, True)
        else:
            moes[0].run(lambda sp, j: ada_load(sp, 1, 0, j), False)
            nc.clear_and_free_semaphores(layer_sems)
            nc.all_engine_barrier()
            moes.append(Moe(1))
            run_layer1()
            moes[1].run(None, True)


_INS = ['x_prompt', 'x_sample', 'c', 'cache_attn_k', 'cache_attn_v', 'cache_mla_ckv', 'cache_mla_krope', 'state_ssm', 'c_ctx',
        'ada_w', 'ada_b', 'ln_mix_g', 'ln_mix_b', 'ln_ffn_g', 'ln_ffn_b', 'w_in_ab', 'attn_sink', 'mla_q_norm', 'mla_kv_norm',
        'mla_w_uq', 'mla_w_ukv', 'w_out_ab', 'w_in_c', 's5_lam_re', 's5_lam_im', 's5_log_dt', 's5_b_re', 's5_b_im', 's5_c_re',
        's5_c_im', 's5_d', 'w_out_c', 'router_w', 'router_bias', 'exp_w_gate', 'exp_w_up', 'exp_w_down', 'sh_w_gate', 'sh_w_up',
        'sh_w_down']
_OUTS = [(1, 128, 1024), (1, 128, 1024), (1, 1, 128, 2, 64), (1, 1, 128, 2, 64), (1, 1, 128, 128), (1, 1, 128, 32), (1, 1, 2, 2, 64, 64)]


def kernel(**inputs):
    import concourse.bacc as bacc
    from concourse.bass_utils import run_bass_kernel_spmd

    nc = bacc.Bacc("TRN2", target_bir_lowering=False, num_devices=1)
    arrays, aps = {}, {}
    given = {name: inputs[name] for name in _INS}
    given["table"], given["pick"] = shape_constants()
    for name, value in given.items():
        a = np.ascontiguousarray(value)
        arrays[f"in_{name}"] = a
        aps[name] = nc.dram_tensor(f"in_{name}", a.shape, mybir.dt.from_np(a.dtype), kind="ExternalInput").ap()
    n_outs = 7 if LAYERS == 2 else 6
    outs = [nc.dram_tensor(f"out_{i}", shape, F32, kind="ExternalOutput").ap() for i, shape in enumerate(_OUTS[:n_outs])]
    build(nc, aps, outs + [None] * (7 - n_outs))
    r = run_bass_kernel_spmd(nc, [arrays], core_ids=[0])
    return tuple(r.results[0][f"out_{i}"] for i in range(n_outs))
```

```python
import math
from contextlib import ExitStack

import numpy as np

import concourse.bass as bass
from concourse import mybir

F32 = mybir.dt.float32
F32R = mybir.dt.float32r
U32 = mybir.dt.uint32
ALU = mybir.AluOpType
ACT = mybir.ActivationFunctionType
AX_X = mybir.AxisListType.X

P = 128
D = 1024
KD = D // P
TOK = 128
REQ = 2
DEPTH = 2
H, KV, HD = 8, 2, 64
GRP = H // KV
RQ, RKV, NOPE, ROPE, VD = 256, 128, 64, 32, 64
QK = NOPE + ROPE
A_Q, A_K, A_V = 0, H * HD, (H + KV) * HD
A_CQ = (H + 2 * KV) * HD
A_CKV = A_CQ + RQ
A_KR = A_CKV + RKV
W_AB = A_KR + ROPE
SC_A = HD ** -0.5
SC_M = QK ** -0.5
NE, TOPK, FF = 64, 6, 128
ROUTED = 2.5
ALPHA = (2.0 * DEPTH) ** 0.25
LN_EPS, RMS_EPS = 1e-5, 1e-6
RING = 4
SLOT = 3 * KD * FF
NADA = 24
GRID_W, ROPE_BASE = 64, 10000.0

G5, C5, P5 = 64, 16, 64
CH = 8
NC5 = TOK // CH
CC = CH * C5


def wait(eng, sem, value):
    if not isinstance(value, int) or value > 0:
        eng.wait_ge(sem, value)


def shape_constants():
    ident = np.eye(P, dtype=np.float32)
    pick = np.zeros((4, 2 + 2 * P), np.float32)
    for row in range(4):
        pick[row, row % 2] = 1.0
        pick[row, 2 + P * (row % 2):2 + P * (row % 2) + P] = 1.0
    tok = np.arange(TOK)
    pos = np.stack([tok // GRID_W, tok % GRID_W], 1).astype(np.float32)

    def rope(width):
        quarter = width // 4
        inv = (np.float32(ROPE_BASE) ** (-np.arange(quarter, dtype=np.float32) / np.float32(quarter))).astype(np.float32)
        ang = (pos[:, :, None] * inv[None, None, :]).astype(np.float32)
        return np.stack([np.cos(ang), np.sin(ang)], 1).astype(np.float32).reshape(TOK, -1)

    table = np.concatenate([ident, rope(HD), rope(ROPE), np.tile(np.arange(NE, dtype=np.float32), (P, 1))], 1)
    step = np.arange(P) // C5
    later = (step[None, :] >= step[:, None]).astype(np.float32)
    masks = np.stack([later, later.T], 1).reshape(P, 2 * P)
    half = P // 2
    swap = np.zeros((P, P), np.float32)
    swap[np.arange(half) + half, np.arange(half)] = -1.0
    swap[np.arange(half), np.arange(half) + half] = 1.0
    return (np.ascontiguousarray(np.concatenate([table, masks, swap], 1)), np.ascontiguousarray(pick))


T_ID = 0
T_RA = P
T_RM = T_RA + HD
T_IO = T_RM + ROPE
T_MK = T_IO + NE
T_SW = T_MK + 2 * P
T_W = T_SW + P


def build(nc, t, outs):
    y_out = outs[0:2]
    k_out, v_out, ckv_out, kr_out, ssm_out = outs[2:7]

    top = ExitStack()
    with top:
        def sb(name, shape, dt=F32, scope=top):
            return scope.enter_context(nc.sbuf_tensor(name, shape, dt))

        layer_sems = []

        def sem(name):
            layer_sems.append(nc.alloc_semaphore(name=name))
            return layer_sems[-1]

        def lasting_sem(name):
            return nc.alloc_semaphore(name=name)

        PS = top.enter_context(nc.psum_tensor("PS", [P, 8, 512], F32))
        table = sb("table", [P, T_W])
        pick = sb("pick", [4, 2 + 2 * P])
        ident = table[:, T_ID:T_ID + P]
        X = sb("X", [P, REQ, D])
        G = sb("G", [P, 2, REQ, D])
        COL = sb("COL", [P, 4, KD, REQ])
        eps = sb("eps", [P, 2])
        raw = [sb(f"raw{i}", [P, SLOT]) for i in range(RING)]
        gate_rows = nc.dram_tensor("gate_rows", [DEPTH, NE, REQ * TOK], F32, kind="Internal").ap()

        s_const = lasting_sem("constants_landed")
        s_x = lasting_sem("x_landed")
        s_eps = lasting_sem("eps_ready")
        s_out = lasting_sem("outputs_stored")
        n_out = [0]
        act_link = lasting_sem("act_step_done")
        dve_link = lasting_sem("dve_step_done")
        links = {"act": 0, "dve": 0}

        def act_step(act, ins):
            links["act"] += 1
            ins.then_inc(act_link, 1)
            act.wait_ge(act_link, links["act"])

        def dve_step(dve, ins):
            links["dve"] += 1
            ins.then_inc(dve_link, 1)
            dve.wait_ge(dve_link, links["dve"])

        def store(eng, out, in_):
            n_out[0] += 16
            eng.dma_start(out, in_).then_inc(s_out, 16)

        ada_landed = [[named(f"ada{l}_weights_landed{i}") for i in range(RING)] for l, named in enumerate((sem, lasting_sem))]

        def ada_columns(it, j):
            return (NADA - RING + j) * 256 if isinstance(it, int) and it == 0 else ((it - 1) * RING + j) * 256

        def ada_load(sp, l, it, j):
            sp.dma_start(raw[j][:, 0:KD * 256].rearrange("p (k n) -> p k n", k=KD),
                         t["ada_w"][l].rearrange("(p k) n -> p k n", k=KD)[:, :, bass.ds(ada_columns(it, j), 256)]).then_inc(ada_landed[l][j], 16)

        cs = sb("conditioning", [P, KD, 4], F32R)

        def ada(l, prefetch):
            with ExitStack() as scope:
                wh = [sb(f"ada{l}_wh{i}", [P, KD, 256], F32R, scope) for i in range(2)]
                wl = [sb(f"ada{l}_wl{i}", [P, KD, 256], F32R, scope) for i in range(2)]
                row4 = sb(f"ada{l}_row4", [4, 6 * D], F32, scope)
                bias4 = sb(f"ada{l}_bias4", [4, 6 * D], F32, scope)
                craw = sb(f"ada{l}_c", [P, REQ, KD], F32, scope)
                csil = sb(f"ada{l}_silu", [P, KD, REQ], F32, scope)
                n = f"ada{l}_"
                first_own = len(layer_sems)
                landed = ada_landed[l]
                c_landed, b_landed, b_zero = sem(n + "c_landed"), sem(n + "bias_landed"), sem(n + "bias_zeroed")
                c_silu, c_hi, c_lo = sem(n + "c_silu"), sem(n + "c_high"), sem(n + "c_low")
                w_hi, w_lo = sem(n + "weights_high"), sem(n + "weights_low")
                rows_mm, rows = sem(n + "rows_multiplied"), sem(n + "rows_ready")
                cols_mm, cols = sem(n + "columns_multiplied"), sem(n + "columns_ready")
                gates_mm, gates_ready = sem(n + "gates_multiplied"), sem(n + "gates_ready")
                ROUNDS = NADA // RING
                GATES = [4, 5, 6, 7, 0, 1, 2, 3]
                MID = ROUNDS - 8 // RING
                gbank = lambda g: 5 + g % 3
                pick_r = sb(f"ada{l}_pick_r", [4, 2 * P], F32R, scope)
                gate_h = [sb(f"ada{l}_gate_h{i}", [4, 512], F32R, scope) for i in range(2)]
                gate_l = [sb(f"ada{l}_gate_l{i}", [4, 512], F32R, scope) for i in range(2)]
                gate_hi, gate_lo = sem(n + "gate_rows_high"), sem(n + "gate_rows_low")
                gate_src = lambda i: (2 if i < 4 else 5) * D + i % 2 * 512
                with nc.Block() as block:
                    @block.sync
                    def _(sp):
                        if l == 0:
                            ada_load(sp, l, 0, 0)
                            sp.dma_start(craw[:, 0, :], t["c_ctx"].rearrange("(p k) -> p k", k=KD)).then_inc(c_landed, 16)
                            sp.dma_start(craw[:, 1, :], t["c"][0].rearrange("(p k) -> p k", k=KD)).then_inc(c_landed, 16)
                            ada_load(sp, l, 0, 1)
                        sp.wait_ge(b_zero, 1)
                        sp.dma_start(bias4[0:2, :], t["ada_b"][l:l + 1, :].partition_broadcast(2)).then_inc(b_landed, 16)
                        if l == 0:
                            for j in range(2, RING):
                                ada_load(sp, l, 0, j)
                            sp.dma_start(table[:, :], t["table"]).then_inc(s_const, 16)
                            sp.dma_start(pick[:, :], t["pick"]).then_inc(s_const, 16)
                            sp.dma_start(X[:, 0, :], t["x_prompt"][0]).then_inc(s_x, 16)
                            sp.dma_start(X[:, 1, :], t["x_sample"][0]).then_inc(s_x, 16)
                        with sp.Fori(1, ROUNDS) as it:
                            for j in range(RING):
                                sp.wait_ge(w_lo, (it - 1) * RING + j + 1)
                                ada_load(sp, l, it, j)
                        for j in range(RING):
                            sp.wait_ge(w_lo, NADA - RING + j + 1)
                            prefetch(sp, j)

                    @block.gpsimd
                    def _(pool):
                        pool.memset(bias4[:, :], 0.0).then_inc(b_zero, 1)
                        for g, i in enumerate(GATES):
                            pool.wait_ge(gate_hi, g + 1)
                            src = gate_src(i)
                            pool.tensor_tensor(gate_l[g % 2][:, :], row4[:, src:src + 512], gate_h[g % 2][:, :].bitcast(F32),
                                               ALU.subtract).then_inc(gate_lo, 1)
                        pool.wait_ge(gate_lo, 8)

                    @block.scalar
                    def _(act):
                        if l == 0:
                            act.wait_ge(c_landed, 32)
                            act.activation(csil[:, :, :], craw[:, :, :].rearrange("p r k -> p k r"), ACT.Silu).then_inc(c_silu, 1)
                            act.wait_ge(c_silu, 1)
                            act.activation(cs[:, :, 0:2], csil[:, :, :], ACT.Copy).then_inc(c_hi, 1)

                        def high(it, j):
                            b = it * RING + j
                            act.wait_ge(landed[j], it * 16 + 16)
                            wait(act, rows_mm, b - 1)
                            act.activation(wh[j % 2][:, :, :], raw[j][:, 0:KD * 256].rearrange("p (k n) -> p k n", k=KD),
                                           ACT.Copy).then_inc(w_hi, 1)
                        for j in range(RING):
                            high(0, j)
                        with act.Fori(1, MID) as it:
                            for j in range(RING):
                                high(it, j)
                        high(MID, 0)
                        act.wait_ge(s_const, 32)
                        act_step(act, act.activation(pick_r[:, :], pick[:, 2:], ACT.Copy))

                        def gate(g):
                            i = GATES[g]
                            act.wait_ge(gates_mm, g + 1)
                            act.activation(G[:, i // 4, i // 2 % 2, i % 2 * 512:i % 2 * 512 + 512], PS[:, gbank(g), :],
                                           ACT.Copy).then_inc(gates_ready, 1)
                        for g, i in enumerate(GATES):
                            if g < 7:
                                high(MID + (g + 1) // RING, (g + 1) % RING)
                            act.wait_ge(rows, RING if g < 4 else 4 * RING)
                            wait(act, gates_mm, g - 1)
                            src = gate_src(i)
                            act.activation(gate_h[g % 2][:, :], row4[:, src:src + 512], ACT.Copy).then_inc(gate_hi, 1)
                            if g:
                                gate(g - 1)
                        gate(7)
                        act.wait_ge(gates_ready, 8)

                    @block.vector
                    def _(dve):
                        if l == 0:
                            dve.memset(eps[:, 0:1], LN_EPS)
                            dve.memset(eps[:, 1:2], RMS_EPS).then_inc(s_eps, 1)
                            dve.wait_ge(c_hi, 1)
                            dve.tensor_tensor(cs[:, :, 2:4], csil[:, :, :], cs[:, :, 0:2].bitcast(F32), ALU.subtract).then_inc(c_lo, 1)

                        def low(it, j):
                            b = it * RING + j
                            dve.wait_ge(w_hi, b + 1)
                            wait(dve, rows_mm, b - 1)
                            dve.tensor_tensor(wl[j % 2][:, :, :], raw[j][:, 0:KD * 256].rearrange("p (k n) -> p k n", k=KD),
                                              wh[j % 2][:, :, :].bitcast(F32), ALU.subtract).then_inc(w_lo, 1)

                        def row(it, j):
                            b = it * RING + j
                            dve.wait_ge(rows_mm, b + 1)
                            at = bass.ds(ada_columns(it, j), 256)
                            dve.tensor_tensor(row4[:, at], PS[0:4, j, 0:256], bias4[:, at], ALU.add).then_inc(rows, 1)
                        for j in range(RING):
                            low(0, j)
                        dve.wait_ge(b_landed, 16)
                        row(0, 0)

                        def columns(s):
                            c4 = PS[:, 4, 0:4 * KD * REQ].rearrange("p (s k r) -> p s k r", s=4, k=KD)
                            dve.tensor_scalar(COL[:, s, :, :], c4[:, s, :, :], float(s % 2), None, ALU.add).then_inc(cols, 1)

                        def round_of(it, j):
                            low(it, j)
                            row(*((it, 0) if j == RING - 1 else (it - 1, j + 1)))
                        for j in range(RING):
                            round_of(1, j)
                        with dve.Fori(2, MID) as it:
                            for j in range(RING):
                                round_of(it, j)
                        round_of(MID, 0)
                        dve.wait_ge(cols_mm, 1)
                        for s in range(2):
                            columns(s)
                        for b in range(MID * RING + 1, NADA):
                            round_of(b // RING, b % RING)
                        for j in range(1, RING):
                            row(ROUNDS - 1, j)
                        dve.wait_ge(cols_mm, 2)
                        for s in range(2, 4):
                            columns(s)
                        dve.wait_ge(cols, 4)

                    @block.tensor
                    def _(pe):
                        if l == 0:
                            pe.wait_ge(c_lo, 1)

                        def rows_product(it, j):
                            b = it * RING + j
                            pe.wait_ge(w_lo, b + 1)
                            wait(pe, rows, b - RING + 1)
                            for k in range(KD):
                                pe.matmul(PS[0:4, j, 0:256], cs[:, k, :], wh[j % 2][:, k, :], start=(k == 0), stop=False)
                                mm = pe.matmul(PS[0:4, j, 0:256], cs[:, k, :], wl[j % 2][:, k, :], start=False, stop=(k == KD - 1))
                            mm.then_inc(rows_mm, 1)
                        for j in range(RING):
                            rows_product(0, j)
                        with pe.Fori(1, MID) as it:
                            for j in range(RING):
                                rows_product(it, j)

                        def columns(first):
                            for s in range(first, first + 2):
                                which = (0, 1, 3, 4)[s]
                                for k in range(KD):
                                    at = (s * KD + k) * REQ
                                    mm = pe.matmul(PS[:, 4, at:at + REQ], row4[:, which * D + k:which * D + D:KD], pick[:, 0:2],
                                                   start=True, stop=True)
                            mm.then_inc(cols_mm, 1)

                        pe.wait_ge(s_const, 32)
                        pe.wait_ge(rows, 3 * RING)
                        columns(0)
                        for g, i in enumerate(GATES):
                            rows_product(MID + g // RING, g % RING)
                            pe.wait_ge(gate_lo, g + 1)
                            wait(pe, gates_ready, g - 2)
                            row = pick_r[:, P * (i // 2 % 2):P * (i // 2 % 2) + P]
                            pe.matmul(PS[:, gbank(g), :], row, gate_h[g % 2][:, :], start=True, stop=False)
                            pe.matmul(PS[:, gbank(g), :], row, gate_l[g % 2][:, :], start=False, stop=True).then_inc(gates_mm, 1)
                        pe.wait_ge(rows, NADA)
                        pe.wait_ge(cols, 2)
                        columns(2)
                nc.clear_and_free_semaphores(layer_sems[first_own:])
                del layer_sems[first_own:]
                nc.all_engine_barrier()

        class Modulate:
            def __init__(self, name, s, scope):
                self.s = s
                self.HT = sb(name + "_HT", [P, KD, REQ * TOK], F32, scope)
                self.h = sb(name + "_HTh", [P, KD, REQ * TOK], F32R, scope)
                self.l = sb(name + "_HTl", [P, KD, REQ * TOK], F32R, scope)
                self.turned = sem(name + "_turned")
                self.mod = [sem(f"{name}_modulated{r}") for r in range(REQ)]
                self.hi = sem(name + "_high")
                self.lo = sem(name + "_low")

            def tensor(self, pe):
                for r in range(REQ):
                    for half in range(2):
                        for i in range(4):
                            k = half * 4 + i
                            mm = pe.transpose(PS[:, 2 * r + half, i * P:(i + 1) * P], X[:, r, k:D:KD], ident)
                        mm.then_inc(self.turned, 1)

            def scalar(self, act):
                act.wait_ge(self.turned, 2)
                for k in range(KD):
                    act.activation(self.HT[:, k, 0:TOK], PS[:, k // 4, k % 4 * P:k % 4 * P + P], ACT.Identity,
                                   bias=COL[:, self.s, k, 0:1], scale=COL[:, self.s + 1, k, 0:1]).then_inc(self.mod[0], 1)
                act.wait_ge(self.mod[0], KD)
                act.activation(self.h[:, :, 0:TOK], self.HT[:, :, 0:TOK], ACT.Copy).then_inc(self.hi, 1)
                act.wait_ge(self.mod[1], KD)
                act.activation(self.h[:, :, TOK:], self.HT[:, :, TOK:], ACT.Copy).then_inc(self.hi, 1)

            def vector(self, dve):
                dve.wait_ge(self.turned, 4)
                for k in range(KD):
                    dve.tensor_scalar(self.HT[:, k, TOK:], PS[:, 2 + k // 4, k % 4 * P:k % 4 * P + P],
                                      COL[:, self.s + 1, k, 1:2], COL[:, self.s, k, 1:2], ALU.mult, ALU.add).then_inc(self.mod[1], 1)
                for r in range(REQ):
                    dve.wait_ge(self.hi, r + 1)
                    at = slice(r * TOK, (r + 1) * TOK)
                    dve.tensor_tensor(self.l[:, :, at], self.HT[:, :, at], self.h[:, :, at].bitcast(F32), ALU.subtract).then_inc(self.lo, 1)

        def three(pe, out, ah, al, bh, bl, start, stop):
            pe.matmul(out, ah, bh, start=start, stop=False, skip_group_check=True)
            pe.matmul(out, ah, bl, start=False, stop=False, skip_group_check=True)
            return pe.matmul(out, al, bh, start=False, stop=stop, skip_group_check=True)

        class Norm:
            def __init__(self, name, l, ffn, banks, out_ready, scope, g_ap, b_ap):
                self.name, self.l, self.ffn, self.banks, self.out_ready = name, l, ffn, banks, out_ready
                self.gb = sb(name + "_gain_bias", [P, 2, D], F32, scope)
                self.tmp = sb(name + "_tmp", [P, REQ, D], F32, scope)
                self.st = sb(name + "_stats", [P, REQ, 2, 6], F32, scope)
                self.mv = sb(name + "_mean_var", [P, REQ, 2], F32, scope)
                self.rs = sb(name + "_rstd", [P, REQ, 4], F32, scope)
                self.landed = sem(name + "_gain_landed")
                self.var = sem(name + "_variance")
                self.std = sem(name + "_std")
                self.coef = sem(name + "_coefficients")
                self.unit = sem(name + "_unit")
                self.done = [sem(f"{name}_done{r}") for r in range(REQ)]
                self.g_ap, self.b_ap = g_ap, b_ap
                self.source = lambda r, n: PS[:, self.banks[2 * r + n], :]

            def sync(self, sp):
                sp.dma_start(self.gb[:, 0, :], self.g_ap.partition_broadcast(P)).then_inc(self.landed, 16)
                sp.dma_start(self.gb[:, 1, :], self.b_ap.partition_broadcast(P)).then_inc(self.landed, 16)

            def vector(self, dve):
                def gated(r):
                    self.out_ready(dve, r)
                    for n in range(2):
                        at = slice(n * 512, n * 512 + 512)
                        i = dve.tensor_tensor(self.tmp[:, r, at], self.source(r, n), G[:, self.ffn, r, at], ALU.mult)
                    dve_step(dve, i)

                def statistics(r):
                    dve_step(dve, dve.scalar_tensor_tensor(self.tmp[:, r, :], X[:, r, :], ALPHA, self.tmp[:, r, :], ALU.mult, ALU.add))
                    for n in range(2):
                        i = dve.bn_stats(self.st[:, r, n, :], self.tmp[:, r, n * 512:n * 512 + 512])
                    dve_step(dve, i)
                    dve.bn_aggr(self.mv[:, r, :], self.st[:, r, :, :]).then_inc(self.var, 1)

                def rstd(r):
                    dve.wait_ge(self.std, r + 1)
                    dve_step(dve, dve.reciprocal(self.rs[:, r, 1:2], self.rs[:, r, 0:1]))
                gated(0)
                statistics(0)
                gated(1)
                rstd(0)
                dve.scalar_tensor_tensor(self.rs[:, 0, 2:3], self.mv[:, 0, 0:1], -1.0, self.rs[:, 0, 1:2],
                                         ALU.mult, ALU.mult).then_inc(self.coef, 1)
                statistics(1)
                dve.wait_ge(self.landed, 32)
                dve.wait_ge(self.var, 2)
                dve_step(dve, dve.scalar_tensor_tensor(X[:, 1, :], self.tmp[:, 1, :], self.mv[:, 1, 0:1], self.gb[:, 0, :],
                                                       ALU.subtract, ALU.mult))
                rstd(1)
                dve.scalar_tensor_tensor(X[:, 1, :], X[:, 1, :], self.rs[:, 1, 1:2], self.gb[:, 1, :],
                                         ALU.mult, ALU.add).then_inc(self.done[1], 1)
                dve.wait_ge(self.done[1], 1)

            def scalar(self, act):
                act.wait_ge(s_eps, 1)
                act_step(act, act.activation(self.rs[:, 0, 3:4], eps[:, 0:1], ACT.Sqrt))
                for r in range(REQ):
                    act.wait_ge(self.var, r + 1)
                    act.activation(self.rs[:, r, 0:1], self.mv[:, r, 1:2], ACT.Sqrt, bias=eps[:, 0:1]).then_inc(self.std, 1)
                    if r == 0:
                        act.wait_ge(self.coef, 1)
                        act.activation(self.tmp[:, r, :], self.tmp[:, r, :], ACT.Identity, bias=self.rs[:, r, 2:3],
                                       scale=self.rs[:, r, 1:2]).then_inc(self.unit, 1)

            def gpsimd(self, pool):
                pool.wait_ge(self.landed, 32)
                pool.wait_ge(self.unit, 1)
                pool.tensor_tensor(X[:, 0, :], self.tmp[:, 0, :], self.gb[:, 0, :], ALU.mult).then_inc(self.done[0], 1)
                pool.wait_ge(self.done[0], 1)
                pool.tensor_tensor(X[:, 0, :], X[:, 0, :], self.gb[:, 1, :], ALU.add).then_inc(self.done[0], 1)
                pool.wait_ge(self.done[0], 2)

        class Project:
            def __init__(self, name, view, width, count, bank, evac=None):
                self.name, self.view, self.width, self.count, self.bank, self.evac = name, view, width, count, bank, evac
                self.landed = [sem(f"{name}_landed{i}") for i in range(RING)]
                self.hi, self.lo = sem(name + "_high"), sem(name + "_low")
                self.mm = sem(name + "_multiplied")
                self.ready = [sem(f"{name}_out{r}") for r in range(REQ)]

            def alloc(self, scope, lh, ll):
                self.lh, self.ll = lh, ll
                self.wh = [sb(f"{self.name}_wh{i}", [P, KD, self.width], F32R, scope) for i in range(2)]
                self.wl = [sb(f"{self.name}_wl{i}", [P, KD, self.width], F32R, scope) for i in range(2)]

            def raw(self, b):
                return raw[b % RING][:, 0:KD * self.width].rearrange("p (k n) -> p k n", k=KD)

            def load(self, sp, b):
                sp.dma_start(self.raw(b), self.view[:, :, b * self.width:(b + 1) * self.width]).then_inc(self.landed[b % RING], 16)

            act_between = dve_between = lambda self, eng, b: None

            def sync(self, sp):
                for b in range(RING, self.count):
                    sp.wait_ge(self.lo, b - RING + 1)
                    self.load(sp, b)

            def scalar(self, act):
                for b in range(self.count + 1):
                    if b < self.count:
                        act.wait_ge(self.landed[b % RING], 16 * (b // RING + 1))
                        wait(act, self.mm, 2 * (b - 1))
                        act.activation(self.wh[b % 2][:, :, :], self.raw(b), ACT.Copy).then_inc(self.hi, 1)
                        self.act_between(act, b)
                    if b and self.evac:
                        act.wait_ge(self.mm, 2 * b - 1)
                        self.evac(act, b - 1, 0).then_inc(self.ready[0], 1)

            def vector(self, dve):
                for b in range(self.count + 1):
                    if b < self.count:
                        dve.wait_ge(self.hi, b + 1)
                        dve.tensor_tensor(self.wl[b % 2][:, :, :], self.raw(b), self.wh[b % 2][:, :, :].bitcast(F32),
                                          ALU.subtract).then_inc(self.lo, 1)
                        self.dve_between(dve, b)
                    if b and self.evac:
                        dve.wait_ge(self.mm, 2 * b)
                        self.evac(dve, b - 1, 1).then_inc(self.ready[1], 1)

            def tensor(self, pe):
                for b in range(self.count):
                    pe.wait_ge(self.lo, b + 1)
                    for r in range(REQ):
                        out = self.bank(b, r)
                        for k in range(KD):
                            at = slice(r * TOK, r * TOK + TOK)
                            mm = three(pe, out, self.lh[:, k, at], self.ll[:, k, at], self.wh[b % 2][:, k, :], self.wl[b % 2][:, k, :],
                                       start=(k == 0), stop=(k == KD - 1))
                        mm.then_inc(self.mm, 1)

        class Turn:
            def __init__(self, name, src, oh, ol):
                self.src, self.oh, self.ol = src, oh, ol
                self.turned, self.hi, self.lo = sem(name + "_turned"), sem(name + "_high"), sem(name + "_low")

            def tensor(self, pe):
                for r in range(REQ):
                    for half in range(2):
                        for i in range(4):
                            k = half * 4 + i
                            mm = pe.transpose(PS[:, 2 * r + half, i * P:(i + 1) * P], self.src[:, r, k:D:KD], ident)
                        mm.then_inc(self.turned, 1)

            def scalar(self, act):
                for q in range(4):
                    act.wait_ge(self.turned, q + 1)
                    act.activation(self.oh[:, q % 2 * 4:q % 2 * 4 + 4, q // 2 * TOK:q // 2 * TOK + TOK],
                                   PS[:, q, :].rearrange("p (k t) -> p k t", k=4), ACT.Copy).then_inc(self.hi, 1)

            def vector(self, dve):
                for q in range(4):
                    dve.wait_ge(self.hi, q + 1)
                    at = (slice(None), slice(q % 2 * 4, q % 2 * 4 + 4), slice(q // 2 * TOK, q // 2 * TOK + TOK))
                    dve.tensor_tensor(self.ol[at], PS[:, q, :].rearrange("p (k t) -> p k t", k=4), self.oh[at].bitcast(F32),
                                      ALU.subtract).then_inc(self.lo, 1)

        class Attend:
            def __init__(self, name, QT, KT, V, dim, scale, sink, merged, at, bufs, scope):
                self.n, self.QT, self.KT, self.V, self.dim, self.scale, self.sink, self.merged, self.at = \
                    name, QT, KT, V, dim, scale, sink, merged, at
                self.Pb, self.PT = bufs
                self.st = sb(name + "_softmax", [P, 8, REQ, H], F32, scope)
                self.scores, self.maxed = sem(name + "_scores"), sem(name + "_negmax")
                self.probs, self.tot, self.es = sem(name + "_probs"), sem(name + "_rowsums"), sem(name + "_sink_exp")
                self.pturn, self.pt = sem(name + "_probs_turned"), [sem(f"{name}_probsT{i}") for i in range(2)]
                self.pv, self.done = sem(name + "_values"), sem(name + "_merged")

            def sbank(self, r):
                if r == 0:
                    return PS[:, 0:2, :].rearrange("p b (h k) -> p (b h) k", k=TOK)
                return PS[:, 2:6, :].rearrange("p b (h k) -> p (b h) k", k=2 * TOK)

            def tensor(self, pe):
                for r in range(REQ):
                    for h in range(H):
                        mm = pe.matmul(self.sbank(r)[:, h, :], self.QT[0:self.dim, r, h, :],
                                       self.KT(h, r, 1 + r), start=True, stop=True)
                    mm.then_inc(self.scores, 1)
                for c in range(6):
                    if c < 2:
                        pe.wait_ge(self.probs, 4 * c + 4)
                        if c == 0:
                            pe.wait_ge(self.probs, 8)
                    else:
                        pe.wait_ge(self.probs, 8 + 2 * (c - 1))
                        if c == 2:
                            pe.wait_ge(self.probs, 16)
                    bank = [6, 7, 0, 1, 2, 3][c]
                    if c >= 2:
                        pe.wait_ge(self.probs, 16)
                    for i in range(4):
                        mm = pe.transpose(PS[:, bank, i * P:(i + 1) * P], self.Pb[:, (4 * c + i) * P:(4 * c + i + 1) * P], ident)
                    mm.then_inc(self.pturn, 1)
                for r in range(REQ):
                    pe.wait_ge(self.pt[0], 1 if r == 0 else 3)
                    pe.wait_ge(self.pt[1], 1 if r == 0 else 3)
                    for h in range(H):
                        out = PS[:, 4 + r, h * VD:(h + 1) * VD]
                        if r == 0:
                            mm = pe.matmul(out, self.PT[:, h * P:(h + 1) * P], self.V(h, 0), start=True, stop=True)
                        else:
                            for s in range(2):
                                c = H + 2 * h + s
                                mm = pe.matmul(out, self.PT[:, c * P:(c + 1) * P], self.V(h, 1 + s), start=(s == 0), stop=(s == 1))
                    mm.then_inc(self.pv, 1)

            def vector(self, dve):
                st = self.st
                for r in range(REQ):
                    dve.wait_ge(self.scores, r + 1)
                    dve_step(dve, dve.tensor_reduce(st[:, 0, r, :], self.sbank(r), AX_X, ALU.max))
                    if self.sink is None:
                        dve.tensor_scalar(st[:, 1, r, :], st[:, 0, r, :], -self.scale, None, ALU.mult).then_inc(self.maxed, 1)
                    else:
                        dve_step(dve, dve.scalar_tensor_tensor(st[:, 2, r, :], st[:, 0, r, :], self.scale, self.sink, ALU.mult, ALU.max))
                        dve_step(dve, dve.tensor_scalar(st[:, 1, r, :], st[:, 2, r, :], -1.0, None, ALU.mult))
                        dve.tensor_tensor(st[:, 3, r, :], self.sink, st[:, 1, r, :], ALU.add).then_inc(self.maxed, 1)
                for c in (1, 3, 5):
                    dve.wait_ge(self.pturn, c + 1)
                    bank = [6, 7, 0, 1, 2, 3][c]
                    dve.tensor_copy(self.PT[:, 4 * c * P:4 * (c + 1) * P], PS[:, bank, :]).then_inc(self.pt[1], 1)
                for r in range(REQ):
                    if self.sink is None:
                        dve.wait_ge(self.probs, 16)
                        dve_step(dve, dve.reciprocal(st[:, 6, r, :], st[:, 4, r, :]))
                    else:
                        dve.wait_ge(self.es, r + 1)
                        dve_step(dve, dve.tensor_tensor(st[:, 7, r, :], st[:, 4, r, :], st[:, 5, r, :], ALU.add))
                        dve_step(dve, dve.reciprocal(st[:, 6, r, :], st[:, 7, r, :]))
                    dve.wait_ge(self.pv, r + 1)
                    dve.tensor_tensor(self.merged[:, r, self.at:self.at + H * VD].rearrange("p (h e) -> p h e", h=H),
                                      PS[:, 4 + r, :].rearrange("p (h e) -> p h e", h=H),
                                      st[:, 6, r, :].unsqueeze(2).to_broadcast([P, H, VD]), ALU.mult).then_inc(self.done, 1)

            def scalar(self, act):
                st = self.st
                for r in range(REQ):
                    act.wait_ge(self.maxed, r + 1)
                    for h in range(H):
                        w = TOK * (1 + r)
                        base = h * TOK if r == 0 else H * TOK + 2 * h * TOK
                        act.activation(self.Pb[:, base:base + w], self.sbank(r)[:, h, :], ACT.Exp, bias=st[:, 1, r, h:h + 1],
                                       scale=self.scale, accum_out=st[:, 4, r, h:h + 1]).then_inc(self.probs, 1)
                    if self.sink is not None:
                        act.activation(st[:, 5, r, :], st[:, 3, r, :], ACT.Exp).then_inc(self.es, 1)
                for c in (0, 2, 4):
                    act.wait_ge(self.pturn, c + 1)
                    bank = [6, 7, 0, 1, 2, 3][c]
                    act.activation(self.PT[:, 4 * c * P:4 * (c + 1) * P], PS[:, bank, :], ACT.Copy).then_inc(self.pt[0], 1)

        def mixer0(w_in, w_out, proj, merged, uq_landed):
            with ExitStack() as scope:
                mod = Modulate("mix0_mod", 0, scope)
                w_in.alloc(scope, mod.h, mod.l)
                with nc.Block() as block:
                    @block.sync
                    def _(sp):
                        sp.wait_ge(w_in.lo, 1)
                        sp.dma_start(raw[0][:, 0:2 * H * QK].rearrange("p (k n) -> p k n", k=2),
                                     t["mla_w_uq"][0].rearrange("(p k) n -> p k n", k=2)).then_inc(uq_landed, 16)
                        sp.dma_start(raw[0][:, 2 * H * QK:2 * H * QK + H * (NOPE + VD)], t["mla_w_ukv"][0]).then_inc(uq_landed, 16)

                    @block.tensor
                    def _(pe):
                        pe.wait_ge(s_x, 32)
                        mod.tensor(pe)
                        pe.wait_ge(mod.lo, 2)
                        w_in.tensor(pe)

                    @block.scalar
                    def _(act):
                        mod.scalar(act)
                        w_in.scalar(act)
                        act.wait_ge(w_in.ready[0], w_in.count)

                    @block.vector
                    def _(dve):
                        mod.vector(dve)
                        w_in.vector(dve)
                        dve.wait_ge(w_in.ready[1], w_in.count)
            with ExitStack() as scope:
                Pb = sb("probs", [P, 3 * H * TOK], F32, scope)
                PT = sb("probsT", [P, 3 * H * TOK], F32, scope)
                QT = sb("QT", [QK, REQ, H, TOK], F32, scope)
                KT = sb("KT", [QK, H, 3, TOK], F32, scope)
                cq = sb("cq_n", [P, REQ, RQ], F32, scope)
                ckv = sb("ckv_n", [P, 3, RKV], F32, scope)
                cqT = sb("cqT", [P, 2, REQ, TOK], F32, scope)
                ckvT = sb("ckvT", [P, 3, TOK], F32, scope)
                QM = sb("QM", [P, REQ, H, QK], F32, scope)
                KM = sb("KM", [P, 3, H, QK], F32, scope)
                VM = sb("VM", [P, 3, H, VD], F32, scope)
                kcv = sb("cache_kv", [P, 2, KV * HD], F32, scope)
                krc = sb("cache_kr", [P, ROPE], F32, scope)
                norms = sb("norm_gains", [P, RQ + RKV], F32, scope)
                sink = sb("sink_b", [P, H], F32, scope)
                rt = sb("rope_tmp", [P, 4, 10 * 32], F32, scope)
                rms = sb("rms", [P, 3, 4], F32, scope)
                junk = sb("junk", [P, RQ], F32, scope)
                landed = sem("attn_inputs_landed")
                roped, kr_roped = sem("rope_done"), sem("mla_k_rope_done")
                a_turn, a_t = sem("a_turned"), [sem("a_turned_act"), sem("a_turned_dve")]
                sq, msq, std, rmsed = sem("rms_squares"), sem("rms_mean"), sem("rms_root"), sem("rms_done")
                c_turn, cT = sem("c_turned"), sem("cT_ready")
                qm_mm, qm = sem("qm_multiplied"), sem("qm_ready")
                kv_mm, kv_e = sem("kv_multiplied"), [sem("kv_act"), sem("kv_dve")]
                qroped = sem("qm_roped")
                m_turn, m_t = sem("m_turned"), [sem("m_turned_act"), sem("m_turned_dve")]
                kfill = sem("k_rope_filled")
                atA = Attend("attA", QT, lambda h, s, n: KT[0:HD, h // GRP, s:s + n, :],
                             lambda h, s: (proj[:, s, A_V + h // GRP * HD:A_V + (h // GRP + 1) * HD] if s < 2
                                           else kcv[:, 1, h // GRP * HD:(h // GRP + 1) * HD]),
                             HD, SC_A, sink[:, :], merged, 0, (Pb, PT), scope)
                atM = Attend("attM", QT, lambda h, s, n: KT[0:QK, h, s:s + n, :], lambda h, s: VM[:, s, h, :],
                             QK, SC_M, None, merged, H * HD, (Pb, PT), scope)

                def rotate(dve, src, heads, quarter, tab):
                    x = src.rearrange("p h (a b w) -> p h a b w", a=2, b=2)
                    x1, x2 = x[:, :, :, 0, :], x[:, :, :, 1, :]
                    cs = tab.rearrange("p (s a w) -> p s a w", s=2, a=2)
                    shape = [P, heads, 2, quarter]
                    co = cs[:, 0, :, :].unsqueeze(1).to_broadcast(shape)
                    si = cs[:, 1, :, :].unsqueeze(1).to_broadcast(shape)
                    tm = [rt[:, i, 0:heads * 2 * quarter].rearrange("p (h a w) -> p h a w", h=heads, a=2) for i in range(4)]
                    dve.tensor_tensor(tm[0], x1, co, ALU.mult)
                    dve.tensor_tensor(tm[1], x2, si, ALU.mult)
                    dve.tensor_tensor(tm[2], x1, si, ALU.mult)
                    dve_step(dve, dve.tensor_tensor(tm[3], x2, co, ALU.mult))
                    dve_step(dve, dve.tensor_tensor(x1, tm[0], tm[1], ALU.subtract))
                    return dve.tensor_tensor(x2, tm[2], tm[3], ALU.add)

                def a_copy(eng, q):
                    src = PS[0:HD, q, :]
                    if q < 4:
                        dst = QT[0:HD, q // 2, q % 2 * 4:q % 2 * 4 + 4, :]
                        src = src.rearrange("p (h t) -> p h t", h=4)
                    else:
                        src = src[:, 0:3 * TOK].rearrange("p (h t) -> p h t", h=3)
                        dst = KT[0:HD, q - 4, :, :]
                    if q % 2 == 0:
                        eng.activation(dst, src, ACT.Copy).then_inc(a_t[0], 1)
                    else:
                        eng.tensor_copy(dst, src).then_inc(a_t[1], 1)

                def kv_copy(eng, i):
                    eng.wait_ge(kv_mm, i + 1)
                    bank = [4, 5, 6, 7, 0, 1][i]
                    v = PS[:, bank, :].rearrange("p (h e) -> p h e", h=4)
                    hs = slice(i % 2 * 4, i % 2 * 4 + 4)
                    if i % 2 == 0:
                        eng.activation(KM[:, i // 2, hs, 0:NOPE], v[:, :, 0:NOPE], ACT.Copy)
                        eng.activation(VM[:, i // 2, hs, :], v[:, :, NOPE:], ACT.Copy).then_inc(kv_e[0], 1)
                    else:
                        eng.tensor_copy(KM[:, i // 2, hs, 0:NOPE], v[:, :, 0:NOPE])
                        eng.tensor_copy(VM[:, i // 2, hs, :], v[:, :, NOPE:]).then_inc(kv_e[1], 1)

                MB = [2, 3, 4, 5, 6, 7, 0, 1, 2, 3]

                def m_copy(eng, q):
                    src = PS[0:QK, MB[q], :].rearrange("p (h t) -> p h t", h=4)
                    hs = slice(q % 2 * 4, q % 2 * 4 + 4)
                    dst = QT[:, q // 2, hs, :] if q < 4 else KT[:, hs, (q - 4) // 2, :]
                    if q % 2 == 0:
                        eng.activation(dst, src, ACT.Copy).then_inc(m_t[0], 1)
                    else:
                        eng.tensor_copy(dst, src).then_inc(m_t[1], 1)

                with nc.Block() as block:
                    @block.sync
                    def _(sp):
                        sp.dma_start(kcv[:, 0, :], t["cache_attn_k"][0, 0].rearrange("k h d -> k (h d)")).then_inc(landed, 16)
                        sp.dma_start(kcv[:, 1, :], t["cache_attn_v"][0, 0].rearrange("k h d -> k (h d)")).then_inc(landed, 16)
                        sp.dma_start(krc[:, :], t["cache_mla_krope"][0, 0]).then_inc(landed, 16)
                        sp.dma_start(ckv[:, 2, :], t["cache_mla_ckv"][0, 0]).then_inc(landed, 16)
                        sp.dma_start(sink[:, :], t["attn_sink"].partition_broadcast(P)).then_inc(landed, 16)
                        sp.dma_start(norms[:, 0:RQ], t["mla_q_norm"].partition_broadcast(P)).then_inc(landed, 16)
                        sp.dma_start(norms[:, RQ:], t["mla_kv_norm"].partition_broadcast(P)).then_inc(landed, 16)
                        store(sp, k_out[0, 0].rearrange("k h d -> k (h d)"), proj[:, 0, A_K:A_V])
                        store(sp, v_out[0, 0].rearrange("k h d -> k (h d)"), proj[:, 0, A_V:A_CQ])
                        store(sp, kr_out[0, 0], proj[:, 0, A_KR:W_AB])
                        sp.wait_ge(rmsed, 4)
                        store(sp, ckv_out[0, 0], ckv[:, 0, :])
                        for b in range(1, RING):
                            w_out.load(sp, b)
                        sp.wait_ge(kv_mm, 6)
                        w_out.load(sp, 0)
                        sp.wait_ge(s_out, n_out[0])

                    @block.scalar
                    def _(act):
                        for r in range(REQ):
                            act.activation(junk[:, 0:RQ], proj[:, r, A_CQ:A_CKV], ACT.Square, accum_out=rms[:, 0, 2 * r:2 * r + 1]).then_inc(sq, 1)
                            act.wait_ge(sq, 2 * r + 1)
                            act.activation(junk[:, 0:RKV], proj[:, r, A_CKV:A_KR], ACT.Square, accum_out=rms[:, 0, 2 * r + 1:2 * r + 2]).then_inc(sq, 1)
                            act.wait_ge(sq, 2 * r + 2)
                        act.wait_ge(msq, 2)
                        act.activation(rms[:, 2, :], rms[:, 1, :], ACT.Sqrt).then_inc(std, 1)
                        for q in (0, 2, 4):
                            act.wait_ge(a_turn, q + 1)
                            a_copy(act, q)
                        atA.scalar(act)
                        for q in range(2):
                            act.wait_ge(c_turn, q + 1)
                            if q == 0:
                                act.activation(cqT[:, :, :, :], PS[:, 6, :].rearrange("p (k r t) -> p k r t", k=2, r=2), ACT.Copy).then_inc(cT, 1)
                            else:
                                act.activation(ckvT[:, :, :], PS[:, 7, 0:3 * TOK].rearrange("p (s t) -> p s t", s=3), ACT.Copy).then_inc(cT, 1)
                        for i in range(4):
                            act.wait_ge(qm_mm, i + 1)
                            act.activation(QM[:, i // 2, i % 2 * 4:i % 2 * 4 + 4, :], PS[:, i, 0:4 * QK].rearrange("p (h d) -> p h d", h=4),
                                           ACT.Copy).then_inc(qm, 1)
                        for i in (0, 2, 4):
                            kv_copy(act, i)
                        for q in range(0, 10, 2):
                            act.wait_ge(m_turn, q + 1)
                            m_copy(act, q)
                        atM.scalar(act)

                    @block.vector
                    def _(dve):
                        rotate(dve, proj[:, 1, 0:A_V].rearrange("p (h d) -> p h d", d=HD), H + KV, HD // 4, table[:, T_RA:T_RM]).then_inc(roped, 1)
                        dve.wait_ge(roped, 1)
                        rotate(dve, proj[:, 1, A_KR:W_AB].unsqueeze(1), 1, ROPE // 4, table[:, T_RM:T_IO]).then_inc(kr_roped, 1)
                        dve.wait_ge(sq, 4)
                        for j, n in enumerate((RQ, RKV)):
                            dve.tensor_scalar(rms[:, 1, j:4:2], rms[:, 0, j:4:2], 1.0 / n, RMS_EPS, ALU.mult, ALU.add).then_inc(msq, 1)
                        dve.wait_ge(std, 1)
                        dve_step(dve, dve.reciprocal(rms[:, 0, :], rms[:, 2, :]))
                        dve.wait_ge(landed, 7 * 16)
                        for r in range(REQ):
                            dve.scalar_tensor_tensor(cq[:, r, :], proj[:, r, A_CQ:A_CKV], rms[:, 0, 2 * r:2 * r + 1], norms[:, 0:RQ],
                                                     ALU.mult, ALU.mult).then_inc(rmsed, 1)
                            dve.scalar_tensor_tensor(ckv[:, r, :], proj[:, r, A_CKV:A_KR], rms[:, 0, 2 * r + 1:2 * r + 2], norms[:, RQ:],
                                                     ALU.mult, ALU.mult).then_inc(rmsed, 1)
                        dve.wait_ge(kr_roped, 1)
                        for s in range(3):
                            src = krc[:, :] if s == 2 else proj[:, s, A_KR:W_AB]
                            dve.tensor_copy(KM[:, s, :, NOPE:], src.unsqueeze(1).to_broadcast([P, H, ROPE])).then_inc(kfill, 1)
                        for q in (1, 3, 5):
                            dve.wait_ge(a_turn, q + 1)
                            a_copy(dve, q)
                        atA.vector(dve)
                        dve.wait_ge(qm, 4)
                        rotate(dve, QM[:, 1, :, NOPE:], H, ROPE // 4, table[:, T_RM:T_IO]).then_inc(qroped, 1)
                        for i in (1, 3, 5):
                            kv_copy(dve, i)
                        for q in range(1, 10, 2):
                            dve.wait_ge(m_turn, q + 1)
                            m_copy(dve, q)
                        atM.vector(dve)
                        dve.wait_ge(atM.done, 2)

                    @block.tensor
                    def _(pe):
                        pe.wait_ge(landed, 7 * 16)
                        pe.wait_ge(roped, 1)
                        for q in range(4):
                            for i in range(4):
                                h = q % 2 * 4 + i
                                mm = pe.transpose(PS[0:HD, q, i * P:(i + 1) * P], proj[:, q // 2, h * HD:(h + 1) * HD], ident)
                            mm.then_inc(a_turn, 1)
                        for g in range(KV):
                            for s in range(3):
                                src = kcv[:, 0, g * HD:(g + 1) * HD] if s == 2 else proj[:, s, A_K + g * HD:A_K + (g + 1) * HD]
                                mm = pe.transpose(PS[0:HD, 4 + g, s * P:(s + 1) * P], src, ident)
                            mm.then_inc(a_turn, 1)
                        pe.wait_ge(a_t[0], 3)
                        pe.wait_ge(a_t[1], 3)
                        atA.tensor(pe)
                        pe.wait_ge(rmsed, 4)
                        for k in range(2):
                            for r in range(REQ):
                                mm = pe.transpose(PS[:, 6, (2 * k + r) * P:(2 * k + r + 1) * P], cq[:, r, k:RQ:2], ident)
                        mm.then_inc(c_turn, 1)
                        for s in range(3):
                            mm = pe.transpose(PS[:, 7, s * P:(s + 1) * P], ckv[:, s, :], ident)
                        mm.then_inc(c_turn, 1)
                        pe.wait_ge(cT, 2)
                        pe.wait_ge(uq_landed, 32)
                        uq = raw[0][:, 0:2 * H * QK].rearrange("p (k n) -> p k n", k=2)
                        for i in range(4):
                            for k in range(2):
                                mm = pe.matmul(PS[:, i, 0:4 * QK], cqT[:, k, i // 2, :], uq[:, k, i % 2 * 4 * QK:i % 2 * 4 * QK + 4 * QK],
                                               start=(k == 0), stop=(k == 1))
                            mm.then_inc(qm_mm, 1)
                        pe.wait_ge(atA.done, 2)
                        for i in range(6):
                            if i == 4:
                                pe.wait_ge(qm, 2)
                            bank = [4, 5, 6, 7, 0, 1][i]
                            w0 = 2 * H * QK + i % 2 * 512
                            pe.matmul(PS[:, bank, :], ckvT[:, i // 2, :], raw[0][:, w0:w0 + 512], start=True, stop=True).then_inc(kv_mm, 1)
                        pe.wait_ge(qm, 4)
                        pe.wait_ge(qroped, 1)
                        pe.wait_ge(kfill, 3)
                        pe.wait_ge(kv_e[0], 3)
                        pe.wait_ge(kv_e[1], 3)
                        for q in range(10):
                            if q >= 8:
                                pe.wait_ge(m_t[q % 2], (q - 8) // 2 + 1)
                            for i in range(4):
                                h = q % 2 * 4 + i
                                src = QM[:, q // 2, h, :] if q < 4 else KM[:, (q - 4) // 2, h, :]
                                mm = pe.transpose(PS[0:QK, MB[q], i * P:(i + 1) * P], src, ident)
                            mm.then_inc(m_turn, 1)
                        pe.wait_ge(m_t[0], 5)
                        pe.wait_ge(m_t[1], 5)
                        atM.tensor(pe)

        def run_layer0():
            with ExitStack() as outer:
                proj = sb("proj", [P, REQ, W_AB], F32, outer)
                merged = sb("merged", [P, REQ, D], F32, outer)
                uq_landed = sem("uq_landed")
                wi = W_AB // 4

                def evac_in(eng, b, r):
                    src = PS[:, (2 * b + r) % 8, 0:wi]
                    dst = proj[:, r, b * wi:(b + 1) * wi]
                    return eng.activation(dst, src, ACT.Copy) if r == 0 else eng.tensor_copy(dst, src)
                w_in = Project("w_in_ab", t["w_in_ab"][0].rearrange("(p k) n -> p k n", k=KD), wi, 4,
                               lambda b, r: PS[:, (2 * b + r) % 8, 0:wi], evac_in)
                ada(0, w_in.load)
                w_out = Project("w_out_ab", t["w_out_ab"][0].rearrange("(p k) n -> p k n", k=KD), 256, 4,
                                lambda b, r: PS[:, 4 + 2 * r + b // 2, b % 2 * 256:b % 2 * 256 + 256])
                mixer0(w_in, w_out, proj, merged, uq_landed)
                with ExitStack() as scope:
                    MTh = sb("mergedT_h", [P, KD, REQ * TOK], F32R, scope)
                    MTl = sb("mergedT_l", [P, KD, REQ * TOK], F32R, scope)
                    w_out.alloc(scope, MTh, MTl)
                    turn = Turn("merged", merged, MTh, MTl)
                    norm = Norm("ln_mix0", 0, 0, [4, 5, 6, 7], lambda e, r: e.wait_ge(w_out.mm, 8), scope, t["ln_mix_g"][0:1, :], t["ln_mix_b"][0:1, :])
                    with nc.Block() as block:
                        @block.sync
                        def _(sp):
                            norm.sync(sp)
                            for j in range(RING):
                                sp.wait_ge(w_out.lo, j + 1)
                                moes[0].load_weights(sp, 0, j)

                        @block.tensor
                        def _(pe):
                            turn.tensor(pe)
                            pe.wait_ge(turn.lo, 4)
                            w_out.tensor(pe)

                        @block.scalar
                        def _(act):
                            turn.scalar(act)
                            w_out.scalar(act)
                            norm.scalar(act)

                        @block.gpsimd
                        def _(pool):
                            norm.gpsimd(pool)

                        @block.vector
                        def _(dve):
                            turn.vector(dve)
                            w_out.vector(dve)
                            norm.vector(dve)

        class Moe:
            def __init__(self, l):
                self.l = l
                n = f"moe{l}_"
                self.landed = [sem(f"{n}weights_landed{i}") for i in range(RING)]
                self.gate_landed = [sem(f"{n}gate_landed{i}") for i in range(RING)]
                names = ("up_high", "up_low", "down_high", "down_low", "up_multiplied", "down_multiplied",
                         "silu", "product", "gated", "hidden_high", "hidden_low",
                         "router_landed", "router_high", "router_low", "router_multiplied", "router_scores",
                         "scores_turned", "gates", "gates_turned", "gatesT", "gates_stored", "first_request_done")
                self.s = {k: sem(n + k) for k in names}

            def load_weights(self, sp, it, j):
                l, e = self.l, it * RING + j - 1
                if isinstance(e, int) and e < 0:
                    src = (t["sh_w_gate"][l], t["sh_w_up"][l], t["sh_w_down"][l])
                else:
                    src = [t[k][l, bass.ds(e, 1)].rearrange("o a b -> (o a) b") for k in ("exp_w_gate", "exp_w_up", "exp_w_down")]
                for i in range(2):
                    sp.dma_start(raw[j][:, i * D:(i + 1) * D], src[i].rearrange("(p k) f -> p (k f)", k=KD)).then_inc(self.landed[j], 16)
                sp.dma_start(raw[j][:, 2 * D:3 * D], src[2]).then_inc(self.landed[j], 16)

            def run(self, prefetch, final):
                l, s = self.l, self.s
                n = f"moe{l}_"
                GRPS = (NE - RING) // RING
                with ExitStack() as scope:
                    mod = Modulate(n + "mod", 2, scope)
                    uh = [sb(f"{n}up_h{i}", [P, 2, KD, FF], F32R, scope) for i in range(2)]
                    ul = [sb(f"{n}up_l{i}", [P, 2, KD, FF], F32R, scope) for i in range(2)]
                    dh = [sb(f"{n}down_h{i}", [P, D], F32R, scope) for i in range(2)]
                    dl = [sb(f"{n}down_l{i}", [P, D], F32R, scope) for i in range(2)]
                    gb = [sb(f"{n}gate_b{i}", [P, REQ * TOK], F32, scope) for i in range(RING)]
                    sg = [sb(f"{n}silu{i}", [P, REQ * TOK], F32, scope) for i in range(2)]
                    pr = [sb(f"{n}prod{i}", [P, REQ * TOK], F32, scope) for i in range(2)]
                    hg = [sb(f"{n}hid{i}", [P, REQ * TOK], F32, scope) for i in range(2)]
                    hh = [sb(f"{n}hid_h{i}", [P, REQ * TOK], F32R, scope) for i in range(2)]
                    hl = [sb(f"{n}hid_l{i}", [P, REQ * TOK], F32R, scope) for i in range(2)]
                    rw = sb(n + "router", [P, KD, NE], F32, scope)
                    rwh = sb(n + "router_h", [P, KD, NE], F32R, scope)
                    rwl = sb(n + "router_l", [P, KD, NE], F32R, scope)
                    rb = sb(n + "router_b", [P, NE], F32, scope)
                    scT = sb(n + "scoresT", [NE, REQ * TOK], F32, scope)
                    sc = PS[:, 3, 0:REQ * NE].rearrange("p (r e) -> p r e", r=REQ)
                    sel = sb(n + "biased", [P, REQ, NE], F32, scope)
                    m8 = sb(n + "top8", [P, REQ, 8], F32, scope)
                    i8 = sb(n + "top8_at", [P, REQ, 8], U32, scope)
                    f8 = sb(n + "top8_f", [P, REQ, 8], F32, scope)
                    mask = sb(n + "mask", [P, REQ, NE], F32, scope)
                    gt = sb(n + "gates_t", [P, REQ, NE], F32, scope)
                    sm = sb(n + "gate_sum", [P, REQ, 2], F32, scope)
                    gT = sb(n + "gatesT_sb", [NE, REQ * TOK], F32, scope)
                    norm = Norm(f"ln_ffn{l}", l, 1, [4, 5, 6, 7], lambda e, r: e.wait_ge(*((s["down_multiplied"], NE + 1) if r else (s["first_request_done"], 1))), scope,
                                t["ln_ffn_g"][l:l + 1, :], t["ln_ffn_b"][l:l + 1, :])

                    def items(eng, first, body):
                        for j in range(first, RING):
                            body(0, j)
                        with eng.Fori(1, 1 + GRPS) as it:
                            for j in range(RING):
                                body(it, j)
                        body(1 + GRPS, 0)

                    def split_up_high(act, it, j):
                        act.wait_ge(self.landed[j], it * 48 + 48)
                        wait(act, s["up_multiplied"], it * RING + j - 1)
                        act.activation(uh[j % 2][:, :, :, :].rearrange("p a k f -> p (a k f)"), raw[j][:, 0:2 * D], ACT.Copy).then_inc(s["up_high"], 1)

                    def split_down_high(act, it, j):
                        wait(act, s["down_multiplied"], it * RING + j - 1)
                        act.activation(dh[j % 2][:, :], raw[j][:, 2 * D:3 * D], ACT.Copy).then_inc(s["down_high"], 1)

                    def following(it, j):
                        return (it, j + 1) if j + 1 < RING else (it + 1, 0)

                    def split_up_low(dve, it, j):
                        dve.wait_ge(s["up_high"], it * RING + j + 1)
                        dve.tensor_tensor(ul[j % 2][:, :, :, :].rearrange("p a k f -> p (a k f)"), raw[j][:, 0:2 * D],
                                          uh[j % 2][:, :, :, :].rearrange("p a k f -> p (a k f)").bitcast(F32), ALU.subtract).then_inc(s["up_low"], 1)

                    def split_down_low(dve, it, j):
                        dve.wait_ge(s["down_high"], it * RING + j + 1)
                        dve.tensor_tensor(dl[j % 2][:, :], raw[j][:, 2 * D:3 * D], dh[j % 2][:, :].bitcast(F32), ALU.subtract).then_inc(s["down_low"], 1)

                    with nc.Block() as block:
                        @block.sync
                        def _(sp):
                            sp.dma_start(rw[:, :, :], t["router_w"][l].rearrange("(p k) e -> p k e", k=KD)).then_inc(s["router_landed"], 16)
                            sp.dma_start(rb[:, :], t["router_bias"][l:l + 1, :].partition_broadcast(P)).then_inc(s["router_landed"], 16)
                            norm.sync(sp)
                            sp.wait_ge(s["gatesT"], 1)
                            sp.dma_start(gate_rows[l], gT[:, :]).then_inc(s["gates_stored"], 16)
                            sp.wait_ge(s["gates_stored"], 16)

                            def load(it, j):
                                i = it * RING + j
                                if not (isinstance(it, int) and it == 0):
                                    sp.wait_ge(s["down_low"], i - RING + 1)
                                    self.load_weights(sp, it, j)
                                    wait(sp, s["gated"], i - RING)
                                sp.dma_start(gb[j][:, :], gate_rows[l, bass.ds(i - 1, 1), :].partition_broadcast(P)).then_inc(self.gate_landed[j], 16)
                            items(sp, 1, load)
                            if prefetch:
                                for n in range(1, RING + 1):
                                    sp.wait_ge(s["down_low"], NE - RING + n + 1)
                                    prefetch(sp, n % RING)
                            if final:
                                for r in range(REQ):
                                    sp.wait_ge(norm.done[r], 2 - r)
                                    store(sp, y_out[r][0], X[:, r, :])
                                sp.wait_ge(s_out, n_out[0])

                        @block.scalar
                        def _(act):
                            split_up_high(act, 0, 0)
                            act.wait_ge(s["router_landed"], 32)
                            act.activation(rwh[:, :, :], rw[:, :, :], ACT.Copy).then_inc(s["router_high"], 1)
                            mod.scalar(act)
                            split_up_high(act, 0, 1)
                            split_down_high(act, 0, 0)
                            act.wait_ge(s["router_multiplied"], 1)
                            act.activation(scT[:, :], PS[0:NE, 2, 0:REQ * TOK], ACT.Sigmoid).then_inc(s["router_scores"], 1)

                            def item(it, j, first=False, last=False):
                                i = it * RING + j
                                if not last and not first:
                                    split_up_high(act, *following(it, j))
                                act.wait_ge(s["up_multiplied"], i + 1)
                                wait(act, s["product"], i - 1)
                                act.activation(sg[j % 2][:, :], PS[:, j % 2, 0:REQ * TOK], ACT.Silu).then_inc(s["silu"], 1)
                                if not last:
                                    split_down_high(act, *following(it, j))
                            item(0, 0, first=True)
                            split_up_high(act, 0, 2)
                            act.wait_ge(s["gates_turned"], 1)
                            act.activation(gT[:, :], PS[0:NE, 2, 0:REQ * TOK], ACT.Copy).then_inc(s["gatesT"], 1)
                            for j in range(1, RING):
                                item(0, j, first=(j == 1))
                            with act.Fori(1, 1 + GRPS) as it:
                                for j in range(RING):
                                    item(it, j)
                            item(1 + GRPS, 0, last=True)
                            norm.scalar(act)

                        @block.gpsimd
                        def _(pool):
                            norm.gpsimd(pool)

                        @block.vector
                        def _(dve):
                            split_up_low(dve, 0, 0)
                            dve.wait_ge(s["router_high"], 1)
                            dve.tensor_tensor(rwl[:, :, :], rw[:, :, :], rwh[:, :, :].bitcast(F32), ALU.subtract).then_inc(s["router_low"], 1)
                            mod.vector(dve)
                            split_up_low(dve, 0, 1)
                            split_down_low(dve, 0, 0)
                            dve.wait_ge(s["scores_turned"], 1)
                            dve_step(dve, dve.tensor_tensor(sel[:, :, :], sc[:, :, :], rb[:, :].unsqueeze(1).to_broadcast([P, REQ, NE]), ALU.add))
                            for r in range(REQ):
                                dve_step(dve, dve.max(m8[:, r, :], sel[:, r, :]))
                                dve_step(dve, dve.max_index(i8[:, r, :], m8[:, r, :], sel[:, r, :]))
                            dve_step(dve, dve.tensor_copy(f8[:, :, :], i8[:, :, :]))
                            for r in range(REQ):
                                dve_step(dve, dve.tensor_scalar(mask[:, r, :], table[:, T_IO:T_MK], f8[:, r, 0:1], None, ALU.is_equal))
                                for j in range(1, TOPK):
                                    dve_step(dve, dve.scalar_tensor_tensor(mask[:, r, :], table[:, T_IO:T_MK], f8[:, r, j:j + 1], mask[:, r, :],
                                                                           ALU.is_equal, ALU.add))
                            dve_step(dve, dve.tensor_tensor(gt[:, :, :], mask[:, :, :], sc[:, :, :], ALU.mult))
                            dve_step(dve, dve.tensor_reduce(sm[:, :, 0], gt[:, :, :], AX_X, ALU.add))
                            dve_step(dve, dve.reciprocal(sm[:, :, 1], sm[:, :, 0]))
                            for r in range(REQ):
                                i = dve.tensor_scalar(gt[:, r, :], gt[:, r, :], sm[:, r, 1:2], ROUTED, ALU.mult, ALU.mult)
                                i.then_inc(s["gates"], 1)

                            def item(it, j, last=False, shared=False):
                                i = it * RING + j
                                b = j % 2
                                if not last and not shared:
                                    split_up_low(dve, *following(it, j))
                                dve.wait_ge(s["silu"], i + 1)
                                wait(dve, s["hidden_low"], i - 1)
                                up = PS[:, b, REQ * TOK:2 * REQ * TOK]
                                if shared:
                                    dve.tensor_tensor(hg[b][:, :], sg[b][:, :], up, ALU.mult).then_inc(s["product"], 1)
                                    dve.wait_ge(s["product"], 1)
                                else:
                                    dve.tensor_tensor(pr[b][:, :], sg[b][:, :], up, ALU.mult).then_inc(s["product"], 1)
                                    dve.wait_ge(s["product"], i + 1)
                                    dve.wait_ge(self.gate_landed[j], it * 16 + (16 if j else 0))
                                    dve.tensor_tensor(hg[b][:, :], pr[b][:, :], gb[j][:, :], ALU.mult).then_inc(s["gated"], 1)
                                    dve.wait_ge(s["gated"], i)
                                wait(dve, s["down_multiplied"], i - 1)
                                dve.tensor_copy(hh[b][:, :], hg[b][:, :]).then_inc(s["hidden_high"], 1)
                                dve.wait_ge(s["hidden_high"], i + 1)
                                dve.tensor_tensor(hl[b][:, :], hg[b][:, :], hh[b][:, :].bitcast(F32), ALU.subtract).then_inc(s["hidden_low"], 1)
                                if not last:
                                    split_down_low(dve, *following(it, j))
                            for j in range(RING):
                                item(0, j, shared=(j == 0))
                            with dve.Fori(1, 1 + GRPS) as it:
                                for j in range(RING):
                                    item(it, j)
                            item(1 + GRPS, 0, last=True)
                            norm.vector(dve)

                        @block.tensor
                        def _(pe):
                            mod.tensor(pe)
                            pe.wait_ge(mod.lo, 2)
                            pe.wait_ge(s["router_low"], 1)
                            for k in range(KD):
                                mm = three(pe, PS[0:NE, 2, 0:REQ * TOK], rwh[:, k, :], rwl[:, k, :], mod.h[:, k, :], mod.l[:, k, :],
                                           start=(k == 0), stop=(k == KD - 1))
                            mm.then_inc(s["router_multiplied"], 1)

                            def turn_scores():
                                pe.wait_ge(s["router_scores"], 1)
                                for r in range(REQ):
                                    mm = pe.transpose(PS[:, 3, r * NE:(r + 1) * NE], scT[:, r * TOK:(r + 1) * TOK], ident[0:NE, 0:NE])
                                mm.then_inc(s["scores_turned"], 1)

                            def up(it, j, between=None):
                                i = it * RING + j
                                b = j % 2
                                pe.wait_ge(s["up_low"], i + 1)
                                wait(pe, s["product"], i - 1)
                                for a in range(2):
                                    if a and between:
                                        between()
                                    for k in range(KD):
                                        mm = three(pe, PS[:, b, a * REQ * TOK:(a + 1) * REQ * TOK], uh[b][:, a, k, :], ul[b][:, a, k, :],
                                                   mod.h[:, k, :], mod.l[:, k, :], start=(k == 0), stop=(k == KD - 1))
                                mm.then_inc(s["up_multiplied"], 1)

                            def down(it, j, first=False, last=False):
                                i = it * RING + j
                                b = j % 2
                                pe.wait_ge(s["hidden_low"], i + 1)
                                pe.wait_ge(s["down_low"], i + 1)
                                for r in range(REQ):
                                    at = slice(r * TOK, r * TOK + TOK)
                                    for c in range(2):
                                        cols = slice(c * 512, c * 512 + 512)
                                        mm = three(pe, PS[:, 4 + 2 * r + c, :], hh[b][:, at], hl[b][:, at], dh[b][:, cols], dl[b][:, cols],
                                                   start=first, stop=last)
                                    if last and r == 0:
                                        mm.then_inc(s["first_request_done"], 1)
                                mm.then_inc(s["down_multiplied"], 1)
                            up(0, 0, between=turn_scores)
                            up(0, 1)
                            down(0, 0, first=True)
                            pe.wait_ge(s["gates"], 2)
                            for r in range(REQ):
                                mm = pe.transpose(PS[0:NE, 2, r * TOK:(r + 1) * TOK], gt[:, r, :], ident)
                            mm.then_inc(s["gates_turned"], 1)
                            for j in range(2, RING):
                                up(0, j)
                                down(0, j - 1)
                            with pe.Fori(1, 1 + GRPS) as it:
                                for j in range(RING):
                                    up(it, j)
                                    if j:
                                        down(it, j - 1)
                                    else:
                                        down(it - 1, RING - 1)
                            up(1 + GRPS, 0)
                            down(GRPS, RING - 1)
                            down(1 + GRPS, 0, last=True)

        NS = 2 * G5
        RJ = REQ * NC5
        TG = 8
        UNITS = [(tile, d) for tile in range(G5 // TG) for d in range(2)]
        swap = table[:, T_SW:T_SW + P]
        u_d = nc.dram_tensor("u_saved", [P, KD * CH * RJ], F32, kind="Internal").ap()

        def run_layer1():
            with ExitStack() as outer:
                w_in = Project("w_in_c", t["w_in_c"][0].rearrange("(p k) n -> p k n", k=KD), 256, 4, None)
                w_out = Project("w_out_c", t["w_out_c"][0].rearrange("(k p) n -> p k n", p=P), 256, 8,
                                lambda b, r: PS[:, 4 * r + b // 2, b % 2 * 256:b % 2 * 256 + 256])
                ada(1, w_in.load)
                PW = sb("powers", [P, 12, 2, NS], F32, outer)
                X0 = sb("s5_start", [P, P], F32, outer)
                u_stored = sem("u_stored")
                b_landed, c_landed = sem("s5_b_landed"), sem("s5_c_landed")
                pw_step, pw_ready = sem("powers_step"), sem("powers_ready")
                Braw = raw[0][:, 0:2048].rearrange("n (i p c) -> n i p c", i=2, c=C5)
                Craw = raw[1][:, 0:2048].rearrange("n (c i p) -> n c i p", i=2, c=C5)
                U = [raw[i][:, 2048:3072].rearrange("p (g n) -> p g n", g=G5 // 2) for i in range(2)]
                E = sb("E", [P, 2, TG, CC], F32, outer)
                cols = lambda ap: ap.rearrange("p (n c) -> p n c", n=NS)
                flat = lambda ap: ap.rearrange("p n c -> p (n c)")
                B2 = cols(raw[0][:, 0:2048])
                Bb = cols(raw[1][:, 0:2048])
                Ct = cols(raw[2][:, 0:2048])
                C2 = cols(raw[3][:, 0:2048])
                Bs = cols(E[:, :, :, :].rearrange("p d g x -> p (d g x)"))
                c_turned, c_ready, swapped, bs_ready = sem("BC_turned"), sem("C_ready"), sem("BC_swapped"), sem("B_columns_ready")

                with ExitStack() as scope:
                    mod = Modulate("mix1_mod", 0, scope)
                    w_in.alloc(scope, mod.h, mod.l)
                    uT = sb("uT", [P, KD, CH, RJ], F32, scope)
                    q = sb("s5_pre", [P, 24, P5], F32, scope)
                    q2 = sb("s5_twice", [P, 6, 2, P5], F32, scope)
                    x0s = sb("s5_start_turned", [P, 3, NS], F32, scope)
                    ldt = sb("s5_log_dt_sb", [P, 2], F32, scope)
                    sraw = sb("s5_state_raw", [G5, 2, 2, P5], F32, scope)
                    lam_landed, st_landed = sem("lambda_landed"), sem("state_landed")
                    dt_e, angles, exps, sins = sem("dt_ready"), sem("angles_ready"), sem("magnitudes_ready"), sem("sines_ready")
                    pre = sem("discretised")
                    turned, s6_ready = sem("s5_params_turned"), sem("s5_params_ready")
                    V = sb("u_rows", [RJ, G5, CC], F32, scope)
                    v_mm, v_ready = sem("u_rows_turned"), [sem("u_rows_act"), sem("u_rows_dve")]
                    u_mm, u_ready = sem("u_chunks_turned"), [sem("u_chunks_act"), sem("u_chunks_dve")]

                    def u_copies(eng, me):
                        copy = (lambda o, i: eng.activation(o, i, ACT.Copy)) if me == 0 else eng.tensor_copy
                        for k in range(KD):
                            f = 2 * k + me
                            eng.wait_ge(v_mm, f + 1)
                            copy(V[:, 8 * k:8 * k + 8, me * 64:me * 64 + 64].rearrange("n g (s c) -> n s g c", s=4),
                                 PS[0:RJ, f % 4, :].rearrange("n (s g c) -> n s g c", s=4, g=8)).then_inc(v_ready[me], 1)
                            if k and (k - 1) % 2 == me:
                                chunk_copy(eng, copy, k - 1, me)
                        if me == (KD - 1) % 2:
                            chunk_copy(eng, copy, KD - 1, me)

                    def chunk_copy(eng, copy, k, me):
                        eng.wait_ge(u_mm, k + 1)
                        copy(U[k // 4][:, k % 4 * 8:k % 4 * 8 + 8, :], PS[:, 4 + k % 4, 0:8 * RJ].rearrange("p (g n) -> p g n", g=8)).then_inc(u_ready[me], 1)
                    pt_tmp = mod.HT[:, 0:4, :].rearrange("p k (m n) -> p k m n", m=2)

                    def evac(eng, b, a):
                        i = 2 * b + a
                        src = PS[:, i, 0:REQ * TOK].rearrange("p (r j s) -> p s r j", r=REQ, s=CH)
                        dst = uT[:, i, :, :].rearrange("p s (j r) -> p s r j", r=REQ)
                        return eng.activation(dst, src, ACT.Copy) if a == 0 else eng.tensor_copy(dst, src)
                    w_in.evac = evac
                    with nc.Block() as block:
                        @block.sync
                        def _(sp):
                            sp.dma_start(q[:, 0, :], t["s5_lam_re"][0].rearrange("d g p -> (d g) p")).then_inc(lam_landed, 16)
                            sp.dma_start(q[:, 1, :], t["s5_lam_im"][0].rearrange("d g p -> (d g) p")).then_inc(lam_landed, 16)
                            sp.dma_start(ldt[:, 0:1], t["s5_log_dt"][0].rearrange("d (g o) -> (d g) o", o=1)).then_inc(lam_landed, 16)
                            for d in range(2):
                                sp.dma_start(sraw[:, d, :, :], t["state_ssm"][0, 0, d].rearrange("i g p -> g i p")).then_inc(st_landed, 16)
                            sp.wait_ge(w_in.lo, 1)
                            for i, key in enumerate(("s5_b_re", "s5_b_im")):
                                sp.dma_start(Braw[:, i, :, :], t[key][0].rearrange("d g p c -> (d g) p c")).then_inc(b_landed, 16)
                            sp.wait_ge(w_in.lo, 2)
                            for i, key in enumerate(("s5_c_re", "s5_c_im")):
                                sp.dma_start(Craw[:, :, i, :], t[key][0].rearrange("d g c p -> (d g) c p")).then_inc(c_landed, 16)
                            sp.wait_ge(w_in.ready[0], 4)
                            sp.wait_ge(w_in.ready[1], 4)
                            sp.dma_start(u_d, uT[:, :, :, :].rearrange("p k s n -> p (k s n)")).then_inc(u_stored, 16)
                            sp.wait_ge(u_stored, 16)

                        @block.tensor
                        def _(pe):
                            mod.tensor(pe)
                            pe.wait_ge(mod.lo, 2)
                            for b in range(4):
                                if b == 3:
                                    pe.wait_ge(w_in.ready[0], 2)
                                    pe.wait_ge(w_in.ready[1], 2)
                                    pe.wait_ge(pre, 1)
                                    for i in range(6):
                                        mm = pe.transpose(PS[:, i // 4, i % 4 * NS:(i % 4 + 1) * NS], q2[:, i, :, :].rearrange("n a p -> n (a p)"), ident)
                                    mm.then_inc(turned, 1)
                                    pe.wait_ge(st_landed, 32)
                                    for d in range(2):
                                        mm = pe.transpose(PS[:, 2, d * G5:(d + 1) * G5], sraw[:, d, :, :].rearrange("g i p -> g (i p)"), ident[0:G5, 0:G5])
                                    mm.then_inc(turned, 1)
                                pe.wait_ge(w_in.lo, b + 1)
                                for a in range(2):
                                    for k in range(KD):
                                        at = slice(a * P, a * P + P)
                                        mm = three(pe, PS[:, 2 * b + a, 0:REQ * TOK], w_in.wh[b % 2][:, k, at], w_in.wl[b % 2][:, k, at],
                                                   mod.h[:, k, :], mod.l[:, k, :], start=(k == 0), stop=(k == KD - 1))
                                    mm.then_inc(w_in.mm, 1)
                            pe.wait_ge(w_in.ready[0], 4)
                            pe.wait_ge(w_in.ready[1], 4)

                            pe.wait_ge(s6_ready, 4)
                            pe.matmul(PS[:, 3, 0:NS], swap, x0s[:, 0, :], start=True, stop=True).then_inc(turned, 1)

                            def rows(f):
                                if f == 3:
                                    pe.wait_ge(s6_ready, 5)
                                wait(pe, v_ready[f % 2], f // 2 - 1)
                                for i in range(4):
                                    mm = pe.transpose(PS[0:RJ, f % 4, i * P:i * P + P], uT[:, f // 2, f % 2 * 4 + i, :], ident)
                                mm.then_inc(v_mm, 1)

                            def columns(k):
                                pe.wait_ge(v_ready[0], k + 1)
                                pe.wait_ge(v_ready[1], k + 1)
                                if k >= 4:
                                    pe.wait_ge(u_ready[k % 2], k // 2 - 1)
                                for g in range(8):
                                    mm = pe.transpose(PS[:, 4 + k % 4, g * RJ:(g + 1) * RJ], V[:, 8 * k + g, :], ident[0:RJ, 0:RJ])
                                mm.then_inc(u_mm, 1)
                            for k in range(KD):
                                rows(2 * k)
                                rows(2 * k + 1)
                                if k:
                                    columns(k - 1)
                            columns(KD - 1)
                            def turn(bank, source):
                                for c in range(C5):
                                    mm = pe.transpose(PS[:, bank + c // 4, c % 4 * NS:(c % 4 + 1) * NS], source(c), ident)
                                mm.then_inc(c_turned, 1)

                            def swap_halves(bank, columns):
                                for b in range(4):
                                    mm = pe.matmul(PS[:, bank + b, :], swap, flat(columns)[:, b * 512:(b + 1) * 512], start=True, stop=True)
                                mm.then_inc(swapped, 1)
                            pe.wait_ge(c_landed, 32)
                            pe.wait_ge(u_ready[0], KD // 2)
                            pe.wait_ge(u_ready[1], KD // 2)
                            turn(4, lambda c: Craw.rearrange("n c i p -> n c (i p)")[:, c, :])
                            pe.wait_ge(b_landed, 32)
                            pe.wait_ge(v_ready[0], KD)
                            pe.wait_ge(v_ready[1], KD)
                            turn(0, lambda c: Braw.rearrange("n i p c -> n (i p) c")[:, :, c])
                            pe.wait_ge(c_ready, 2)
                            swap_halves(4, Ct)
                            pe.wait_ge(bs_ready, 1)
                            swap_halves(0, Bs)

                        @block.scalar
                        def _(act):
                            mod.scalar(act)

                            def besides(act, b):
                                if b == 1:
                                    act.wait_ge(lam_landed, 48)
                                    act.activation(ldt[:, 1:2], ldt[:, 0:1], ACT.Exp).then_inc(dt_e, 1)
                                    act.wait_ge(angles, 1)
                                    act.activation(q[:, 4, :], q[:, 2, :], ACT.Exp).then_inc(exps, 1)
                                    act.activation(q[:, 5, :], q[:, 2, :], ACT.Exp, scale=-1.0).then_inc(exps, 1)
                                if b == 2:
                                    act.wait_ge(angles, 2)
                                    act.activation(q[:, 8, :], q[:, 6, :], ACT.Sin).then_inc(sins, 1)
                                    act.activation(q[:, 9, :], q[:, 7, :], ACT.Sin).then_inc(sins, 1)
                                if b == 3:
                                    act.wait_ge(turned, 1)
                                    for slot, at in ((5, PS[:, 0, 0:2 * NS]), (3, PS[:, 0, 2 * NS:4 * NS]), (11, PS[:, 1, 0:2 * NS])):
                                        act.activation(PW[:, slot, :, :], at.rearrange("p (i n) -> p i n", i=2), ACT.Copy).then_inc(s6_ready, 1)
                                    act.wait_ge(turned, 2)
                                    act.activation(x0s[:, 0, :], PS[:, 2, 0:NS], ACT.Copy).then_inc(s6_ready, 1)
                            w_in.act_between = besides
                            w_in.scalar(act)
                            act.wait_ge(w_in.ready[0], 4)
                            act.wait_ge(turned, 3)
                            act.activation(x0s[:, 2, :], PS[:, 3, 0:NS], ACT.Copy).then_inc(s6_ready, 1)
                            u_copies(act, 0)
                            act.wait_ge(u_ready[0], KD // 2)
                            act.wait_ge(w_in.lo, 4)
                            act.wait_ge(c_turned, 1)
                            for h, sign in ((0, 1.0), (1, -1.0)):
                                rows = slice(h * P5, (h + 1) * P5)
                                act.activation(Ct[rows, :, :], PS[rows, 4:8, :].rearrange("p b (c n) -> p n (b c)", n=NS), ACT.Copy, scale=sign).then_inc(c_ready, 1)
                            act.wait_ge(swapped, 1)
                            act.activation(flat(C2), PS[:, 4:8, :].rearrange("p b x -> p (b x)"), ACT.Copy, scale=-1.0).then_inc(c_ready, 1)
                            act.wait_ge(c_ready, 3)

                        @block.vector
                        def _(dve):
                            mod.vector(dve)
                            S = lambda i: q[:, i, :]
                            step = lambda ins: dve_step(dve, ins)

                            def angles_of_lambda():
                                dve.wait_ge(dt_e, 1)
                                dve.tensor_scalar(S(2), S(0), ldt[:, 1:2], None, ALU.mult)
                                i = dve.tensor_scalar(S(3), S(1), ldt[:, 1:2], None, ALU.mult)
                                i.then_inc(angles, 1)
                                dve.wait_ge(angles, 1)
                                BIG, C1 = 12582912.0, 6.28125
                                C2 = 2 * math.pi - C1
                                PI = 3.1415925
                                step(dve.tensor_scalar(S(10), S(3), 1 / (2 * math.pi), BIG, ALU.mult, ALU.add))
                                step(dve.tensor_scalar(S(11), S(10), -BIG, None, ALU.add))
                                step(dve.scalar_tensor_tensor(S(10), S(11), -C1, S(3), ALU.mult, ALU.add))
                                step(dve.scalar_tensor_tensor(S(12), S(11), -C2, S(10), ALU.mult, ALU.add))
                                step(dve.tensor_scalar(S(6), S(12), PI, -PI, ALU.min, ALU.max))
                                step(dve.tensor_scalar(S(13), S(6), math.pi / 2, None, ALU.add))
                                step(dve.tensor_scalar(S(14), S(13), PI, -2 * math.pi, ALU.is_gt, ALU.mult))
                                step(dve.tensor_tensor(S(15), S(13), S(14), ALU.add))
                                dve.tensor_scalar(S(7), S(15), PI, -PI, ALU.min, ALU.max).then_inc(angles, 1)

                            def discretise():
                                dve.wait_ge(sins, 2)
                                dve.wait_ge(exps, 2)
                                dve.tensor_tensor(S(18), S(4), S(9), ALU.mult)
                                dve.tensor_tensor(S(19), S(4), S(8), ALU.mult)
                                dve.tensor_tensor(S(20), S(5), S(9), ALU.mult)
                                step(dve.scalar_tensor_tensor(S(21), S(8), -1.0, S(5), ALU.mult, ALU.mult))
                                dve.tensor_scalar(S(10), S(18), -1.0, None, ALU.add)
                                dve.tensor_tensor(S(11), S(0), S(0), ALU.mult)
                                step(dve.tensor_tensor(S(12), S(1), S(1), ALU.mult))
                                step(dve.tensor_tensor(S(13), S(11), S(12), ALU.add))
                                dve.reciprocal(S(14), S(13))
                                dve.tensor_tensor(S(15), S(10), S(0), ALU.mult)
                                dve.tensor_tensor(S(16), S(19), S(1), ALU.mult)
                                dve.tensor_tensor(S(17), S(19), S(0), ALU.mult)
                                step(dve.tensor_tensor(S(2), S(10), S(1), ALU.mult))
                                dve.tensor_tensor(S(12), S(15), S(16), ALU.add)
                                step(dve.tensor_tensor(S(13), S(17), S(2), ALU.subtract))
                                dve.tensor_tensor(S(22), S(12), S(14), ALU.mult)
                                step(dve.tensor_tensor(S(23), S(13), S(14), ALU.mult))
                                dve.tensor_copy(q2[:, :, 0, :], q[:, 18:24, :])
                                dve.tensor_copy(q2[:, :, 1, :], q[:, 18:24, :]).then_inc(pre, 1)

                            w_in.dve_between = lambda eng, b: angles_of_lambda() if b == 1 else discretise() if b == 2 else None
                            w_in.vector(dve)
                            u_copies(dve, 1)
                            dve.wait_ge(u_ready[1], KD // 2)
                            dve.wait_ge(c_turned, 2)
                            dve.tensor_copy(Bs, PS[:, 0:4, :].rearrange("p b (c n) -> p n (b c)", n=NS)).then_inc(bs_ready, 1)
                            dve.wait_ge(bs_ready, 1)

                        @block.gpsimd
                        def _(pool):
                            steps = [0]

                            def step(ins):
                                steps[0] += 1
                                ins.then_inc(pw_step, 1)
                                pool.wait_ge(pw_step, steps[0])

                            def cmul(dst, n, a, b):
                                br = PW[:, b, 0, :].unsqueeze(1).to_broadcast([P, n, NS])
                                bi = PW[:, b, 1, :].unsqueeze(1).to_broadcast([P, n, NS])
                                ar, ai = PW[:, a:a + n, 0, :], PW[:, a:a + n, 1, :]
                                T = [pt_tmp[:, i, 0:n, :] for i in range(4)]
                                pool.tensor_tensor(T[0], ar, br, ALU.mult)
                                pool.tensor_tensor(T[1], ai, bi, ALU.mult)
                                pool.tensor_tensor(T[2], ar, bi, ALU.mult)
                                step(pool.tensor_tensor(T[3], ai, br, ALU.mult))
                                pool.tensor_tensor(PW[:, dst:dst + n, 0, :], T[0], T[1], ALU.subtract)
                                step(pool.tensor_tensor(PW[:, dst:dst + n, 1, :], T[2], T[3], ALU.add))
                            pool.memset(PW[:, 4, 0, :], 1.0)
                            pool.memset(PW[:, 4, 1, :], 0.0)
                            pool.wait_ge(mod.lo, 2)
                            pool.wait_ge(s6_ready, 3)
                            cmul(6, 1, 5, 5)
                            cmul(7, 2, 5, 6)
                            cmul(2, 1, 3, 3)
                            cmul(1, 1, 2, 3)
                            cmul(0, 1, 2, 2)
                            cmul(9, 1, 8, 5)
                            cmul(10, 1, 8, 8)
                            pool.wait_ge(s6_ready, 5)
                            pool.tensor_tensor(x0s[:, 1, :], x0s[:, 0, :], PW[:, 9, 0, :], ALU.mult)
                            step(pool.tensor_tensor(x0s[:, 2, :], x0s[:, 2, :], PW[:, 9, 1, :], ALU.mult))
                            pool.tensor_tensor(X0[:, :], x0s[:, 1, :], x0s[:, 2, :], ALU.add).then_inc(pw_ready, 1)
                            pool.wait_ge(pw_ready, 1)

                with ExitStack() as scope:
                    F = sb("F", [P, 2, G5, CC], F32, scope)
                    ZX = sb("ZX", [P, 2, G5, NC5 + 1, REQ], F32, scope)
                    Et = sb("E_turned", [P, TG * P], F32, scope)
                    tmpE = sb("tmpE", [P, TG * CC], F32, scope)
                    tmpF = sb("tmpF", [P, TG * CC], F32, scope)
                    A = sb("scan_sums", [P, 3, 2, G5, REQ], F32, scope)
                    HS = sb("s5_end", [P, 2, G5], F32, scope)
                    HSt = sb("s5_end_t", [G5, 2, P], F32, scope)
                    Ms = [raw[2 + i][:, 2048:3072] for i in range(2)]
                    scr = cols(F[:, 1, G5 - 16:G5, :].rearrange("p g x -> p (g x)"))
                    bb, b_ready = sem("B_step"), sem("B_ready")
                    e_p, e_ready, f_p, f_ready = sem("E_step"), sem("E_ready"), sem("F_step"), sem("F_ready")
                    et_mm, et_ready = sem("E_turned_pe"), sem("E_turned_ready")
                    m_mm, m_ready = sem("M_multiplied"), sem("M_ready")
                    z_mm, z_ready, ym_mm = sem("z_multiplied"), sem("z_ready"), sem("y_inside_multiplied")
                    scan_a = [sem("scan_sum_forward"), sem("scan_sum_backward")]
                    scan_j = [sem("scan_swapped_forward"), sem("scan_swapped_backward")]
                    scan_re = [sem("scan_real_product_forward"), sem("scan_real_product_backward")]
                    scan_x = [sem("scan_state_forward"), sem("scan_state_backward")]
                    ends, end_t, end_s = sem("end_states"), sem("end_states_turned"), sem("end_states_sb")
                    y_mm = sem("y_multiplied")

                    def build_matrix(eng, s1, s2, tmp, out, v, base, other, slots):
                        tile, d = UNITS[v]
                        n0 = d * G5 + tile * TG
                        shape = [P, TG, CH, C5]
                        pr = PW[:, slots, 0, n0:n0 + TG].rearrange("p s n -> p n s").unsqueeze(3).to_broadcast(shape)
                        pi = PW[:, slots, 1, n0:n0 + TG].rearrange("p s n -> p n s").unsqueeze(3).to_broadcast(shape)
                        o = out.rearrange("p g (s c) -> p g s c", s=CH)
                        tm = tmp[:, :].rearrange("p (g s c) -> p g s c", g=TG, s=CH)
                        eng.tensor_tensor(o, base[:, n0:n0 + TG, :].unsqueeze(2).to_broadcast(shape), pr, ALU.mult)
                        eng.tensor_tensor(tm, other[:, n0:n0 + TG, :].unsqueeze(2).to_broadcast(shape), pi, ALU.mult).then_inc(s1, 1)
                        eng.wait_ge(s1, v + 1)
                        eng.tensor_tensor(out.rearrange("p g x -> p (g x)"), out.rearrange("p g x -> p (g x)"), tmp[:, :], ALU.add).then_inc(s2, 1)

                    slot = lambda d, j: ZX[:, d, :, j, :]
                    power = lambda m, i, d: PW[:, m, i, d * G5:(d + 1) * G5]
                    both = lambda ap: ap.unsqueeze(2).to_broadcast([P, G5, REQ])
                    steps = lambda d, j: (j, j + 1) if d == 0 else (NC5 - j, NC5 - j - 1)

                    def scan_sum(eng, d, j):
                        cur, nxt = steps(d, j)
                        eng.wait_ge(scan_x[d], 2 * j + 2)
                        eng.tensor_tensor(A[:, 0, d, :, :], slot(d, cur), slot(d, nxt), ALU.add).then_inc(scan_a[d], 1)
                        eng.wait_ge(scan_a[d], j + 1)
                        if j == NC5 - 1:
                            eng.tensor_tensor(A[:, 1, d, :, 0], A[:, 0, d, :, 0], power(7, 0, d), ALU.mult).then_inc(scan_re[d], 1)
                        else:
                            eng.tensor_tensor(A[:, 1, d, :, :], A[:, 0, d, :, :], both(power(10, 0, d)), ALU.mult).then_inc(scan_re[d], 1)

                    def scan_next(dve, d, j):
                        swapped_sum = PS[:, 6 + d, 0:G5 * REQ].rearrange("p (g r) -> p g r", r=REQ)
                        dve.wait_ge(scan_j[d], j + 1)
                        if j == NC5 - 1:
                            dve.tensor_tensor(A[:, 2, d, :, 0], swapped_sum[:, :, 0], power(7, 1, d), ALU.mult).then_inc(scan_x[d], 1)
                        else:
                            dve.tensor_tensor(A[:, 2, d, :, :], swapped_sum, both(power(10, 1, d)), ALU.mult).then_inc(scan_x[d], 1)
                        dve.wait_ge(scan_x[d], 2 * j + 3)
                        dve.wait_ge(scan_re[d], j + 1)
                        if j == NC5 - 1:
                            dve.tensor_tensor(HS[:, d, :], A[:, 1, d, :, 0], A[:, 2, d, :, 0], ALU.add).then_inc(ends, 1)
                        else:
                            dve.tensor_tensor(slot(d, steps(d, j)[1]), A[:, 1, d, :, :], A[:, 2, d, :, :], ALU.add).then_inc(scan_x[d], 1)

                    def y_at(g):
                        q, at = g // 16, g % 16
                        return PS[q * RJ:(q + 1) * RJ, at // 4, at % 4 * CC:(at % 4 + 1) * CC]

                    with nc.Block() as block:
                        @block.tensor
                        def _(pe):
                            pe.wait_ge(b_ready, 2)

                            def inside(v):
                                tile, d = UNITS[v]
                                for x in range(TG):
                                    g = tile * TG + x
                                    pe.wait_ge(m_ready, 2 * v + 1 + x // 4)
                                    mm = pe.matmul(y_at(g), U[g // 32][:, g % 32, :], Ms[v % 2][:, x * P:(x + 1) * P],
                                                   start=(d == 0 and g % 4 == 0), stop=False, skip_group_check=True)
                                mm.then_inc(ym_mm, 1)
                            for v, (tile, d) in enumerate(UNITS):
                                pe.wait_ge(e_ready, v + 1)
                                wait(pe, z_ready, v)
                                for x in range(TG):
                                    mm = pe.transpose(PS[:, 6 + x // 4, x % 4 * P:x % 4 * P + P], E[:, d, x, :], ident)
                                    if x % 4 == 3:
                                        mm.then_inc(et_mm, 1)
                                pe.wait_ge(f_ready, v + 1)
                                wait(pe, m_ready, 2 * v)
                                for x in range(TG):
                                    mm = pe.matmul(PS[:, 4 + x // 4, x % 4 * P:x % 4 * P + P], E[:, d, x, :],
                                                   F[:, d, tile * TG + x, :], start=True, stop=True)
                                    if x % 4 == 3:
                                        mm.then_inc(m_mm, 1)
                                pe.wait_ge(et_ready, 2 * v + 2)
                                for x in range(TG):
                                    g = tile * TG + x
                                    mm = pe.matmul(PS[:, 6, x * RJ:(x + 1) * RJ], Et[:, x * P:(x + 1) * P], U[g // 32][:, g % 32, :],
                                                   start=True, stop=True)
                                mm.then_inc(z_mm, 1)
                                if v:
                                    inside(v - 1)
                            inside(len(UNITS) - 1)
                            for j in range(NC5):
                                for d in range(2):
                                    pe.wait_ge(scan_a[d], j + 1)
                                    pe.matmul(PS[:, 6 + d, 0:G5 * REQ], swap, A[:, 0, d, :, :].rearrange("p g r -> p (g r)"),
                                              start=True, stop=True).then_inc(scan_j[d], 1)
                            for g in range(G5):
                                for d in range(2):
                                    pe.wait_ge(scan_x[d], 2 * NC5)
                                    mm = pe.matmul(y_at(g), ZX[:, d, g, d:d + NC5, :].rearrange("p j r -> p (j r)"), F[:, d, g, :], start=False,
                                                   stop=(d == 1 and g % 4 == 3), skip_group_check=True)
                                if g % 16 == 15:
                                    mm.then_inc(y_mm, 1)
                            pe.wait_ge(ends, 2)
                            for d in range(2):
                                mm = pe.transpose(PS[0:G5, 7, d * P:(d + 1) * P], HS[:, d, :], ident)
                            mm.then_inc(end_t, 1)

                        @block.scalar
                        def _(act):
                            for v, (tile, d) in enumerate(UNITS):
                                for half in range(2):
                                    act.wait_ge(et_mm, 2 * v + half + 1)
                                    wait(act, z_mm, v)
                                    act.activation(Et[:, half * 512:half * 512 + 512], PS[:, 6 + half, :], ACT.Copy).then_inc(et_ready, 1)
                                act.wait_ge(z_mm, v + 1)
                                act.activation(ZX[:, d, tile * TG:(tile + 1) * TG, 1 - d:1 - d + NC5, :],
                                               PS[:, 6, 0:TG * RJ].rearrange("p (g j r) -> p g j r", r=REQ, j=NC5), ACT.Copy).then_inc(z_ready, 1)
                            act.wait_ge(end_t, 1)
                            act.activation(HSt[:, :, :], PS[0:G5, 7, 0:2 * P].rearrange("g (d x) -> g d x", d=2), ACT.Copy).then_inc(end_s, 1)

                        @block.vector
                        def _(dve):
                            cr = PW[:, 11, 0, :].unsqueeze(2).to_broadcast([P, NS, C5])
                            ci = PW[:, 11, 1, :].unsqueeze(2).to_broadcast([P, NS, C5])
                            Bp = cols(PS[:, 0:4, :].rearrange("p b x -> p (b x)"))
                            dve.tensor_tensor(Bb, Bs, cr, ALU.mult)
                            dve.tensor_tensor(scr, Bp, ci, ALU.mult).then_inc(bb, 1)
                            dve.tensor_tensor(B2, Bp, cr, ALU.mult)
                            dve.wait_ge(bb, 1)
                            dve.tensor_tensor(Bb, Bb, scr, ALU.add).then_inc(b_ready, 1)
                            dve.wait_ge(b_ready, 1)
                            dve.tensor_tensor(scr, Bs, ci, ALU.mult).then_inc(bb, 1)
                            dve.wait_ge(bb, 2)
                            dve.tensor_tensor(B2, B2, scr, ALU.subtract).then_inc(b_ready, 1)
                            dve.wait_ge(b_ready, 2)

                            def masked(v):
                                d = UNITS[v][1]
                                mk = table[:, T_MK + d * P:T_MK + (d + 1) * P].unsqueeze(1).to_broadcast([P, 4, P])
                                for half in range(2):
                                    dve.wait_ge(m_mm, 2 * v + half + 1)
                                    wait(dve, ym_mm, v - 1)
                                    dve.tensor_tensor(Ms[v % 2][:, half * 512:half * 512 + 512].rearrange("p (x q) -> p x q", x=4),
                                                      PS[:, 4 + half, :].rearrange("p (x q) -> p x q", x=4), mk, ALU.mult).then_inc(m_ready, 1)
                            for v, (tile, d) in enumerate(UNITS):
                                if v >= 2:
                                    dve.wait_ge(m_mm, 2 * (v - 1))
                                build_matrix(dve, e_p, e_ready, tmpE, E[:, d, :, :], v, Bb, B2, slice(8, 0, -1) if d == 0 else slice(1, 9))
                                dve.wait_ge(e_ready, v + 1)
                                if v:
                                    masked(v - 1)
                            masked(len(UNITS) - 1)
                            dve.wait_ge(z_ready, len(UNITS))
                            for d in range(2):
                                x0 = slot(d, steps(d, 0)[0])
                                dve.memset(x0[:, :, 0], 0.0).then_inc(scan_x[d], 1)
                                dve.tensor_copy(x0[:, :, 1], X0[:, d * G5:(d + 1) * G5]).then_inc(scan_x[d], 1)
                            for j in range(NC5):
                                scan_sum(dve, 0, j)
                                scan_next(dve, 0, j)
                                scan_next(dve, 1, j)

                        @block.gpsimd
                        def _(pool):
                            for v, (tile, d) in enumerate(UNITS):
                                if v == len(UNITS) - 4:
                                    pool.wait_ge(b_ready, 2)
                                build_matrix(pool, f_p, f_ready, tmpF, F[:, d, tile * TG:(tile + 1) * TG, :], v, Ct, C2,
                                             slice(0, 8) if d == 0 else slice(7, None, -1))
                                pool.wait_ge(f_ready, v + 1)
                            pool.wait_ge(z_ready, len(UNITS))
                            for j in range(NC5):
                                scan_sum(pool, 1, j)

                        @block.sync
                        def _(sp):
                            sp.wait_ge(ym_mm, len(UNITS))
                            for j in range(RING):
                                w_out.load(sp, j)
                            sp.wait_ge(end_s, 1)
                            store(sp, ssm_out[0, 0].rearrange("d i g p -> g d i p"), HSt[:, :, :].rearrange("g d (i p) -> g d i p", i=2))
                            sp.wait_ge(y_mm, 4)

                Yt = sb("Yt", [P, KD, CH, RJ], F32, outer)
                with ExitStack() as scope:
                    QT = G5 // 4 * C5
                    V = sb("y_rows", [P, CH, QT], F32, scope)
                    uT = sb("uT_again", [P, KD, CH, RJ], F32, scope)
                    dcol = sb("s5_d_col", [P, KD], F32, scope)
                    back, v_ready = sem("u_back_landed"), [sem("y_rows_act"), sem("y_rows_dve")]
                    y_mm2, y_done = sem("y_channels_turned"), sem("y_plus_du")

                    def y_copies(copy, me):
                        for b in range(me, 4, 2):
                            copy(V[:, :, 64 * b:64 * b + 64].rearrange("n s (g c) -> n g s c", g=4),
                                 PS[:, b, :].rearrange("n (g s c) -> n g s c", g=4, s=CH)).then_inc(v_ready[me], 1)
                    with nc.Block() as block:
                        @block.sync
                        def _(sp):
                            sp.dma_start(uT[:, :, :, :].rearrange("p k s n -> p (k s n)"), u_d).then_inc(back, 16)
                            sp.dma_start(dcol[:, :], t["s5_d"][0].rearrange("(k p) -> p k", p=P), allow_slow_non_contiguous=True).then_inc(back, 16)

                        @block.tensor
                        def _(pe):
                            for half in range(2):
                                for e in range(2):
                                    pe.wait_ge(v_ready[e], half + 1)
                                for s in range(CH):
                                    mm = pe.transpose(PS[:, 4 + 2 * half + s // 4, s % 4 * P:(s % 4 + 1) * P], V[:, s, half * P:(half + 1) * P], ident)
                                mm.then_inc(y_mm2, 1)

                        @block.scalar
                        def _(act):
                            y_copies(lambda o, i: act.activation(o, i, ACT.Copy), 0)
                            act.wait_ge(v_ready[0], 2)

                        @block.vector
                        def _(dve):
                            y_copies(dve.tensor_copy, 1)
                            dve.wait_ge(back, 32)
                            for half in range(2):
                                dve.wait_ge(y_mm2, half + 1)
                                turned = PS[:, 4 + 2 * half:6 + 2 * half, :].rearrange("p b (s q n) -> p (b s) q n", s=4, q=4)
                                for q in range(4):
                                    k = 2 * q + half
                                    dve.scalar_tensor_tensor(Yt[:, k, :, :], uT[:, k, :, :], dcol[:, k:k + 1], turned[:, :, q, :],
                                                             ALU.mult, ALU.add).then_inc(y_done, 1)
                            dve.wait_ge(y_done, KD)

                with ExitStack() as scope:
                    Gf = sb("gelu", [P, KD, REQ * TOK], F32, scope)
                    Gh = sb("gelu_h", [P, KD, REQ * TOK], F32R, scope)
                    Gl = sb("gelu_l", [P, KD, REQ * TOK], F32R, scope)
                    w_out.alloc(scope, Gh, Gl)
                    sig = Gf[:, :, :].rearrange("p k t -> p (k t)").rearrange("p (r n) -> p r n", r=REQ)
                    gelu, g_hi, g_lo = sem("gelu_ready"), sem("gelu_high"), sem("gelu_low")
                    sigm, glu = sem("gate_sigmoid"), sem("glu_ready")
                    norm = Norm("ln_mix1", 1, 0, [0, 1, 4, 5], lambda e, r: e.wait_ge(glu, 2 * r + 2), scope, t["ln_mix_g"][1:2, :], t["ln_mix_b"][1:2, :])
                    glu_sb = Yt[:, :, :, :].rearrange("p k s n -> p (k s n)").rearrange("p (r n) -> p r n", r=REQ)
                    norm.source = lambda r, n: glu_sb[:, r, n * 512:n * 512 + 512]
                    with nc.Block() as block:
                        @block.sync
                        def _(sp):
                            norm.sync(sp)
                            w_out.sync(sp)
                            for j in range(RING):
                                sp.wait_ge(w_out.lo, 5 + j)
                                moes[1].load_weights(sp, 0, j)

                        @block.tensor
                        def _(pe):
                            pe.wait_ge(g_lo, 2)
                            w_out.tensor(pe)

                        @block.scalar
                        def _(act):
                            for k in range(KD):
                                act.activation(Gf[:, k, :].rearrange("p (r j s) -> p s r j", r=REQ, s=CH),
                                               Yt[:, k, :, :].rearrange("p s (j r) -> p s r j", r=REQ), ACT.Gelu_apprx_tanh).then_inc(gelu, 1)
                            for half in range(2):
                                act.wait_ge(gelu, 4 * half + 4)
                                act.activation(Gh[:, 4 * half:4 * half + 4, :], Gf[:, 4 * half:4 * half + 4, :], ACT.Copy).then_inc(g_hi, 1)
                            w_out.scalar(act)
                            act.wait_ge(w_out.mm, 16)
                            act.wait_ge(g_lo, 2)
                            for r in range(REQ):
                                for n in range(2):
                                    act.activation(sig[:, r, n * 512:n * 512 + 512], PS[:, 4 * r + 2 + n, :], ACT.Sigmoid).then_inc(sigm, 1)
                            norm.scalar(act)

                        @block.gpsimd
                        def _(pool):
                            norm.gpsimd(pool)

                        @block.vector
                        def _(dve):
                            for half in range(2):
                                dve.wait_ge(g_hi, half + 1)
                                at = slice(4 * half, 4 * half + 4)
                                dve.tensor_tensor(Gl[:, at, :], Gf[:, at, :], Gh[:, at, :].bitcast(F32), ALU.subtract).then_inc(g_lo, 1)
                            w_out.vector(dve)
                            for r in range(REQ):
                                for n in range(2):
                                    dve.wait_ge(sigm, 2 * r + n + 1)
                                    dve.tensor_tensor(glu_sb[:, r, n * 512:n * 512 + 512], PS[:, 4 * r + n, :], sig[:, r, n * 512:n * 512 + 512],
                                                      ALU.mult).then_inc(glu, 1)
                            norm.vector(dve)

        moes = [Moe(0)]
        run_layer0()
        moes[0].run(lambda sp, j: ada_load(sp, 1, 0, j), False)
        nc.clear_and_free_semaphores(layer_sems)
        nc.all_engine_barrier()
        moes.append(Moe(1))
        run_layer1()
        moes[1].run(None, True)


_INS = ['x_prompt', 'x_sample', 'c', 'cache_attn_k', 'cache_attn_v', 'cache_mla_ckv', 'cache_mla_krope', 'state_ssm', 'c_ctx',
        'ada_w', 'ada_b', 'ln_mix_g', 'ln_mix_b', 'ln_ffn_g', 'ln_ffn_b', 'w_in_ab', 'attn_sink', 'mla_q_norm', 'mla_kv_norm',
        'mla_w_uq', 'mla_w_ukv', 'w_out_ab', 'w_in_c', 's5_lam_re', 's5_lam_im', 's5_log_dt', 's5_b_re', 's5_b_im', 's5_c_re',
        's5_c_im', 's5_d', 'w_out_c', 'router_w', 'router_bias', 'exp_w_gate', 'exp_w_up', 'exp_w_down', 'sh_w_gate', 'sh_w_up',
        'sh_w_down']
_OUTS = [(1, 128, 1024), (1, 128, 1024), (1, 1, 128, 2, 64), (1, 1, 128, 2, 64), (1, 1, 128, 128), (1, 1, 128, 32), (1, 1, 2, 2, 64, 64)]


def kernel(**inputs):
    import concourse.bacc as bacc
    from concourse.bass_utils import run_bass_kernel_spmd

    nc = bacc.Bacc("TRN2", target_bir_lowering=False, num_devices=1)
    arrays, aps = {}, {}
    given = {name: inputs[name] for name in _INS}
    given["table"], given["pick"] = shape_constants()
    for name, value in given.items():
        a = np.ascontiguousarray(value)
        arrays[f"in_{name}"] = a
        aps[name] = nc.dram_tensor(f"in_{name}", a.shape, mybir.dt.from_np(a.dtype), kind="ExternalInput").ap()
    outs = [nc.dram_tensor(f"out_{i}", shape, F32, kind="ExternalOutput").ap() for i, shape in enumerate(_OUTS)]
    build(nc, aps, outs)
    r = run_bass_kernel_spmd(nc, [arrays], core_ids=[0])
    return tuple(r.results[0][f"out_{i}"] for i in range(len(_OUTS)))
```
